# Optimizing a Trainium2 kernel written in Bass

```python
import jax, jax.numpy as jnp
from jax import lax
import numpy as np
import math

D_MODEL = 1024
BATCH = 1
SEQ = 256
DEPTH = 2

GRID_W = 64
CTX_LEN = 256
H_M = 4
DH_M = 128
M_W = H_M * DH_M
H_A = 8
H_KV = 2
DH_A = 64
A_Q = H_A * DH_A
A_KV = H_KV * DH_A
GQA_GROUP = H_A // H_KV
WINDOW = 128
WIN_BLOCK = 128
ROPE_THETA = 10000.0
AB_WIDTHS = (M_W, M_W, M_W, M_W, 4 * H_M, A_Q, A_KV, A_KV)
MIX_W = M_W + A_Q
H_C = 4
DK_C = 128
DV_C = 256
C_K = H_C * DK_C
C_V = H_C * DV_C
GATE_RANK = 16
GATE_TAU = 16.0
C_WIDTHS = (C_K, C_K, C_V, C_V, 2 * GATE_RANK)
CHUNK = 64
N_KEYS = 128
N_EXPERTS = N_KEYS * N_KEYS
PEER_HEADS = 8
PEER_TOPK = 16
PEER_KEY_DIM = 256
PEER_HALF = PEER_KEY_DIM // 2
PEER_CHUNK = 128
N_EVEN = (DEPTH + 1) // 2
N_ODD = DEPTH // 2
DEEPNORM_ALPHA = (2 * DEPTH) ** 0.25
DEEPNORM_BETA = (8 * DEPTH) ** -0.25
LN_EPS = 1e-5


def _layernorm(x, w, b):
    xf = x.astype(jnp.float32)
    mu = xf.mean(-1, keepdims=True)
    var = jnp.mean(jnp.square(xf - mu), -1, keepdims=True)
    return ((xf - mu) * lax.rsqrt(var + LN_EPS)).astype(x.dtype) * w + b

def _split(a, widths):
    idx = np.cumsum(widths)[:-1].tolist()
    return jnp.split(a, idx, axis=-1)

def _heads(a, h):
    b, s = a.shape[:2]
    return a.reshape(b, s, h, -1).transpose(0, 2, 1, 3)

def _head_norm(h, w):
    hf = h.astype(jnp.float32)
    hf = hf * lax.rsqrt(jnp.mean(hf * hf, -1, keepdims=True) + LN_EPS)
    b, nh, s, d = h.shape
    return hf.transpose(0, 2, 1, 3).reshape(b, s, nh * d) * w

def _to_chunks(a):
    b, h, s = a.shape[:3]
    a = a.reshape((b, h, s // CHUNK, CHUNK) + a.shape[3:])
    return jnp.moveaxis(a, 2, 0)

def _from_chunks(a):
    a = jnp.moveaxis(a, 0, 2)
    return a.reshape(a.shape[:2] + (-1,) + a.shape[4:])

def _mlstm_scan(q, k, v, log_i, log_f, state):
    causal = jnp.tril(jnp.ones((CHUNK, CHUNK), bool))

    def step(carry, inp):
        c_st, n_st, m_st = carry
        qc, kc, vc, li, lf = inp
        cum = jnp.cumsum(lf, axis=-1)
        dmat = cum[..., :, None] - cum[..., None, :] + li[..., None, :]
        dmat = jnp.where(causal, dmat, -jnp.inf)
        m_inter = cum + m_st[..., None]
        m_t = jnp.maximum(m_inter, dmat.max(-1))
        w = jnp.exp(dmat - m_t[..., None]) * jnp.einsum('bhtd,bhsd->bhts', qc, kc)
        a_inter = jnp.exp(m_inter - m_t)
        num = a_inter[..., None] * jnp.einsum('bhtd,bhde->bhte', qc, c_st) + jnp.einsum('bhts,bhse->bhte', w, vc)
        den = a_inter * jnp.einsum('bhtd,bhd->bht', qc, n_st) + w.sum(-1)
        h = num / jnp.maximum(jnp.abs(den), jnp.exp(-m_t))[..., None]
        total = cum[..., -1]
        decay_s = total[..., None] - cum + li
        m_new = jnp.maximum(total + m_st, decay_s.max(-1))
        ws = jnp.exp(decay_s - m_new[..., None])
        a_st = jnp.exp(total + m_st - m_new)
        c_st = a_st[..., None, None] * c_st + jnp.einsum('bhs,bhsd,bhse->bhde', ws, kc, vc)
        n_st = a_st[..., None] * n_st + jnp.einsum('bhs,bhsd->bhd', ws, kc)
        return (c_st, n_st, m_new), h

    state, hs = lax.scan(step, state, tuple(_to_chunks(a) for a in (q, k, v, log_i, log_f)))
    return _from_chunks(hs), state

def _gla_scan(q, k, v, log_a, state):
    causal = jnp.tril(jnp.ones((CHUNK, CHUNK), bool))

    def step(st, inp):
        qc, kc, vc, la = inp
        cum = jnp.cumsum(la, axis=2)
        rel = cum[:, :, :, None, :] - cum[:, :, None, :, :]
        rel = jnp.where(causal[:, :, None], rel, -jnp.inf)
        scores = jnp.einsum('bhtk,bhsk,bhtsk->bhts', qc, kc, jnp.exp(rel))
        out = jnp.einsum('bhtk,bhkv->bhtv', qc * jnp.exp(cum), st) + jnp.einsum('bhts,bhsv->bhtv', scores, vc)
        total = cum[:, :, -1:, :]
        st = jnp.exp(total[:, :, 0, :, None]) * st + jnp.einsum('bhsk,bhsv->bhkv', kc * jnp.exp(total - cum), vc)
        return st, out

    state, outs = lax.scan(step, state, tuple(_to_chunks(a) for a in (q, k, v, log_a)))
    return _from_chunks(outs), state

def _directional(scan_fn, ctx_seq, lat_seq, init, reverse):
    if reverse:
        ctx_seq = tuple(jnp.flip(a, 2) for a in ctx_seq)
        lat_seq = tuple(jnp.flip(a, 2) for a in lat_seq)
    h_ctx, state = scan_fn(*ctx_seq, init)
    h_lat, _ = scan_fn(*lat_seq, state)
    if reverse:
        h_ctx, h_lat = jnp.flip(h_ctx, 2), jnp.flip(h_lat, 2)
    return h_ctx, h_lat

def _axial_rope(s):
    rows = s // GRID_W
    row = jnp.repeat(jnp.arange(rows), GRID_W).astype(jnp.float32)
    col = jnp.tile(jnp.arange(GRID_W), rows).astype(jnp.float32)
    n_freq = DH_A // 4
    inv = ROPE_THETA ** (-jnp.arange(n_freq, dtype=jnp.float32) / n_freq)
    ang = jnp.concatenate([row[:, None] * inv, col[:, None] * inv], -1)
    return jnp.cos(ang), jnp.sin(ang)

def _rope(x, cos, sin):
    xf = x.astype(jnp.float32)
    x1, x2 = xf[..., 0::2], xf[..., 1::2]
    c = cos[None, :, None, :]
    sn = sin[None, :, None, :]
    return jnp.stack([x1 * c - x2 * sn, x1 * sn + x2 * c], -1).reshape(x.shape).astype(x.dtype)

def _window_attention(q, k, v, k_ctx, v_ctx, sink):
    b, s = q.shape[:2]
    nb = s // WIN_BLOCK
    lc = k_ctx.shape[1]
    qb = jnp.moveaxis(q.reshape(b, nb, WIN_BLOCK, H_KV, GQA_GROUP, DH_A), 1, 0)

    def bands(a):
        ap = jnp.pad(a, ((0, 0), (WIN_BLOCK, WIN_BLOCK), (0, 0), (0, 0))).reshape(b, nb + 2, WIN_BLOCK, H_KV, DH_A)
        return jnp.moveaxis(jnp.concatenate([ap[:, :-2], ap[:, 1:-1], ap[:, 2:]], 2), 1, 0)

    kw, vw = bands(k), bands(v)
    qi = jnp.arange(WIN_BLOCK)[:, None]
    kj = jnp.arange(3 * WIN_BLOCK)[None, :]
    key_pos = jnp.arange(nb)[:, None, None] * WIN_BLOCK + kj - WIN_BLOCK
    valid = (jnp.abs(kj - WIN_BLOCK - qi) <= WINDOW) & (key_pos >= 0) & (key_pos < s)
    scale = DH_A ** -0.5
    sink_l = sink.reshape(H_KV, GQA_GROUP).astype(jnp.float32)

    def block(args):
        qn, kn, vn, mask = args
        s_ctx = jnp.einsum('bqhgd,bchd->bhgqc', qn, k_ctx).astype(jnp.float32) * scale
        s_win = jnp.einsum('bqhgd,bkhd->bhgqk', qn, kn).astype(jnp.float32) * scale
        s_win = jnp.where(mask, s_win, -jnp.inf)
        sink_col = jnp.broadcast_to(sink_l[None, :, :, None, None], s_ctx.shape[:-1] + (1,))
        p = jax.nn.softmax(jnp.concatenate([sink_col, s_ctx, s_win], -1), -1).astype(qn.dtype)
        return (jnp.einsum('bhgqc,bchd->bqhgd', p[..., 1:1 + lc], v_ctx)
                + jnp.einsum('bhgqk,bkhd->bqhgd', p[..., 1 + lc:], vn))

    out = lax.map(block, (qb, kw, vw, valid))
    return jnp.moveaxis(out, 0, 1).reshape(b, s, H_A, DH_A)

def _context_attention(q, k, v, sink):
    b, lc = q.shape[:2]
    qg = q.reshape(b, lc, H_KV, GQA_GROUP, DH_A)
    sc = jnp.einsum('bqhgd,bkhd->bhgqk', qg, k).astype(jnp.float32) * DH_A ** -0.5
    sink_col = jnp.broadcast_to(sink.reshape(H_KV, GQA_GROUP).astype(jnp.float32)[None, :, :, None, None],
                                sc.shape[:-1] + (1,))
    p = jax.nn.softmax(jnp.concatenate([sink_col, sc], -1), -1)[..., 1:].astype(q.dtype)
    return jnp.einsum('bhgqk,bkhd->bqhgd', p, v).reshape(b, lc, H_A, DH_A)

def _ab_streams(h, w_in, gate_b):
    q_m, k_m, v_m, o_m, g_m, q_a, k_a, v_a = _split(h @ w_in, AB_WIDTHS)
    b, s = h.shape[:2]
    g = g_m.reshape(b, s, 2, 2, H_M).astype(jnp.float32) + gate_b.astype(jnp.float32)
    mlstm = (_heads(q_m, H_M).astype(jnp.float32),
             _heads(k_m, H_M).astype(jnp.float32) * DH_M ** -0.5,
             _heads(v_m, H_M).astype(jnp.float32))
    gates = [(g[:, :, d, 0].transpose(0, 2, 1), jax.nn.log_sigmoid(g[:, :, d, 1]).transpose(0, 2, 1))
             for d in range(2)]
    attn = (q_a.reshape(b, s, H_A, DH_A), k_a.reshape(b, s, H_KV, DH_A), v_a.reshape(b, s, H_KV, DH_A))
    return mlstm, gates, o_m, attn

def _merge_ab(m, o, a, norm_w, w_out):
    hm = _head_norm(m, norm_w).astype(o.dtype) * jax.nn.sigmoid(o)
    cat = jnp.concatenate([hm, a.reshape(a.shape[0], a.shape[1], A_Q)], -1)
    return cat @ w_out

def _mixer_ab(hl, hc, w_in, gate_b, norm_w, sink, w_out, ctx_out):
    ml, gl, ol, (ql, kl, vl) = _ab_streams(hl, w_in, gate_b)
    mc, gc, oc, (qc, kc, vc) = _ab_streams(hc, w_in, gate_b)
    b = hl.shape[0]
    init = (jnp.zeros((b, H_M, DH_M, DH_M), jnp.float32), jnp.zeros((b, H_M, DH_M), jnp.float32),
            jnp.zeros((b, H_M), jnp.float32))
    outs = [_directional(_mlstm_scan, mc + gc[d], ml + gl[d], init, d == 1) for d in range(2)]
    cos, sin = _axial_rope(hl.shape[1])
    a_lat = _window_attention(_rope(ql, cos, sin), _rope(kl, cos, sin), vl, kc, vc, sink)
    y_lat = _merge_ab(outs[0][1] + outs[1][1], ol, a_lat, norm_w, w_out)
    if not ctx_out:
        return y_lat, None
    y_ctx = _merge_ab(outs[0][0] + outs[1][0], oc, _context_attention(qc, kc, vc, sink), norm_w, w_out)
    return y_lat, y_ctx

def _c_streams(h, w_in, gate_up, gate_b):
    q, k, v, g, low = _split(h @ w_in, C_WIDTHS)
    b, s = h.shape[:2]
    qkv = (_heads(q, H_C).astype(jnp.float32) * DK_C ** -0.5,
           _heads(k, H_C).astype(jnp.float32),
           _heads(v, H_C).astype(jnp.float32))
    low = low.reshape(b, s, 2, GATE_RANK)
    log_a = [_heads(jax.nn.log_sigmoid((low[:, :, d] @ gate_up[d] + gate_b[d]).astype(jnp.float32)) / GATE_TAU, H_C)
             for d in range(2)]
    return qkv, log_a, g

def _merge_c(h, g, norm_w, w_out):
    return (_head_norm(h, norm_w).astype(g.dtype) * jax.nn.silu(g)) @ w_out

def _mixer_c(hl, hc, w_in, gate_up, gate_b, norm_w, w_out, ctx_out):
    sl, al, gl = _c_streams(hl, w_in, gate_up, gate_b)
    sc, ac, gc = _c_streams(hc, w_in, gate_up, gate_b)
    init = jnp.zeros((hl.shape[0], H_C, DK_C, DV_C), jnp.float32)
    outs = [_directional(_gla_scan, sc + (ac[d],), sl + (al[d],), init, d == 1) for d in range(2)]
    y_lat = _merge_c(outs[0][1] + outs[1][1], gl, norm_w, w_out)
    if not ctx_out:
        return y_lat, None
    return y_lat, _merge_c(outs[0][0] + outs[1][0], gc, norm_w, w_out)

def _peer(h, wq, keys, u, v):
    shape = h.shape
    tokens = h.reshape(-1, PEER_CHUNK, shape[-1])

    def block(hb):
        tc = hb.shape[0]
        q = (hb @ wq).reshape(tc, PEER_HEADS, 2, PEER_HALF)
        s = jnp.einsum('thpk,hpnk->thpn', q, keys)
        s_top, i_top = lax.top_k(s, PEER_TOPK)
        cand = s_top[:, :, 0, :, None] + s_top[:, :, 1, None, :]
        cid = i_top[:, :, 0, :, None] * N_KEYS + i_top[:, :, 1, None, :]
        best, pos = lax.top_k(cand.reshape(tc, PEER_HEADS, -1), PEER_TOPK)
        eid = jnp.take_along_axis(cid.reshape(tc, PEER_HEADS, -1), pos, -1)
        g = jax.nn.softmax(best.astype(jnp.float32), -1).astype(hb.dtype)
        act = jax.nn.gelu(jnp.einsum('td,thed->the', hb, u[eid]), approximate=False)
        return jnp.einsum('the,thed->td', g * act, v[eid])

    return lax.map(block, tokens).reshape(shape)

def first_inputs(seed: int = 0) -> dict:
    key = jax.random.key(seed)
    ks = jax.random.split(key, 26)
    f32 = jnp.float32

    def nrm(k, shape, s):
        return jax.random.normal(k, shape, f32) * s

    d = D_MODEL
    f_bias = 3.0 + 3.0 * jnp.arange(H_M, dtype=f32) / (H_M - 1)
    gate_offset = jnp.stack([jnp.zeros((H_M,), f32), f_bias])[None, None]
    return {
        "x": nrm(ks[0], (BATCH, SEQ, d), 1.0),
        "c": nrm(ks[1], (BATCH, d), 1.0),
        "ctx": nrm(ks[2], (BATCH, CTX_LEN, d), 1.0),
        "c_ctx": nrm(ks[3], (d,), 1.0),
        "w_mod": nrm(ks[4], (DEPTH, d, 6 * d), 0.5 * d ** -0.5),
        "b_mod": nrm(ks[5], (DEPTH, 6 * d), 0.02),
        "ln_w": 1.0 + nrm(ks[6], (DEPTH, 2, d), 0.02),
        "ln_b": nrm(ks[7], (DEPTH, 2, d), 0.02),
        "ab_w_in": nrm(ks[8], (N_EVEN, d, sum(AB_WIDTHS)), d ** -0.5),
        "ab_gate_b": nrm(ks[9], (N_EVEN, 2, 2, H_M), 0.1) + gate_offset,
        "ab_norm_w": 1.0 + nrm(ks[10], (N_EVEN, M_W), 0.02),
        "ab_sink": nrm(ks[11], (N_EVEN, H_A), 0.5),
        "ab_w_out": nrm(ks[12], (N_EVEN, MIX_W, d), DEEPNORM_BETA * MIX_W ** -0.5),
        "gla_w_in": nrm(ks[13], (N_ODD, d, sum(C_WIDTHS)), d ** -0.5),
        "gla_gate_up": nrm(ks[14], (N_ODD, 2, GATE_RANK, C_K), GATE_RANK ** -0.5),
        "gla_gate_b": 1.0 + nrm(ks[15], (N_ODD, 2, C_K), 0.5),
        "gla_norm_w": 1.0 + nrm(ks[16], (N_ODD, C_V), 0.02),
        "gla_w_out": nrm(ks[17], (N_ODD, C_V, d), DEEPNORM_BETA * C_V ** -0.5),
        "peer_wq": nrm(ks[18], (DEPTH, d, PEER_HEADS * PEER_KEY_DIM), d ** -0.5),
        "peer_keys": nrm(ks[19], (DEPTH, PEER_HEADS, 2, N_KEYS, PEER_HALF), PEER_HALF ** -0.5),
        "peer_u": nrm(ks[20], (DEPTH, N_EXPERTS, d), d ** -0.5),
        "peer_v": nrm(ks[21], (DEPTH, N_EXPERTS, d), DEEPNORM_BETA * (PEER_HEADS * PEER_TOPK) ** -0.5),
    }

def first_block(x, c, ctx, c_ctx, w_mod, b_mod, ln_w, ln_b, ab_w_in, ab_gate_b, ab_norm_w, ab_sink, ab_w_out,
              gla_w_in, gla_gate_up, gla_gate_b, gla_norm_w, gla_w_out, peer_wq, peer_keys, peer_u, peer_v):
    for layer in range(DEPTH):
        last = layer == DEPTH - 1
        j = layer // 2
        mod_l = jax.nn.silu(c) @ w_mod[layer] + b_mod[layer]
        mod_c = jax.nn.silu(c_ctx) @ w_mod[layer] + b_mod[layer]
        sh1, sc1, g1, sh2, sc2, g2 = jnp.split(mod_l[:, None, :], 6, axis=-1)
        csh1, csc1, cg1, csh2, csc2, cg2 = jnp.split(mod_c, 6)
        hl = x * (1.0 + sc1) + sh1
        hc = ctx * (1.0 + csc1) + csh1
        if layer % 2 == 0:
            y_lat, y_ctx = _mixer_ab(hl, hc, ab_w_in[j], ab_gate_b[j], ab_norm_w[j], ab_sink[j], ab_w_out[j], not last)
        else:
            y_lat, y_ctx = _mixer_c(hl, hc, gla_w_in[j], gla_gate_up[j], gla_gate_b[j], gla_norm_w[j], gla_w_out[j],
                                    not last)
        x = _layernorm(DEEPNORM_ALPHA * x + g1 * y_lat, ln_w[layer, 0], ln_b[layer, 0])
        f_lat = _peer(x * (1.0 + sc2) + sh2, peer_wq[layer], peer_keys[layer], peer_u[layer], peer_v[layer])
        x = _layernorm(DEEPNORM_ALPHA * x + g2 * f_lat, ln_w[layer, 1], ln_b[layer, 1])
        if not last:
            ctx = _layernorm(DEEPNORM_ALPHA * ctx + cg1 * y_ctx, ln_w[layer, 0], ln_b[layer, 0])
            f_ctx = _peer(ctx * (1.0 + csc2) + csh2, peer_wq[layer], peer_keys[layer], peer_u[layer], peer_v[layer])
            ctx = _layernorm(DEEPNORM_ALPHA * ctx + cg2 * f_ctx, ln_w[layer, 1], ln_b[layer, 1])
    return x


DEPTH_2 = 1

EPS = 1e-6
CONV_WIDTH = 4
N_BRANCHES = 3
GMLP_WIDTH = D_MODEL
GMLP_GROUPS = 8
GMLP_GROUP_DIM = GMLP_WIDTH // GMLP_GROUPS
GMLP_CHUNK = 128
LRU_WIDTH = D_MODEL
LRU_HEADS = 8
LRU_HEAD_DIM = LRU_WIDTH // LRU_HEADS
LRU_C = 8.0
SSD_WIDTH = D_MODEL
SSD_HEAD_DIM = 64
SSD_HEADS = SSD_WIDTH // SSD_HEAD_DIM
SSD_GROUPS = 4
SSD_HEADS_PER_GROUP = SSD_HEADS // SSD_GROUPS
SSD_STATE = 128
SSD_CHUNK = 128
SSD_CONV_DIM = SSD_WIDTH + 2 * SSD_GROUPS * SSD_STATE
MLP_HIDDEN = 4 * D_MODEL
GMLP_IN = 2 * GMLP_WIDTH
LRU_IN = 2 * LRU_WIDTH
SSD_IN = SSD_WIDTH + SSD_CONV_DIM + SSD_HEADS
GATE_IN = N_BRANCHES * D_MODEL
D_IN = GMLP_IN + LRU_IN + SSD_IN + GATE_IN
SPLIT_POINTS = (GMLP_IN,
                GMLP_IN + LRU_IN,
                GMLP_IN + LRU_IN + SSD_WIDTH,
                GMLP_IN + LRU_IN + SSD_WIDTH + SSD_CONV_DIM,
                GMLP_IN + LRU_IN + SSD_IN)


def rms_norm(x, g):
    x32 = x.astype(jnp.float32)
    y = x32 * lax.rsqrt(jnp.mean(x32 * x32, axis=-1, keepdims=True) + EPS)
    return (y * g.astype(jnp.float32)).astype(x.dtype)

def layer_norm(x, g, b):
    x32 = x.astype(jnp.float32)
    mu = jnp.mean(x32, axis=-1, keepdims=True)
    xc = x32 - mu
    y = xc * lax.rsqrt(jnp.mean(xc * xc, axis=-1, keepdims=True) + EPS)
    return (y * g.astype(jnp.float32) + b.astype(jnp.float32)).astype(x.dtype)

def causal_dwconv(x, w, b):
    k, c = w.shape
    y = lax.conv_general_dilated(x, w[:, None, :], window_strides=(1,), padding=[(k - 1, 0)],
                                 dimension_numbers=('NWC', 'WIO', 'NWC'), feature_group_count=c)
    return y + b

def gmlp_mixer(za, ln_g, ln_b, w_s, b_s):
    bsz, seq, _ = za.shape
    u, v = jnp.split(jax.nn.gelu(za), 2, axis=-1)
    v = layer_norm(v, ln_g, ln_b)
    nc = seq // GMLP_CHUNK
    vc = v.reshape(bsz, nc, GMLP_CHUNK, GMLP_GROUPS, GMLP_GROUP_DIM)
    causal = jnp.tril(jnp.ones((GMLP_CHUNK, GMLP_CHUNK), dtype=bool))
    w = jnp.where(causal, w_s, 0)
    mixed = jnp.einsum('gts,bcsgd->bctgd', w, vc) + b_s.T[:, :, None]
    return u * mixed.reshape(bsz, seq, GMLP_WIDTH)

def rg_lru_mixer(zb, conv_w, conv_b, w_r, b_r, w_i, b_i, lam):
    bsz, seq, _ = zb.shape
    xb, gate = jnp.split(zb, 2, axis=-1)
    xb = causal_dwconv(xb, conv_w, conv_b)
    xh = xb.reshape(bsz, seq, LRU_HEADS, LRU_HEAD_DIM)
    r = jax.nn.sigmoid(jnp.einsum('bshi,hij->bshj', xh, w_r).reshape(bsz, seq, LRU_WIDTH) + b_r)
    i = jax.nn.sigmoid(jnp.einsum('bshi,hij->bshj', xh, w_i).reshape(bsz, seq, LRU_WIDTH) + b_i)
    log_a = -LRU_C * r.astype(jnp.float32) * jax.nn.softplus(-lam.astype(jnp.float32))
    a = jnp.exp(log_a)
    inp = jnp.sqrt(-jnp.expm1(2.0 * log_a)) * (i * xb).astype(jnp.float32)

    def combine(c1, c2):
        a1, b1 = c1
        a2, b2 = c2
        return a1 * a2, a2 * b1 + b2

    _, h = lax.associative_scan(combine, (a, inp), axis=1)
    return jax.nn.gelu(gate) * h.astype(gate.dtype)

def segsum(x):
    t = x.shape[-1]
    cs = jnp.cumsum(x, axis=-1)
    seg = cs[..., :, None] - cs[..., None, :]
    return jnp.where(jnp.tril(jnp.ones((t, t), dtype=bool)), seg, -jnp.inf)

def ssd_mixer(z, xbc, dt_raw, conv_w, conv_b, dt_bias, a_log, d_skip, norm_g):
    bsz, seq, _ = z.shape
    nc = seq // SSD_CHUNK
    g, r, q = SSD_GROUPS, SSD_HEADS_PER_GROUP, SSD_CHUNK
    xbc = jax.nn.silu(causal_dwconv(xbc, conv_w, conv_b))
    xs, bm, cm = jnp.split(xbc, [SSD_WIDTH, SSD_WIDTH + g * SSD_STATE], axis=-1)
    dt = jax.nn.softplus((dt_raw + dt_bias).astype(jnp.float32))
    a = -jnp.exp(a_log.astype(jnp.float32))
    x32 = xs.astype(jnp.float32).reshape(bsz, nc, q, g, r, SSD_HEAD_DIM)
    xdt = x32 * dt.reshape(bsz, nc, q, g, r)[..., None]
    bc = bm.astype(jnp.float32).reshape(bsz, nc, q, g, SSD_STATE)
    cc = cm.astype(jnp.float32).reshape(bsz, nc, q, g, SSD_STATE)
    adt = (dt * a).reshape(bsz, nc, q, g, r).transpose(0, 3, 4, 1, 2)
    a_cs = jnp.cumsum(adt, axis=-1)
    decay = jnp.exp(segsum(adt))
    cb = jnp.einsum('bclgn,bcsgn->bgcls', cc, bc)
    y_diag = jnp.einsum('bgcls,bgrcls,bcsgrp->bclgrp', cb, decay, xdt)
    decay_states = jnp.exp(a_cs[..., -1:] - a_cs)
    states = jnp.einsum('bcsgn,bgrcs,bcsgrp->cbgrpn', bc, decay_states, xdt)
    chunk_decay = jnp.exp(a_cs[..., -1]).transpose(3, 0, 1, 2)

    def step(h, inp):
        dec, st = inp
        return h * dec[..., None, None] + st, h

    _, prev = lax.scan(step, jnp.zeros_like(states[0]), (chunk_decay, states))
    y_off = jnp.einsum('bclgn,cbgrpn,bgrcl->bclgrp', cc, prev, jnp.exp(a_cs))
    y = y_diag + y_off + x32 * d_skip.astype(jnp.float32).reshape(g, r)[:, :, None]
    y = y.reshape(bsz, seq, SSD_WIDTH) * jax.nn.silu(z.astype(jnp.float32))
    yg = y.reshape(bsz, seq, g, SSD_WIDTH // g)
    yg = yg * lax.rsqrt(jnp.mean(yg * yg, axis=-1, keepdims=True) + EPS)
    y = yg.reshape(bsz, seq, SSD_WIDTH) * norm_g.astype(jnp.float32)
    return y.astype(z.dtype)

def _normal(k, shape, scale):
    return scale * jax.random.normal(k, shape, jnp.float32)

def second_inputs(seed: int = 0) -> dict:
    key = jax.random.key(seed)
    ks = jax.random.split(key, 32)
    L = DEPTH_2
    a0 = jax.random.uniform(ks[15], (L, LRU_WIDTH), jnp.float32, minval=0.9, maxval=0.999)
    dt0 = jnp.exp(jax.random.uniform(ks[18], (L, SSD_HEADS), jnp.float32,
                                     minval=math.log(1e-3), maxval=math.log(1e-1)))
    return {
        'x': _normal(ks[0], (BATCH, SEQ, D_MODEL), 1.0),
        'norm_mix_g': 1.0 + _normal(ks[1], (L, D_MODEL), 0.1),
        'w_in': _normal(ks[2], (L, D_MODEL, D_IN), D_MODEL ** -0.5),
        'b_gate': _normal(ks[3], (L, N_BRANCHES, D_MODEL), 0.1),
        'gmlp_ln_g': 1.0 + _normal(ks[4], (L, GMLP_WIDTH), 0.1),
        'gmlp_ln_b': _normal(ks[5], (L, GMLP_WIDTH), 0.1),
        'gmlp_w_s': _normal(ks[6], (L, GMLP_GROUPS, GMLP_CHUNK, GMLP_CHUNK), GMLP_CHUNK ** -0.5),
        'gmlp_b_s': 1.0 + _normal(ks[7], (L, GMLP_GROUPS, GMLP_CHUNK), 0.1),
        'lru_conv_w': _normal(ks[8], (L, CONV_WIDTH, LRU_WIDTH), CONV_WIDTH ** -0.5),
        'lru_conv_b': _normal(ks[9], (L, LRU_WIDTH), 0.1),
        'lru_w_r': _normal(ks[10], (L, LRU_HEADS, LRU_HEAD_DIM, LRU_HEAD_DIM), LRU_HEAD_DIM ** -0.5),
        'lru_b_r': _normal(ks[11], (L, LRU_WIDTH), 0.1),
        'lru_w_i': _normal(ks[12], (L, LRU_HEADS, LRU_HEAD_DIM, LRU_HEAD_DIM), LRU_HEAD_DIM ** -0.5),
        'lru_b_i': _normal(ks[13], (L, LRU_WIDTH), 0.1),
        'lru_lambda': jnp.log(a0) - jnp.log1p(-a0),
        'ssd_conv_w': _normal(ks[16], (L, CONV_WIDTH, SSD_CONV_DIM), CONV_WIDTH ** -0.5),
        'ssd_conv_b': _normal(ks[17], (L, SSD_CONV_DIM), 0.1),
        'ssd_dt_bias': dt0 + jnp.log(-jnp.expm1(-dt0)),
        'ssd_a_log': jnp.log(jax.random.uniform(ks[19], (L, SSD_HEADS), jnp.float32, minval=1.0, maxval=16.0)),
        'ssd_d': 1.0 + _normal(ks[20], (L, SSD_HEADS), 0.1),
        'ssd_norm_g': 1.0 + _normal(ks[21], (L, SSD_WIDTH), 0.1),
        'w_branch_a': _normal(ks[22], (L, GMLP_WIDTH, D_MODEL), GMLP_WIDTH ** -0.5),
        'w_branch_b': _normal(ks[23], (L, LRU_WIDTH, D_MODEL), LRU_WIDTH ** -0.5),
        'w_branch_c': _normal(ks[24], (L, SSD_WIDTH, D_MODEL), SSD_WIDTH ** -0.5),
        'w_out': _normal(ks[25], (L, D_MODEL, D_MODEL), D_MODEL ** -0.5),
        'norm_mlp_g': 1.0 + _normal(ks[26], (L, D_MODEL), 0.1),
        'w_mlp_up': _normal(ks[27], (L, D_MODEL, MLP_HIDDEN), D_MODEL ** -0.5),
        'w_mlp_down': _normal(ks[28], (L, MLP_HIDDEN, D_MODEL), MLP_HIDDEN ** -0.5),
        'final_norm_g': 1.0 + _normal(ks[29], (D_MODEL,), 0.1),
    }

def second_block(x, norm_mix_g, w_in, b_gate, gmlp_ln_g, gmlp_ln_b, gmlp_w_s, gmlp_b_s,
              lru_conv_w, lru_conv_b, lru_w_r, lru_b_r, lru_w_i, lru_b_i, lru_lambda,
              ssd_conv_w, ssd_conv_b, ssd_dt_bias, ssd_a_log, ssd_d, ssd_norm_g,
              w_branch_a, w_branch_b, w_branch_c, w_out, norm_mlp_g, w_mlp_up, w_mlp_down,
              final_norm_g):
    bsz, seq, _ = x.shape
    h = x
    for l in range(DEPTH_2):
        hn = rms_norm(h, norm_mix_g[l])
        proj = jnp.einsum('bsd,de->bse', hn, w_in[l])
        za, zb, zc, xbc, dt_raw, g_raw = jnp.split(proj, SPLIT_POINTS, axis=-1)
        ya = gmlp_mixer(za, gmlp_ln_g[l], gmlp_ln_b[l], gmlp_w_s[l], gmlp_b_s[l])
        yb = rg_lru_mixer(zb, lru_conv_w[l], lru_conv_b[l], lru_w_r[l], lru_b_r[l],
                          lru_w_i[l], lru_b_i[l], lru_lambda[l])
        yc = ssd_mixer(zc, xbc, dt_raw, ssd_conv_w[l], ssd_conv_b[l], ssd_dt_bias[l],
                       ssd_a_log[l], ssd_d[l], ssd_norm_g[l])
        gates = jax.nn.sigmoid(g_raw.reshape(bsz, seq, N_BRANCHES, D_MODEL) + b_gate[l])
        merged = (gates[:, :, 0] * jnp.einsum('bse,ed->bsd', ya, w_branch_a[l])
                  + gates[:, :, 1] * jnp.einsum('bse,ed->bsd', yb, w_branch_b[l])
                  + gates[:, :, 2] * jnp.einsum('bse,ed->bsd', yc, w_branch_c[l]))
        h = h + jnp.einsum('bsd,de->bse', merged, w_out[l])
        hn = rms_norm(h, norm_mlp_g[l])
        up = jax.nn.relu(jnp.einsum('bsd,df->bsf', hn, w_mlp_up[l]))
        h = h + jnp.einsum('bsf,fd->bsd', up * up, w_mlp_down[l])
    return rms_norm(h, final_norm_g)


def setup_inputs(seed=0):
    out = dict(first_inputs(seed))
    for name, value in second_inputs(seed + 1).items():
        if name != "x":
            out[name + "_2"] = value
    return out


def reference(
    x, c, ctx, c_ctx, w_mod, b_mod, ln_w, ln_b, ab_w_in, ab_gate_b, ab_norm_w, ab_sink,
    ab_w_out, gla_w_in, gla_gate_up, gla_gate_b, gla_norm_w, gla_w_out, peer_wq, peer_keys,
    peer_u, peer_v, norm_mix_g_2, w_in_2, b_gate_2, gmlp_ln_g_2, gmlp_ln_b_2, gmlp_w_s_2,
    gmlp_b_s_2, lru_conv_w_2, lru_conv_b_2, lru_w_r_2, lru_b_r_2, lru_w_i_2, lru_b_i_2,
    lru_lambda_2, ssd_conv_w_2, ssd_conv_b_2, ssd_dt_bias_2, ssd_a_log_2, ssd_d_2, ssd_norm_g_2,
    w_branch_a_2, w_branch_b_2, w_branch_c_2, w_out_2, norm_mlp_g_2, w_mlp_up_2, w_mlp_down_2,
    final_norm_g_2,
):
    x = first_block(
        x, c, ctx, c_ctx, w_mod, b_mod, ln_w, ln_b, ab_w_in, ab_gate_b, ab_norm_w, ab_sink,
        ab_w_out, gla_w_in, gla_gate_up, gla_gate_b, gla_norm_w, gla_w_out, peer_wq, peer_keys,
        peer_u, peer_v,
    )
    return second_block(
        x, norm_mix_g_2, w_in_2, b_gate_2, gmlp_ln_g_2, gmlp_ln_b_2, gmlp_w_s_2, gmlp_b_s_2,
        lru_conv_w_2, lru_conv_b_2, lru_w_r_2, lru_b_r_2, lru_w_i_2, lru_b_i_2, lru_lambda_2,
        ssd_conv_w_2, ssd_conv_b_2, ssd_dt_bias_2, ssd_a_log_2, ssd_d_2, ssd_norm_g_2,
        w_branch_a_2, w_branch_b_2, w_branch_c_2, w_out_2, norm_mlp_g_2, w_mlp_up_2,
        w_mlp_down_2, final_norm_g_2,
    )


_drawn_inputs = setup_inputs


def setup_inputs(seed=0):
    import zlib

    import numpy as np

    out = dict(_drawn_inputs(seed))
    spreads = {}
    factors = {'b_mod': 4.77,
     'ab_norm_w': 8.0,
     'ab_sink': 8.0,
     'gla_gate_up': 3.091,
     'gla_norm_w': 8.0,
     'peer_wq': 5.851,
     'peer_keys': 5.783,
     'peer_u': 6.449,
     'peer_v': 5.739,
     'lru_b_r_2': 8.0,
     'lru_b_i_2': 7.497,
     'gmlp_ln_g_2': 2.722,
     'gmlp_ln_b_2': 3.053}
    for name, (base, spread) in spreads.items():
        noise = np.random.default_rng([zlib.crc32(name.encode()), seed]).standard_normal(out[name].shape)
        drawn = base * np.exp(spread * noise) if base else spread * noise
        out[name] = __import__('jax').numpy.asarray(drawn.astype(out[name].dtype))
    for name, factor in factors.items():
        out[name] = (out[name] * factor).astype(out[name].dtype)
    return out
```

```python
import math
from contextlib import ExitStack, contextmanager

import numpy as np

import concourse.bass as bass
from concourse import mybir
from concourse.alu_op_type import AluOpType as ALU

F32 = mybir.dt.float32
U32 = mybir.dt.uint32
ACT = mybir.ActivationFunctionType
AX_X = mybir.AxisListType.X

P = 128
D = 1024
KC = D // P
SEQ = 256
CTX = 256
TOK = CTX + SEQ
TT = TOK // P
BANK = 512
DEPTH = 2
ALPHA = (2 * DEPTH) ** 0.25
LN_EPS = 1e-5
EPS2 = 1e-6
BIG = 1e30
N_EXPERTS = 128 * 128


def ds(start, size):
    return bass.ds(start, size)


class Stage:

    def __init__(self, nc, name, ctx):
        self.nc, self.name, self.ctx, self.sems = nc, name, ctx, []

    def sem(self, name):
        s = self.ctx.enter_context(self.nc.semaphore(f"{self.name}_{name}"))
        self.sems.append(s)
        return s

    def sb(self, name, shape, dt=F32):
        return self.ctx.enter_context(self.nc.sbuf_tensor(f"{self.name}_{name}", shape, dt))

    def ps(self, name, shape, dt=F32):
        return self.ctx.enter_context(self.nc.psum_tensor(f"{self.name}_{name}", shape, dt))


@contextmanager
def stage(nc, name):
    with ExitStack() as ctx:
        st = Stage(nc, name, ctx)
        yield st
        for s in st.sems:
            nc.gpsimd.sem_clear(s)
        nc.all_engine_barrier()


class Link:

    def __init__(self, eng, sem, base=0):
        self.eng, self.sem, self.n = eng, sem, base

    def __call__(self, ins):
        self.n = self.n + 1
        ins.then_inc(self.sem, 1)
        self.eng.wait_ge(self.sem, self.n)


def stage_load(nc, name, pairs):
    with stage(nc, name) as st:
        loaded = st.sem("loaded")
        with nc.Block() as block:
            @block.sync
            def _(sp):
                for dst, src in pairs:
                    sp.dma_start(dst, src).then_inc(loaded, 16)
                sp.wait_ge(loaded, 16 * len(pairs))


def stage_linear(nc, name, act_t, tiles, w, n_cols, out, feature=False, func=None, kb=1):
    n_tok = tiles[-1][0] + tiles[-1][1]
    full, tail = divmod(n_cols, BANK)
    w_rows = w.rearrange("(b k p) n -> b p k n", p=P, k=KC)
    if feature:
        flat = out.rearrange("p f t -> p (f t)")
    else:
        flat = out.rearrange("p m n -> p (m n)")

    def banks(width):
        if feature:
            return [(f, P, n_tok) for f in range(width // P)]
        return [(m, size, width) for m, (_, size) in enumerate(tiles)]

    def where(n0, b, size):
        if feature:
            return ds((n0 // P + b) * n_tok if isinstance(n0, int) else n0 * n_tok // P + b * n_tok, size)
        return ds(b * n_cols + n0, size)

    both = func is None and len(banks(BANK)) > 1
    with stage(nc, name) as st:
        wt = st.sb("weights", [P, 2, KC, BANK])
        acc = st.ps("acc", [P, 2, 4, BANK])
        w_loaded = [st.sem("w_loaded0"), st.sem("w_loaded1")]
        mm_done = st.sem("mm_done")
        act_out = st.sem("act_out")
        dve_out = st.sem("dve_out")

        def load(sp, n, n0, width, slot, turn, b=0):
            sp.wait_ge(mm_done, n + 1)
            sp.dma_start(wt[:, slot, :, 0:width], w_rows[b][:, :, ds(n0, width)]).then_inc(w_loaded[slot], 16)

        def multiply(pe, n, width, slot, turn, half, b, t):
            pe.wait_ge(w_loaded[slot], 16 * turn + 16)
            if b == 0:
                pe.wait_ge(act_out, t + 1)
                if both:
                    pe.wait_ge(dve_out, t + 1)
            last = None
            for bank, rows, cols in banks(width):
                for k in range(KC):
                    a = act_t[:, b * KC + k, tiles[bank][0]:tiles[bank][0] + rows] if not feature else act_t[:, b * KC + k, 0:n_tok]
                    wv = wt[:, slot, k, bank * P:(bank + 1) * P] if feature else wt[:, slot, k, 0:width]
                    lhs, rhs = (wv, a) if feature else (a, wv)
                    last = nc.tensor.matmul(acc[0:rows, half, bank, 0:cols], lhs, rhs,
                                            start=(b == 0 and k == 0), stop=(b == kb - 1 and k == KC - 1))
            last.then_inc(mm_done, 1)

        def empty(eng, mine, n_steps, n0, width, half, dve):
            eng.wait_ge(mm_done, n_steps + 2)
            todo = [x for x in banks(width) if not both or x[0] % 2 == (1 if dve else 0)]
            for i, (bank, rows, cols) in enumerate(todo):
                dst, src = flat[0:rows, where(n0, bank, cols)], acc[0:rows, half, bank, 0:cols]
                if dve:
                    ins = nc.vector.tensor_copy(dst, src)
                else:
                    ins = nc.scalar.activation(dst, src, func or ACT.Copy)
                if i == len(todo) - 1:
                    ins.then_inc(mine, 1)
            if not todo:
                eng.sem_inc(mine, 1)

        looped = kb == 1 and full >= 4
        pairs = full // 2 if looped else 0
        rest = list(range(2 * pairs, full + (1 if tail else 0)))

        def run(eng, one):
            if pairs:
                with eng.Fori(0, pairs) as i:
                    for s in range(2):
                        one(i * 2 + s, i * (2 * BANK) + s * BANK, BANK, s, i)
            for t in rest:
                one(t, t * BANK, tail if t == full else BANK, t % 2, t // 2)

        with nc.Block() as block:
            @block.sync
            def _(sp):
                def one(t, n0, width, half, turn):
                    for b in range(kb):
                        s = t * kb + b
                        slot = s % 2 if kb > 1 else half
                        load(sp, s, n0, width, slot, s // 2 if kb > 1 else turn, b)
                run(sp, one)

            @block.tensor
            def _(pe):
                pe.sem_inc(mm_done, 2)

                def one(t, n0, width, half, turn):
                    for b in range(kb):
                        s = t * kb + b
                        slot = s % 2 if kb > 1 else half
                        multiply(pe, s, width, slot, s // 2 if kb > 1 else turn, half, b, t)
                run(pe, one)

            @block.scalar
            def _(act):
                act.sem_inc(act_out, 2)
                run(act, lambda t, n0, width, half, turn: empty(act, act_out, t * kb + kb, n0, width, half, False))

            @block.vector
            def _(dve):
                dve.sem_inc(dve_out, 2)
                if both:
                    run(dve, lambda t, n0, width, half, turn: empty(dve, dve_out, t * kb + kb, n0, width, half, True))


def stage_transpose(nc, name, ident, src, dst, tiles, chunks, mod=None, x=None):
    with stage(nc, name) as st:
        loaded = st.sem("loaded")
        made = st.sem("made")
        turned = st.sem("turned")
        emptied = st.sem("emptied")
        chain = st.sem("chain")
        ps = st.ps("turned", [P, 4, 4, P])
        rows = st.sb("rows", [P, 4, D]) if mod else None
        per = min(4, chunks)
        quads = [(m, q) for m in range(len(tiles)) for q in range(chunks // per)]
        with nc.Block() as block:
            if mod:
                @block.sync
                def _(sp):
                    for i, (_, scale, shift) in enumerate(mod):
                        sp.dma_start(rows[:, 2 * i, :], scale.partition_broadcast(P)).then_inc(loaded, 16)
                        sp.dma_start(rows[:, 2 * i + 1, :], shift.partition_broadcast(P)).then_inc(loaded, 16)

                @block.vector
                def _(dve):
                    link = Link(dve, chain)
                    dve.wait_ge(loaded, 32 * len(mod))
                    for i, (ms, _, _) in enumerate(mod):
                        for m in ms:
                            link(nc.vector.tensor_tensor(src[:, m, :], x[:, m, :], rows[:, 2 * i, :], ALU.mult))
                            nc.vector.tensor_tensor(src[:, m, :], src[:, m, :], rows[:, 2 * i + 1, :], ALU.add).then_inc(made, 1)

            @block.tensor
            def _(pe):
                for i, (m, q) in enumerate(quads):
                    if mod:
                        pe.wait_ge(made, m + 1)
                    if i >= 4:
                        pe.wait_ge(emptied, i - 3)
                    for k in range(per):
                        c = per * q + k
                        last = nc.tensor.transpose(ps[:, i % 4, k, :], src[:, tiles[m], c * P:(c + 1) * P], ident)
                    last.then_inc(turned, 1)

            @block.scalar
            def _(act):
                for i, (m, q) in enumerate(quads):
                    act.wait_ge(turned, i + 1)
                    nc.scalar.activation(dst[:, per * q:per * q + per, m * P:(m + 1) * P], ps[:, i % 4, 0:per, :], ACT.Copy).then_inc(emptied, 1)


def stage_modulation(nc, c, c_ctx, w_mod, b_mod, mod_rows):
    n = 6 * D
    with stage(nc, "modc") as st:
        cols = st.sb("cols", [P, KC, 2])
        silu_c = st.sb("silu_c", [P, KC, 2])
        rows = st.sb("rows", [2, DEPTH, n])
        bias = st.sb("bias", [2, DEPTH, n])
        loaded, done = st.sem("loaded"), st.sem("done")
        with nc.Block() as block:
            @block.sync
            def _(sp):
                sp.dma_start(cols[:, :, 0], c.rearrange("a (k p) -> p (a k)", p=P), allow_slow_non_contiguous=True).then_inc(loaded, 16)
                sp.dma_start(cols[:, :, 1], c_ctx.rearrange("(k p) -> p k", p=P), allow_slow_non_contiguous=True).then_inc(loaded, 16)
                for i in range(DEPTH):
                    sp.dma_start(bias[:, i, :], b_mod[i:i + 1, :].rearrange("a n -> (a n)").partition_broadcast(2)).then_inc(loaded, 16)
                sp.wait_ge(loaded, 16 * (2 + DEPTH))

            @block.scalar
            def _(act):
                act.wait_ge(loaded, 16 * (2 + DEPTH))
                nc.scalar.activation(silu_c[:, :, :], cols[:, :, :], ACT.Silu).then_inc(done, 1)
        for i in range(DEPTH):
            stage_linear(nc, f"mod{i}", silu_c, [(0, 2)], w_mod[i], n, rows[:, i:i + 1, :])
        with stage(nc, "modb") as sb:
            chain, added, stored = sb.sem("chain"), sb.sem("added"), sb.sem("stored")
            with nc.Block() as block:
                @block.vector
                def _(dve):
                    link = Link(dve, chain)
                    for i in range(DEPTH):
                        link(nc.vector.tensor_tensor(rows[:, i, :], rows[:, i, :], bias[:, i, :], ALU.add))
                        for s in (1, 4):
                            part = rows[:, i, s * D:(s + 1) * D]
                            link(nc.vector.tensor_scalar(part, part, 1.0, None, ALU.add))
                    dve.sem_inc(added, 1)

                @block.sync
                def _(sp):
                    sp.wait_ge(added, 1)
                    sp.dma_start(mod_rows.rearrange("l c n -> c l n"), rows[:, :, :]).then_inc(stored, 16)
                    sp.wait_ge(stored, 16)


def stage_residual_norm(nc, name, x, y, tiles, gates, ln_w, ln_b):
    with stage(nc, name) as st:
        loaded, chain, var_ready, std_ready = st.sem("loaded"), st.sem("chain"), st.sem("var_ready"), st.sem("std_ready")
        rows = st.sb("rows", [P, 2 + len(gates), D])
        stats = st.sb("stats", [P, 2, 6])
        agg = st.sb("agg", [P, 4, 2])
        std = st.sb("std", [P, 4])
        rstd = st.sb("rstd", [P, 4])
        gate_of = {m: 2 + i for i, (ms, _) in enumerate(gates) for m in ms}
        with nc.Block() as block:
            @block.sync
            def _(sp):
                for i, src in enumerate([ln_w, ln_b] + [g for _, g in gates]):
                    sp.dma_start(rows[:, i, :], src.partition_broadcast(P)).then_inc(loaded, 16)

            @block.vector
            def _(dve):
                link = Link(dve, chain)
                dve.wait_ge(loaded, 16 * (2 + len(gates)))
                for i, (m, ym) in enumerate(tiles):
                    link(nc.vector.tensor_tensor(y[:, ym, :], y[:, ym, :], rows[:, gate_of[m], :], ALU.mult))
                    link(nc.vector.scalar_tensor_tensor(x[:, m, :], x[:, m, :], ALPHA, y[:, ym, :], ALU.mult, ALU.add))
                    nc.vector.bn_stats(stats[:, 0, :], x[:, m, 0:BANK]).then_inc(chain, 1)
                    link.n += 1
                    link(nc.vector.bn_stats(stats[:, 1, :], x[:, m, BANK:D]))
                    link(nc.vector.bn_aggr(agg[:, i, :], stats[:, :, :].rearrange("p a b -> p (a b)")))
                    nc.vector.tensor_scalar(agg[:, i, 1:2], agg[:, i, 1:2], LN_EPS, None, ALU.add).then_inc(var_ready, 1)
                for i, (m, ym) in enumerate(tiles):
                    dve.wait_ge(std_ready, i + 1)
                    link(nc.vector.reciprocal(rstd[:, i:i + 1], std[:, i:i + 1]))
                    link(nc.vector.tensor_scalar(x[:, m, :], x[:, m, :], agg[:, i, 0:1], rstd[:, i:i + 1], ALU.subtract, ALU.mult))
                    link(nc.vector.tensor_tensor(x[:, m, :], x[:, m, :], rows[:, 0, :], ALU.mult))
                    link(nc.vector.tensor_tensor(x[:, m, :], x[:, m, :], rows[:, 1, :], ALU.add))

            @block.scalar
            def _(act):
                for i in range(len(tiles)):
                    act.wait_ge(var_ready, i + 1)
                    nc.scalar.activation(std[:, i:i + 1], agg[:, i, 1:2], ACT.Sqrt).then_inc(std_ready, 1)


H_M = 4
H_A, H_KV, DH_A = 8, 2, 64
GROUP = H_A // H_KV
M_W = H_M * P
A_Q = H_A * DH_A
A_KV = H_KV * DH_A

SEEN = [{0: [(1, 4)], 1: [(2, 4)], 2: [(3, 4)], 3: []},
        {0: [(2, 4)], 1: [(0, 1), (2, 4)], 2: [], 3: [(2, 3)]}]


def sources(d, t):
    return [s for s in range(TT) if s == t or any(a <= t < b for a, b in SEEN[d][s])]


def reversed_time(ap2, seg):
    a = ap2[:, seg * SEQ:(seg + 1) * SEQ]
    return a[:, ::-1]


def stage_gates(nc, act_t, w, gate_b, ident, sel, g_cols, m_rows):
    with stage(nc, "gates") as st:
        wg = st.sb("w", [P, KC, 16])
        bias = st.sb("bias", [4, 4])
        g = st.sb("g", [4, 4, TOK])
        tmp = st.sb("tmp", [4, 2, TOK])
        lf = st.sb("lf", [4, 2, TOK])
        scan = st.sb("scan", [4, 2, 4, TOK])
        zero_one = st.sb("zero_one", [4, 2, TOK])
        mm = st.sb("mm", [4, 2, 2, TOK])
        rows = st.sb("rows", [4, 2, 2, TOK])
        ps = st.ps("ps", [P, 4, BANK])
        pc = st.ps("pc", [P, 2, TT, 2, 4])
        loaded, mm_done, g_ready = st.sem("loaded"), st.sem("mm_done"), st.sem("g_ready")
        ln_ready, chain, m_ready, e_ready, rows_ready, cols_done = (
            st.sem(x) for x in ("ln_ready", "chain", "m_ready", "e_ready", "rows_ready", "cols_done"))
        achain = st.sem("achain")
        with nc.Block() as block:
            @block.sync
            def _(sp):
                sp.dma_start(wg[:, :, :], w.rearrange("(k p) n -> p k n", p=P)).then_inc(loaded, 16)
                sp.dma_start(bias[:, :], gate_b.rearrange("d y h -> h (d y)"), allow_slow_non_contiguous=True).then_inc(loaded, 16)

            @block.tensor
            def _(pe):
                pe.wait_ge(loaded, 32)
                for j in range(4):
                    for k in range(KC):
                        last = nc.tensor.matmul(ps[0:4, j, :], wg[:, k, 4 * j:4 * j + 4], act_t[:, k, 0:TOK],
                                                start=(k == 0), stop=(k == KC - 1))
                last.then_inc(mm_done, 1)
                pe.wait_ge(rows_ready, 1)
                for d in range(2):
                    for m in range(TT):
                        for y in range(2):
                            last = nc.tensor.matmul(pc[:, d, m, y, :], rows[:, d, y, m * P:(m + 1) * P], ident[0:4, 0:4],
                                                    start=True, stop=True)
                last.then_inc(cols_done, 1)

            @block.scalar
            def _(act):
                link = Link(act, achain)
                act.wait_ge(mm_done, 1)
                for j in range(4):
                    link(nc.scalar.activation(g[:, j, :], ps[0:4, j, :], ACT.Identity, bias=bias[:, j:j + 1]))
                for d in range(2):
                    link(nc.scalar.activation(tmp[:, d, :], g[:, 2 * d + 1, :], ACT.Abs))
                    link(nc.scalar.activation(tmp[:, d, :], tmp[:, d, :], ACT.Exp, scale=-1.0))
                    nc.scalar.activation(tmp[:, d, :], tmp[:, d, :], ACT.Ln, bias=1.0).then_inc(ln_ready, 1)
                for d in range(2):
                    act.wait_ge(m_ready, d + 1)
                    nc.scalar.activation(mm[:, d, 1, :], mm[:, d, 1, :], ACT.Exp, scale=-1.0).then_inc(e_ready, 1)

            @block.vector
            def _(dve):
                link = Link(dve, chain)
                link(nc.vector.memset(zero_one[:, 0, :], 0.0))
                link(nc.vector.memset(zero_one[:, 1, :], 1.0))
                for d in range(2):
                    dve.wait_ge(ln_ready, d + 1)
                    link(nc.vector.scalar_tensor_tensor(lf[:, d, :], g[:, 2 * d + 1, :], 0.0, tmp[:, d, :], ALU.min, ALU.subtract))
                    for seg in range(2):
                        sl = slice(seg * SEQ, (seg + 1) * SEQ)
                        src = (lambda ap: ap[:, sl]) if d == 0 else (lambda ap: reversed_time(ap, seg))
                        link(nc.vector.tensor_copy(scan[:, d, 0, sl], src(lf[:, d, :])))
                        link(nc.vector.tensor_copy(scan[:, d, 1, sl], src(g[:, 2 * d, :])))
                    link(nc.vector.tensor_tensor_scan(scan[:, d, 2, :], zero_one[:, 1, :], scan[:, d, 0, :], 0.0, ALU.mult, ALU.add))
                    link(nc.vector.tensor_tensor(scan[:, d, 3, :], scan[:, d, 1, :], scan[:, d, 2, :], ALU.subtract))
                    link(nc.vector.tensor_tensor_scan(mm[:, d, 0, :], zero_one[:, 0, :], scan[:, d, 3, :], 0.0, ALU.add, ALU.max))
                    nc.vector.tensor_tensor(mm[:, d, 1, :], mm[:, d, 0, :], scan[:, d, 2, :], ALU.add).then_inc(m_ready, 1)
                for d in range(2):
                    dve.wait_ge(e_ready, d + 1)
                    for seg in range(2):
                        sl = slice(seg * SEQ, (seg + 1) * SEQ)
                        src = (lambda ap: ap[:, sl]) if d == 0 else (lambda ap: reversed_time(ap, seg))
                        link(nc.vector.tensor_copy(rows[:, d, 0, sl], src(scan[:, d, 3, :])))
                        link(nc.vector.tensor_copy(rows[:, d, 1, sl], src(mm[:, d, 1, :])))
                        link(nc.vector.tensor_copy(m_rows[:, d, sl], src(mm[:, d, 0, :])))
                dve.sem_inc(rows_ready, 1)
                dve.wait_ge(cols_done, 1)
                nc.vector.tensor_copy(g_cols[:, :, :, :, :].rearrange("p d m y h -> p (d m y h)"),
                                      pc[:, :, :, :, :].rearrange("p d m y h -> p (d m y h)"))


def stage_mlstm(nc, qk_t, v_aug, g_cols, m_rows, sel, far, hm):
    with stage(nc, "mlstm") as st:
        m_far = st.sb("m_far", [P, TOK])
        e = st.sb("e", [P, TT, TOK])
        w = st.sb("w", [P, TT, TOK])
        den = st.sb("den", [P, TT])
        ps_s = st.ps("scores", [P, TT, BANK])
        ps_m = st.ps("m_bcast", [P, BANK])
        ps_o = st.ps("out", [P, 2, BANK])
        scored, m_sent, far_ready, e_ready, w_ready, out_done, out_taken, chain = (
            st.sem(x) for x in ("scored", "m_sent", "far_ready", "e_ready", "w_ready", "out_done", "out_taken", "chain"))
        units = [(h, d) for h in range(H_M) for d in range(2)]

        def out_ap(t, cols):
            return ps_o[:, t // 2, (t % 2) * 256:(t % 2) * 256 + cols]

        with nc.Block() as block:
            @block.tensor
            def _(pe):
                for u, (h, d) in enumerate(units):
                    if u:
                        pe.wait_ge(w_ready, u)
                    if d == 0:
                        for s in range(TT):
                            last = nc.tensor.matmul(ps_s[:, s, :], qk_t[:, H_M + h, s * P:(s + 1) * P], qk_t[:, h, :],
                                                    start=True, stop=True)
                        last.then_inc(scored, 1)
                    nc.tensor.matmul(ps_m[:, :], sel[0:4, h, :], m_rows[:, d, :], start=True, stop=True).then_inc(m_sent, 1)
                    pe.wait_ge(w_ready, u + 1)
                    if u:
                        pe.wait_ge(out_taken, u)
                    for t in range(TT):
                        src = sources(d, t)
                        for s in src:
                            last = nc.tensor.matmul(out_ap(t, P + 1), w[:, s, t * P:(t + 1) * P], v_aug[:, s, h, 0:P + 1],
                                                    start=(s == src[0]), stop=(s == src[-1]))
                    last.then_inc(out_done, 1)

            @block.scalar
            def _(act):
                for u, (h, d) in enumerate(units):
                    act.wait_ge(m_sent, u + 1)
                    act.wait_ge(far_ready, u + 1)
                    if u:
                        act.wait_ge(w_ready, u)
                    for s in range(TT):
                        a = g_cols[:, d, s, 0, h:h + 1]
                        last = nc.scalar.activation(e[:, s, s * P:(s + 1) * P], m_far[:, s * P:(s + 1) * P], ACT.Exp, bias=a, scale=-1.0)
                        for t0, t1 in SEEN[d][s]:
                            last = nc.scalar.activation(e[:, s, t0 * P:t1 * P], ps_m[:, t0 * P:t1 * P], ACT.Exp, bias=a, scale=-1.0)
                    last.then_inc(e_ready, 1)

            @block.vector
            def _(dve):
                link = Link(dve, chain)
                for u, (h, d) in enumerate(units):
                    dve.wait_ge(m_sent, u + 1)
                    if u:
                        dve.wait_ge(e_ready, u)
                    nc.vector.tensor_tensor(m_far[:, :], ps_m[:, :], far[:, d, :], ALU.add).then_inc(far_ready, 1)
                    dve.wait_ge(e_ready, u + 1)
                    dve.wait_ge(scored, h + 1)
                    if u:
                        dve.wait_ge(out_done, u)
                    for s in range(TT):
                        for t0, t1 in [(s, s + 1)] + SEEN[d][s]:
                            sl = slice(t0 * P, t1 * P)
                            last = nc.vector.scalar_tensor_tensor(w[:, s, sl], ps_s[:, s, sl], float(P) ** -0.5, e[:, s, sl], ALU.mult, ALU.mult)
                    last.then_inc(w_ready, 1)
                    dve.wait_ge(out_done, u + 1)
                    sums = ps_o[:, :, :].rearrange("p a (b c) -> p (a b) c", c=256)[:, :, P]
                    link(nc.vector.tensor_copy(den[:, :], sums))
                    link(nc.vector.scalar_tensor_tensor(den[:, :], den[:, :], -1.0, den[:, :], ALU.mult, ALU.max))
                    link(nc.vector.tensor_tensor(den[:, :], den[:, :], g_cols[:, d, :, 1, h], ALU.max))
                    link(nc.vector.reciprocal(den[:, :], den[:, :]))
                    for t in range(TT):
                        o = hm[:, t, h * P:(h + 1) * P]
                        if d == 0:
                            link(nc.vector.tensor_scalar(o, out_ap(t, P), den[:, t:t + 1], None, ALU.mult))
                        else:
                            link(nc.vector.scalar_tensor_tensor(o, out_ap(t, P), den[:, t:t + 1], o, ALU.mult, ALU.add))
                    dve.sem_inc(out_taken, 1)


def stage_value_ones(nc, name, v, v_aug):
    with stage(nc, name) as st:
        chain = st.sem("chain")
        with nc.Block() as block:
            @block.vector
            def _(dve):
                link = Link(dve, chain)
                link(nc.vector.memset(v_aug[:, :, :, P:P + 1].rearrange("p m h o -> p (m h) o"), 1.0))
                for m in range(TT):
                    link(nc.vector.tensor_copy(v_aug[:, m, :, 0:P], v[:, m, :].rearrange("p (h e) -> p h e", e=P)))


def stage_attention(nc, qkv, cos, sin, bars, sink, ident, cat):
    heads = H_A + H_KV
    scale = DH_A ** -0.5
    with stage(nc, "attn") as st:
        qr = st.sb("qr", [P, GROUP, H_KV, DH_A])
        kr = st.sb("kr", [P, H_KV, DH_A])
        t1, t2, t3, t4 = (st.sb(f"rot{i}", [P, heads, 32]) for i in range(4))
        qt = st.sb("qt", [P, GROUP, TOK])
        kt = st.sb("kt", [P, TOK])
        sink_b = st.sb("sink", [P, H_A])
        s_sb = st.sb("s", [P, 2, TOK])
        p_sb = st.sb("p", [P, 2, TOK])
        pt = st.sb("pt", [P, 2, TOK])
        small = st.sb("small", [P, 2, 8])
        ps_t = st.ps("turn", [P, 2, BANK])
        ps_s = st.ps("scores", [P, 2, BANK])
        ps_p = st.ps("p_turn", [P, 2, BANK])
        ps_o = st.ps("out", [P, 2, BANK])
        names = ("loaded", "rotated", "turned", "copied", "scored", "masked", "max_ready", "exped", "p_turned",
                 "p_copied", "out_done", "out_taken", "chain", "achain")
        loaded, rotated, turned, copied, scored, masked, max_ready, exped, p_turned, p_copied, out_done, out_taken, chain, achain = (
            st.sem(x) for x in names)
        units = [(m, kv, j) for m in range(TT) for kv in range(H_KV) for j in range(GROUP)]

        def keys(m):
            return CTX if m < 2 else TOK

        with nc.Block() as block:
            @block.sync
            def _(sp):
                sp.dma_start(sink_b[:, :], sink.partition_broadcast(P)).then_inc(loaded, 16)

            @block.tensor
            def _(pe):
                for m in range(TT):
                    pe.wait_ge(rotated, m + 1)
                    if m:
                        pe.wait_ge(copied, m)
                    for j in range(GROUP):
                        nc.tensor.transpose(ps_t[:, 0, j * P:(j + 1) * P], qr[:, j, :, :].rearrange("p a b -> p (a b)"), ident)
                    nc.tensor.transpose(ps_t[:, 1, 0:P], kr[:, :, :].rearrange("p a b -> p (a b)"), ident).then_inc(turned, 1)
                pe.wait_ge(copied, TT)

                def score(u):
                    m, kv, j = units[u]
                    if u >= 2:
                        pe.wait_ge(masked, u - 1)
                    rows = slice(kv * DH_A, (kv + 1) * DH_A)
                    nc.tensor.matmul(ps_s[:, u % 2, 0:keys(m)], qt[rows, j, m * P:(m + 1) * P], kt[rows, 0:keys(m)],
                                     start=True, stop=True).then_inc(scored, 1)

                score(0)
                for u, (m, kv, j) in enumerate(units):
                    if u + 1 < len(units):
                        score(u + 1)
                    pe.wait_ge(exped, u + 1)
                    if u >= 2:
                        pe.wait_ge(p_copied, u - 1)
                    for s in range(keys(m) // P):
                        last = nc.tensor.transpose(ps_p[:, u % 2, s * P:(s + 1) * P], p_sb[:, u % 2, s * P:(s + 1) * P], ident)
                    last.then_inc(p_turned, 1)
                    pe.wait_ge(p_copied, u + 1)
                    if u >= 2:
                        pe.wait_ge(out_taken, u - 1)
                    for s in range(keys(m) // P):
                        v = qkv[:, s, A_Q + A_KV + kv * DH_A:A_Q + A_KV + (kv + 1) * DH_A]
                        last = nc.tensor.matmul(ps_o[:, u % 2, 0:DH_A], pt[:, u % 2, s * P:(s + 1) * P], v,
                                                start=(s == 0), stop=(s == keys(m) // P - 1))
                    last.then_inc(out_done, 1)

            @block.scalar
            def _(act):
                link = Link(act, achain)
                for m in range(TT):
                    act.wait_ge(turned, m + 1)
                    link(nc.scalar.activation(qt[:, :, m * P:(m + 1) * P], ps_t[:, 0, :].rearrange("p (j t) -> p j t", t=P), ACT.Copy))
                    nc.scalar.activation(kt[:, m * P:(m + 1) * P], ps_t[:, 1, 0:P], ACT.Copy).then_inc(copied, 1)
                for u, (m, kv, j) in enumerate(units):
                    b, n = u % 2, keys(m)
                    act.wait_ge(max_ready, u + 1)
                    if u >= 2:
                        act.wait_ge(p_turned, u - 1)
                        act.wait_ge(out_taken, u - 1)
                    h = kv * GROUP + j
                    nc.scalar.activation(small[:, b, 3:4], sink_b[:, h:h + 1], ACT.Exp, bias=small[:, b, 1:2])
                    nc.scalar.activation(p_sb[:, b, 0:n], s_sb[:, b, 0:n], ACT.Exp, bias=small[:, b, 1:2], scale=scale,
                                         accum_out=small[:, b, 2:3]).then_inc(exped, 1)
                    act.wait_ge(p_turned, u + 1)
                    if u >= 2:
                        act.wait_ge(out_done, u - 1)
                    nc.scalar.activation(pt[:, b, 0:n], ps_p[:, b, 0:n], ACT.Copy).then_inc(p_copied, 1)

            @block.vector
            def _(dve):
                link = Link(dve, chain)
                for m in range(TT):
                    x = qkv[:, m, 0:heads * DH_A].rearrange("p (h r two) -> p h r two", two=2, r=32)
                    x1, x2 = x[:, :, :, 0], x[:, :, :, 1]
                    c = cos[:, m, :].unsqueeze(1).to_broadcast([P, heads, 32])
                    s = sin[:, m, :].unsqueeze(1).to_broadcast([P, heads, 32])
                    nc.vector.tensor_tensor(t1[:, :, :], x1, c, ALU.mult)
                    nc.vector.tensor_tensor(t2[:, :, :], x2, s, ALU.mult)
                    nc.vector.tensor_tensor(t3[:, :, :], x1, s, ALU.mult)
                    link(nc.vector.tensor_tensor(t4[:, :, :], x2, c, ALU.mult))
                    if m:
                        dve.wait_ge(turned, m)
                    for a, b, op, which in ((t1, t2, ALU.subtract, 0), (t3, t4, ALU.add, 1)):
                        for kv in range(H_KV):
                            hs = slice(kv * GROUP, (kv + 1) * GROUP)
                            o = qr[:, :, kv, :].rearrange("p j (r two) -> p j r two", two=2)[:, :, :, which]
                            nc.vector.tensor_tensor(o, a[:, hs, :], b[:, hs, :], op)
                        o = kr[:, :, :].rearrange("p j (r two) -> p j r two", two=2)[:, :, :, which]
                        link(nc.vector.tensor_tensor(o, a[:, H_A:heads, :], b[:, H_A:heads, :], op))
                    dve.sem_inc(rotated, 1)
                dve.wait_ge(loaded, 16)

                def first(u):
                    m, kv, j = units[u]
                    b, n = u % 2, keys(m)
                    h = kv * GROUP + j
                    dve.wait_ge(scored, u + 1)
                    if u >= 2:
                        dve.wait_ge(exped, u - 1)
                    if m < 2:
                        ins = nc.vector.tensor_copy(s_sb[:, b, 0:n], ps_s[:, b, 0:n])
                    else:
                        ins = nc.vector.tensor_tensor(s_sb[:, b, 0:n], ps_s[:, b, 0:n], bars[:, m - 2, :], ALU.add)
                    ins.then_inc(masked, 1)
                    dve.wait_ge(masked, u + 1)
                    link(nc.vector.reduce_max(small[:, b, 0:1], s_sb[:, b, 0:n], AX_X))
                    link(nc.vector.tensor_scalar(small[:, b, 0:1], small[:, b, 0:1], scale, sink_b[:, h:h + 1], ALU.mult, ALU.max))
                    nc.vector.tensor_scalar(small[:, b, 1:2], small[:, b, 0:1], -1.0, None, ALU.mult).then_inc(max_ready, 1)

                first(0)
                for u, (m, kv, j) in enumerate(units):
                    if u + 1 < len(units):
                        first(u + 1)
                    b = u % 2
                    h = kv * GROUP + j
                    dve.wait_ge(exped, u + 1)
                    link(nc.vector.tensor_tensor(small[:, b, 4:5], small[:, b, 2:3], small[:, b, 3:4], ALU.add))
                    link(nc.vector.reciprocal(small[:, b, 5:6], small[:, b, 4:5]))
                    dve.wait_ge(out_done, u + 1)
                    nc.vector.tensor_scalar(cat[:, m, M_W + h * DH_A:M_W + (h + 1) * DH_A], ps_o[:, b, 0:DH_A], small[:, b, 5:6], None,
                                            ALU.mult).then_inc(out_taken, 1)


def stage_head_norm(nc, name, h, tiles, heads, width, norm_w, gate, gate_func, out, eps):
    n = heads * width
    with stage(nc, name) as st:
        rows = st.sb("rows", [P, n])
        sq = st.sb("sq", [P, n])
        ss = st.sb("ss", [P, 4, heads])
        rs = st.sb("rs", [P, 4, heads])
        loaded, chain, ss_ready, rs_ready, gated = (st.sem(x) for x in ("loaded", "chain", "ss_ready", "rs_ready", "gated"))
        with nc.Block() as block:
            @block.sync
            def _(sp):
                sp.dma_start(rows[:, :], norm_w.partition_broadcast(P)).then_inc(loaded, 16)

            @block.scalar
            def _(act):
                for i, m in enumerate(tiles):
                    act.wait_ge(ss_ready, i + 1)
                    nc.scalar.activation(rs[:, i, :], ss[:, i, :], ACT.Sqrt).then_inc(rs_ready, 1)
                for i, m in enumerate(tiles):
                    if gate is not None:
                        nc.scalar.activation(gate[:, m, :], gate[:, m, :], gate_func).then_inc(gated, 1)

            @block.vector
            def _(dve):
                link = Link(dve, chain)
                for i, m in enumerate(tiles):
                    link(nc.vector.tensor_tensor(sq[:, :], h[:, m, 0:n], h[:, m, 0:n], ALU.mult))
                    link(nc.vector.reduce_sum(ss[:, i, :], sq[:, :].rearrange("p (h e) -> p h e", e=width), AX_X))
                    nc.vector.tensor_scalar(ss[:, i, :], ss[:, i, :], 1.0 / width, eps, ALU.mult, ALU.add).then_inc(ss_ready, 1)
                dve.wait_ge(loaded, 16)
                for i, m in enumerate(tiles):
                    dve.wait_ge(rs_ready, i + 1)
                    link(nc.vector.reciprocal(rs[:, i, :], rs[:, i, :]))
                    hv = h[:, m, 0:n].rearrange("p (h e) -> p h e", e=width)
                    ov = out[:, m, 0:n].rearrange("p (h e) -> p h e", e=width)
                    link(nc.vector.tensor_tensor(ov, hv, rs[:, i, :].unsqueeze(2).to_broadcast([P, heads, width]), ALU.mult))
                    if gate is None:
                        link(nc.vector.tensor_tensor(out[:, m, 0:n], out[:, m, 0:n], rows[:, :], ALU.mult))
                        continue
                    link(nc.vector.tensor_tensor(out[:, m, 0:n], out[:, m, 0:n], rows[:, :], ALU.mult))
                    dve.wait_ge(gated, i + 1)
                    link(nc.vector.tensor_tensor(out[:, m, 0:n], out[:, m, 0:n], gate[:, m, 0:n], ALU.mult))


HEADS, TOPK, KEYS = 8, 16, 128
HALVES = 2 * HEADS
PICKS = HEADS * TOPK


def stage_peer_select(nc, name, q_t, k_t, n_tiles, iota, layer, expert, weight):
    with stage(nc, name) as st:
        top = st.sb("top", [P, HALVES, TOPK])
        idx = st.sb("idx", [P, HALVES, TOPK], U32)
        idx_f = st.sb("idx_f", [P, HALVES, TOPK])
        left = st.sb("left", [P, HALVES, KEYS])
        cand = st.sb("cand", [P, HEADS, TOPK, TOPK])
        cand2 = st.sb("cand2", [P, HEADS, TOPK * TOPK])
        best = st.sb("best", [P, HEADS, TOPK])
        pos = st.sb("pos", [P, HEADS, TOPK], U32)
        ab = st.sb("ab", [P, 2, PICKS], U32)
        ab_f = st.sb("ab_f", [P, 2, PICKS])
        hot = st.sb("hot", [P, PICKS, TOPK])
        ids = st.sb("ids", [P, 2, PICKS])
        soft = st.sb("soft", [P, HEADS, TOPK])
        tot = st.sb("tot", [P, HEADS])
        ps = st.ps("s", [P, 2, HALVES, KEYS])
        scored, read, chain, soft_in, soft_out = (st.sem(x) for x in ("scored", "read", "chain", "soft_in", "soft_out"))

        with nc.Block() as block:
            @block.tensor
            def _(pe):
                for m in range(n_tiles):
                    if m >= 2:
                        pe.wait_ge(read, m - 1)
                    for i in range(HALVES):
                        last = nc.tensor.matmul(ps[:, m % 2, i, :], q_t[:, i, m * P:(m + 1) * P], k_t[:, i, :], start=True, stop=True)
                    last.then_inc(scored, 1)

            @block.scalar
            def _(act):
                for m in range(n_tiles):
                    act.wait_ge(soft_in, m + 1)
                    nc.scalar.activation(soft[:, :, :], soft[:, :, :], ACT.Exp).then_inc(soft_out, 1)

            @block.vector
            def _(dve):
                link = Link(dve, chain)

                def top16(groups, src, rest, out, where):
                    for i in range(groups):
                        last = nc.vector.max(out(i, 0), src(i))
                    link(last)
                    for i in range(groups):
                        nc.vector.max_index(where(i, 0), out(i, 0), src(i))
                        last = nc.vector.match_replace(rest(i), out(i, 0), src(i), -BIG)
                    link(last)
                    for i in range(groups):
                        last = nc.vector.max(out(i, 1), rest(i))
                    link(last)
                    for i in range(groups):
                        last = nc.vector.max_index(where(i, 1), out(i, 1), rest(i))
                    return last

                for m in range(n_tiles):
                    dve.wait_ge(scored, m + 1)
                    half = lambda t: (lambda i, j: t[:, i, 8 * j:8 * j + 8])
                    top16(HALVES, lambda i: ps[:, m % 2, i, :], lambda i: left[:, i, :], half(top), half(idx)).then_inc(read, 1)
                    dve.wait_ge(read, m + 1)
                    link(nc.vector.tensor_copy(idx_f[:, :, :], idx[:, :, :]))
                    tv = top[:, :, :].rearrange("p (h two) a -> p h two a", two=2)
                    shape = [P, HEADS, TOPK, TOPK]
                    for h in range(HEADS):
                        last = nc.vector.tensor_tensor(cand[:, h, :, :], tv[:, h, 0, :].unsqueeze(2).to_broadcast(shape[:1] + shape[2:]),
                                                       tv[:, h, 1, :].unsqueeze(1).to_broadcast(shape[:1] + shape[2:]), ALU.add)
                    link(last)
                    link(top16(HEADS, lambda i: cand[:, i, :, :].rearrange("p a b -> p (a b)"), lambda i: cand2[:, i, :],
                               half(best), half(pos)))
                    flat = pos[:, :, :].rearrange("p h e -> p (h e)")
                    nc.vector.tensor_scalar(ab[:, 0, :], flat, 4, None, ALU.logical_shift_right)
                    link(nc.vector.tensor_scalar(ab[:, 1, :], flat, TOPK - 1, None, ALU.bitwise_and))
                    link(nc.vector.tensor_copy(ab_f[:, :, :], ab[:, :, :]))
                    iv = idx_f[:, :, :].rearrange("p (h two) a -> p h two a", two=2)
                    for y in range(2):
                        link(nc.vector.tensor_tensor(hot[:, :, :], ab_f[:, y, :].unsqueeze(2).to_broadcast([P, PICKS, TOPK]),
                                                     iota[:, :].unsqueeze(1).to_broadcast([P, PICKS, TOPK]), ALU.is_equal))
                        hv = hot[:, :, :].rearrange("p (h e) a -> p h e a", h=HEADS)
                        for h in range(HEADS):
                            last = nc.vector.tensor_tensor(hv[:, h, :, :], hv[:, h, :, :],
                                                           iv[:, h, y, :].unsqueeze(1).to_broadcast([P, TOPK, TOPK]), ALU.mult)
                        link(last)
                        link(nc.vector.reduce_sum(ids[:, y, :], hot[:, :, :], AX_X))
                    link(nc.vector.tensor_scalar(ids[:, 0, :], ids[:, 0, :], float(KEYS), float(layer * N_EXPERTS), ALU.mult, ALU.add))
                    link(nc.vector.tensor_tensor(expert[:, m, :], ids[:, 0, :], ids[:, 1, :], ALU.add))
                    nc.vector.tensor_tensor(soft[:, :, :], best[:, :, :], best[:, :, 0:1].to_broadcast([P, HEADS, TOPK]),
                                            ALU.subtract).then_inc(soft_in, 1)
                    dve.wait_ge(soft_out, m + 1)
                    link(nc.vector.reduce_sum(tot[:, :], soft[:, :, :], AX_X))
                    link(nc.vector.reciprocal(tot[:, :], tot[:, :]))
                    link(nc.vector.tensor_tensor(weight[:, m, :].rearrange("p (h e) -> p h e", e=TOPK), soft[:, :, :],
                                                 tot[:, :].unsqueeze(2).to_broadcast([P, HEADS, TOPK]), ALU.mult))


def stage_peer_experts(nc, name, h, n_tiles, u, v, expert, weight, y, landed, landed0):
    with stage(nc, name) as st:
        ring = st.sb("ring", [P, TOPK, D])
        picks = st.sb("picks", [P, 2, TOPK], U32)
        junk = st.sb("junk", [P, 1])
        dots = st.sb("dots", [P, 2, TOPK])
        gel = st.sb("gel", [P, 2, TOPK])
        wgt = st.sb("wgt", [P, 2, TOPK])
        hp = st.ps("h", [P, D])
        acc = st.ps("acc", [P, 2, D])
        rows_used = st.sem("rows_used")
        picks_ready, h_ready, gelu_done, chain, passed = (
            st.sem(x) for x in ("picks_ready", "h_ready", "gelu_done", "chain", "passed"))
        USED0 = 2 * TOPK
        flat_expert = expert[:, :, :].rearrange("p m e -> p (m e)")
        flat_weight = weight[:, :, :].rearrange("p m e -> p (m e)")
        flat_h = h.rearrange("p m d -> p (m d)")
        flat_y = y.rearrange("p m d -> p (m d)")

        def heads(eng, before, one, after):
            with eng.Fori(0, n_tiles) as t:
                before(t)
                with eng.Fori(0, HEADS // 2) as g:
                    for half in range(2):
                        one(t * HEADS + g * 2 + half, half)
                after(t)

        none = lambda t: None
        with nc.Block() as block:
            @block.gpsimd
            def _(pool):
                def one(it, half):
                    for k in range(TOPK):
                        pool.wait_ge(rows_used, it * USED0 + (TOPK + k + 1))
                        pool.sem_inc(passed, 1)
                        if k == 0:
                            nc.gpsimd.tensor_copy(picks[:, half, :], flat_expert[:, ds(it * TOPK, TOPK)]).then_inc(picks_ready, 1)
                            pool.wait_ge(picks_ready, it + 1)
                            pool.sem_inc(passed, 1)
                        pool.indirect_dma_start(ring[:, k, :], None, u, bass.IndirectOffsetOnAxis(ap=picks[:, half, k:k + 1], axis=0)).then_inc(landed[k], 16)
                    for k in range(TOPK):
                        pool.wait_ge(rows_used, it * USED0 + (USED0 + k + 1))
                        pool.sem_inc(passed, 1)
                        pool.indirect_dma_start(ring[:, k, :], None, v, bass.IndirectOffsetOnAxis(ap=picks[:, half, k:k + 1], axis=0)).then_inc(landed[k], 16)
                heads(pool, none, one, none)

            @block.scalar
            def _(act):
                def before(t):
                    act.wait_ge(rows_used, t * (USED0 * HEADS) + USED0)
                    nc.scalar.activation(hp[:, :], flat_h[:, ds(t * D, D)], ACT.Copy).then_inc(h_ready, 1)

                def one(it, half):
                    act.wait_ge(rows_used, it * USED0 + (USED0 + TOPK))
                    nc.scalar.activation(gel[:, half, :], dots[:, half, :], ACT.Gelu).then_inc(gelu_done, 1)
                act.wait_ge(chain, 1)
                heads(act, before, one, none)

            @block.vector
            def _(dve):
                nc.vector.memset(junk[:, 0:1], 0.0).then_inc(chain, 1)
                dve.sem_inc(rows_used, USED0)
                per_tile = 2 + HEADS + 2

                def before(t):
                    dve.wait_ge(h_ready, t + 1)
                    nc.vector.memset(acc[:, 0, :], 0.0).then_inc(chain, 1)
                    nc.vector.memset(acc[:, 1, :], 0.0).then_inc(chain, 1)
                    dve.wait_ge(chain, t * per_tile + 3)
                    dve.sem_inc(passed, 1)

                def one(it, half):
                    for k in range(TOPK):
                        dve.wait_ge(landed[k], it * 32 + (landed0 + 16))
                        nc.vector.scalar_tensor_tensor(ring[:, k, :], ring[:, k, :], 1.0, hp[:, :], ALU.mult, ALU.mult,
                                                       accum_out=dots[:, half, k:k + 1]).then_inc(rows_used, 1)
                    dve.wait_ge(gelu_done, it + 1)
                    nc.vector.tensor_tensor(wgt[:, half, :], gel[:, half, :], flat_weight[:, ds(it * TOPK, TOPK)], ALU.mult).then_inc(chain, 1)
                    dve.wait_ge(chain, links(it))
                    for k in range(TOPK):
                        dve.wait_ge(landed[k], it * 32 + (landed0 + 32))
                        dve.wait_ge(rows_used, it * USED0 + (USED0 + TOPK + k - 1))
                        nc.vector.scalar_tensor_tensor(acc[:, k % 2, :], ring[:, k, :], wgt[:, half, k:k + 1], acc[:, k % 2, :],
                                                       ALU.mult, ALU.add).then_inc(rows_used, 1)

                def after(t):
                    dve.wait_ge(rows_used, t * (USED0 * HEADS) + USED0 * HEADS + USED0)
                    nc.vector.tensor_copy(flat_y[:, ds(t * D, D)], acc[:, 0, :]).then_inc(chain, 1)
                    dve.wait_ge(chain, t * per_tile + (3 + HEADS + 1))
                    nc.vector.tensor_tensor(flat_y[:, ds(t * D, D)], flat_y[:, ds(t * D, D)], acc[:, 1, :], ALU.add).then_inc(chain, 1)
                    dve.wait_ge(chain, t * per_tile + (3 + HEADS + 2))

                with dve.Fori(0, n_tiles) as t:
                    before(t)
                    with dve.Fori(0, HEADS // 2) as g:
                        for half in range(2):
                            links = lambda it: t * per_tile + g * 2 + (3 + half + 1)
                            one(t * HEADS + g * 2 + half, half)
                    after(t)


H_C, DV_C, RANK = 4, 256, 16
SUB = 32
NSUB = P // SUB
FAR_CAP = 80.0


def stage_gla(nc, low_w, gate_up, gate_b, act_t, q_t, k_t, v, sees, ident, h_out):
    order = [[0, 1, 2, 3], [1, 0, 3, 2]]
    with stage(nc, "gla") as st:
        wl = st.sb("w_low", [P, KC, 2 * RANK])
        up = st.sb("up", [RANK, 2, H_C * P])
        bias = st.sb("bias", [P, 2, H_C])
        low = st.sb("low", [RANK, 2, TOK])
        x = st.sb("x", [P, TOK])
        tmp = st.sb("tmp", [P, TOK])
        la = st.sb("la", [P, TOK])
        ones = st.sb("ones", [P, P])
        cum = st.sb("cum", [P, TT, P])
        kd = st.sb("kd", [P, TT, P])
        ecum = st.sb("ecum", [P, 2, P])
        etot = st.sb("etot", [P, TT])
        ks = st.sb("ks", [P, 2, NSUB, P])
        qs = st.sb("qs", [P, 2, NSUB, SUB])
        kd_tok = st.sb("kd_tok", [P, TT, P])
        sc = st.sb("sc", [P, 2, 2, P])
        state = st.sb("state", [P, 2, DV_C])
        ps_l = st.ps("logits", [P, BANK])
        ps_s = st.ps("scores", [P, 2, 256])
        ps_k = st.ps("kd_turn", [P, TT, P])
        ps_v = st.ps("kv", [P, 4, DV_C])
        ps_o = st.ps("out", [P, 2, DV_C])
        names = ("loaded low_done low_ready logit_done x_taken ln_ready cum_ready kd_arg q_arg sub_arg kd_exp q_exp sub_exp "
                 "kd_ready qk_ready kd_turned kd_copied scored sc_ready kv_done state_ready out_done out_taken chain achain").split()
        (loaded, low_done, low_ready, logit_done, x_taken, ln_ready, cum_ready, kd_arg, q_arg, sub_arg, kd_exp, q_exp, sub_exp,
         kd_ready, qk_ready, kd_turned, kd_copied, scored, sc_ready, kv_done, state_ready, out_done, out_taken, chain, achain) = (
            st.sem(n) for n in names)
        units = [(h, d) for h in range(H_C) for d in range(2)]
        with nc.Block() as block:
            @block.sync
            def _(sp):
                sp.dma_start(wl[:, :, :], low_w.rearrange("(k p) n -> p k n", p=P)).then_inc(loaded, 16)
                sp.dma_start(up[:, :, :], gate_up.rearrange("d r n -> r d n")).then_inc(loaded, 16)
                for d in range(2):
                    sp.dma_start(bias[:, d, :], gate_b[d].rearrange("(h p) -> p h", p=P), allow_slow_non_contiguous=True).then_inc(loaded, 16)

            @block.tensor
            def _(pe):
                pe.wait_ge(loaded, 64)
                for d in range(2):
                    if d:
                        pe.wait_ge(low_ready, 1)
                    for k in range(KC):
                        last = nc.tensor.matmul(ps_l[0:RANK, :], wl[:, k, d * RANK:(d + 1) * RANK], act_t[:, k, 0:TOK],
                                                start=(k == 0), stop=(k == KC - 1))
                    last.then_inc(low_done, 1)
                pe.wait_ge(low_ready, 2)
                for u, (h, d) in enumerate(units):
                    if u:
                        pe.wait_ge(x_taken, u)
                    nc.tensor.matmul(ps_l[:, :], up[:, d, h * P:(h + 1) * P], low[:, d, :], start=True, stop=True).then_inc(logit_done, 1)
                    pe.wait_ge(kd_ready, u + 1)
                    for c in range(TT):
                        last = nc.tensor.transpose(ps_k[:, c, :], kd[:, c, :], ident)
                    last.then_inc(kd_turned, 1)
                    pe.wait_ge(qk_ready, u + 1)
                    for c in range(2):
                        for j in range(NSUB):
                            last = nc.tensor.matmul(ps_s[:, c, j * SUB:(j + 1) * SUB], ks[:, c, j, :], qs[:, c, j, :], start=True, stop=True)
                    last.then_inc(scored, 1)
                    pe.wait_ge(kd_copied, u + 1)
                    if u:
                        pe.wait_ge(state_ready, u)
                    for i in range(3):
                        c = order[d][i]
                        last = nc.tensor.matmul(ps_v[:, i, :], kd_tok[:, c, :], v[:, c, h * DV_C:(h + 1) * DV_C], start=True, stop=True)
                    last.then_inc(kv_done, 1)
                    pe.wait_ge(sc_ready, u + 1)
                    pe.wait_ge(state_ready, u + 1)
                    if u:
                        pe.wait_ge(out_taken, u)
                    for i in range(2):
                        c = order[d][2 + i]
                        nc.tensor.matmul(ps_o[:, c - 2, :], ecum[:, c - 2, :], state[:, i, :], start=True, stop=False)
                        last = nc.tensor.matmul(ps_o[:, c - 2, :], sc[:, d, c - 2, :], v[:, c, h * DV_C:(h + 1) * DV_C], start=False, stop=True)
                    last.then_inc(out_done, 1)

            @block.scalar
            def _(act):
                link = Link(act, achain)
                for d in range(2):
                    act.wait_ge(low_done, d + 1)
                    nc.scalar.activation(low[:, d, :], ps_l[0:RANK, :], ACT.Copy).then_inc(low_ready, 1)
                for u, (h, d) in enumerate(units):
                    act.wait_ge(logit_done, u + 1)
                    if u:
                        act.wait_ge(cum_ready, u)
                    nc.scalar.activation(x[:, :], ps_l[:, :], ACT.Identity, bias=bias[:, d, h:h + 1]).then_inc(x_taken, 1)
                    act.wait_ge(x_taken, u + 1)
                    link(nc.scalar.activation(tmp[:, :], x[:, :], ACT.Abs))
                    link(nc.scalar.activation(tmp[:, :], tmp[:, :], ACT.Exp, scale=-1.0))
                    nc.scalar.activation(tmp[:, :], tmp[:, :], ACT.Ln, bias=1.0).then_inc(ln_ready, 1)
                    act.wait_ge(kd_arg, u + 1)
                    end = P - 1 if d == 0 else 0
                    nc.scalar.activation(kd[:, :, :], kd[:, :, :], ACT.Exp)
                    nc.scalar.activation(etot[:, :], cum[:, :, end], ACT.Exp).then_inc(kd_exp, 1)
                    act.wait_ge(sub_arg, u + 1)
                    nc.scalar.activation(ks[:, :, :, :], ks[:, :, :, :], ACT.Exp)
                    nc.scalar.activation(qs[:, :, :, :], qs[:, :, :, :], ACT.Exp)
                    nc.scalar.activation(ecum[:, :, :], cum[:, 2:4, :], ACT.Exp).then_inc(sub_exp, 1)
                    act.wait_ge(kd_turned, u + 1)
                    nc.scalar.activation(kd_tok[:, :, :], ps_k[:, :, :], ACT.Copy).then_inc(kd_copied, 1)

            @block.vector
            def _(dve):
                link = Link(dve, chain)
                link(nc.vector.memset(ones[:, :], 1.0))
                link(nc.vector.memset(sc[:, :, :, :].rearrange("p a b c -> p (a b c)"), 0.0))
                for u, (h, d) in enumerate(units):
                    end = P - 1 if d == 0 else 0
                    dve.wait_ge(ln_ready, u + 1)
                    link(nc.vector.scalar_tensor_tensor(la[:, :], x[:, :], 0.0, tmp[:, :], ALU.min, ALU.subtract))
                    link(nc.vector.tensor_scalar(la[:, :], la[:, :], 1.0 / 16.0, None, ALU.mult))
                    if u:
                        dve.wait_ge(out_done, u)
                    for c in range(TT):
                        a, o = la[:, c * P:(c + 1) * P], cum[:, c, :]
                        if d:
                            a, o = a[:, ::-1], o[:, ::-1]
                        last = nc.vector.tensor_tensor_scan(o, ones[:, :], a, 0.0, ALU.mult, ALU.add)
                    last.then_inc(cum_ready, 1)
                    dve.wait_ge(cum_ready, u + 1)
                    nc.vector.tensor_tensor(kd[:, :, :], cum[:, :, end:end + 1].to_broadcast([P, TT, P]), cum[:, :, :],
                                            ALU.subtract).then_inc(kd_arg, 1)
                    for c in range(2):
                        cu = cum[:, 2 + c, :]
                        ref = cu.rearrange("p (j s) -> p j s", s=SUB)[:, :, SUB // 2:SUB // 2 + 1]
                        nc.vector.tensor_tensor(ks[:, c, :, :], ref.to_broadcast([P, NSUB, P]), cu.unsqueeze(1).to_broadcast([P, NSUB, P]), ALU.subtract)
                        last = nc.vector.tensor_tensor(qs[:, c, :, :], cu.rearrange("p (j s) -> p j s", s=SUB), ref.to_broadcast([P, NSUB, SUB]), ALU.subtract)
                    link(last)
                    nc.vector.tensor_scalar(ks[:, :, :, :], ks[:, :, :, :], FAR_CAP, None, ALU.min)
                    nc.vector.tensor_scalar(qs[:, :, :, :], qs[:, :, :, :], FAR_CAP, None, ALU.min).then_inc(sub_arg, 1)
                    dve.wait_ge(kd_exp, u + 1)
                    nc.vector.tensor_tensor(kd[:, :, :], kd[:, :, :], k_t[:, h, :].rearrange("p (c s) -> p c s", s=P), ALU.mult).then_inc(kd_ready, 1)
                    dve.wait_ge(sub_exp, u + 1)
                    for c in range(2):
                        kk = k_t[:, h, (2 + c) * P:(3 + c) * P]
                        qq = q_t[:, h, c * P:(c + 1) * P]
                        nc.vector.tensor_tensor(ks[:, c, :, :], ks[:, c, :, :], kk.unsqueeze(1).to_broadcast([P, NSUB, P]), ALU.mult)
                        nc.vector.scalar_tensor_tensor(qs[:, c, :, :].rearrange("p j s -> p (j s)"), qs[:, c, :, :].rearrange("p j s -> p (j s)"),
                                                       float(P) ** -0.5, qq, ALU.mult, ALU.mult)
                        last = nc.vector.scalar_tensor_tensor(ecum[:, c, :], ecum[:, c, :], float(P) ** -0.5, qq, ALU.mult, ALU.mult)
                    last.then_inc(qk_ready, 1)
                    dve.wait_ge(scored, u + 1)
                    for c in range(2):
                        last = nc.vector.copy_predicated(sc[:, d, c, :], sees[:, d, :].bitcast(U32), ps_s[:, c, 0:P])
                    last.then_inc(sc_ready, 1)
                    dve.wait_ge(kv_done, u + 1)
                    link(nc.vector.tensor_copy(state[:, 0, :], ps_v[:, 0, :]))
                    link(nc.vector.scalar_tensor_tensor(state[:, 0, :], state[:, 0, :], etot[:, order[d][1]:order[d][1] + 1], ps_v[:, 1, :], ALU.mult, ALU.add))
                    nc.vector.scalar_tensor_tensor(state[:, 1, :], state[:, 0, :], etot[:, order[d][2]:order[d][2] + 1], ps_v[:, 2, :],
                                                   ALU.mult, ALU.add).then_inc(state_ready, 1)
                    dve.wait_ge(out_done, u + 1)
                    for c in range(2):
                        o = h_out[:, c, h * DV_C:(h + 1) * DV_C]
                        if d == 0:
                            last = nc.vector.tensor_copy(o, ps_o[:, c, :])
                        else:
                            last = nc.vector.tensor_tensor(o, ps_o[:, c, :], o, ALU.add)
                    last.then_inc(out_taken, 1)
                    dve.wait_ge(out_taken, u + 1)


LT = SEQ // P
GROUPS = 8
S_HEADS, S_DIM, S_GROUPS = 16, 64, 4


def stage_layer_norm(nc, name, x, off, w, b, eps):
    with stage(nc, name) as st:
        rows = st.sb("rows", [P, 2, D])
        stats = st.sb("stats", [P, 2, 6])
        agg = st.sb("agg", [P, LT, 2])
        std = st.sb("std", [P, LT])
        loaded, chain, var_ready, std_ready = (st.sem(n) for n in ("loaded", "chain", "var_ready", "std_ready"))
        with nc.Block() as block:
            @block.sync
            def _(sp):
                sp.dma_start(rows[:, 0, :], w.partition_broadcast(P)).then_inc(loaded, 16)
                sp.dma_start(rows[:, 1, :], b.partition_broadcast(P)).then_inc(loaded, 16)

            @block.vector
            def _(dve):
                link = Link(dve, chain)
                for i in range(LT):
                    for j in range(2):
                        link(nc.vector.bn_stats(stats[:, j, :], x[:, i, off + j * BANK:off + (j + 1) * BANK]))
                    link(nc.vector.bn_aggr(agg[:, i, :], stats[:, :, :].rearrange("p a b -> p (a b)")))
                    nc.vector.tensor_scalar(agg[:, i, 1:2], agg[:, i, 1:2], eps, None, ALU.add).then_inc(var_ready, 1)
                dve.wait_ge(loaded, 32)
                for i in range(LT):
                    t = x[:, i, off:off + D]
                    dve.wait_ge(std_ready, i + 1)
                    link(nc.vector.reciprocal(std[:, i:i + 1], std[:, i:i + 1]))
                    link(nc.vector.tensor_scalar(t, t, agg[:, i, 0:1], std[:, i:i + 1], ALU.subtract, ALU.mult))
                    link(nc.vector.tensor_tensor(t, t, rows[:, 0, :], ALU.mult))
                    link(nc.vector.tensor_tensor(t, t, rows[:, 1, :], ALU.add))

            @block.scalar
            def _(act):
                for i in range(LT):
                    act.wait_ge(var_ready, i + 1)
                    nc.scalar.activation(std[:, i:i + 1], agg[:, i, 1:2], ACT.Sqrt).then_inc(std_ready, 1)


def stage_spatial(nc, uv, w_s, b_s, ident, keep, out):
    with stage(nc, "spatial") as st:
        w = st.sb("w", [P, 1, GROUPS * P])
        wt = st.sb("wt", [P, GROUPS, P])
        b = st.sb("b", [P, GROUPS])
        loaded, turned, masked, mixed, read, chain = (st.sem(n) for n in ("loaded", "turned", "masked", "mixed", "read", "chain"))
        ps_w = st.ps("w_turn", [P, GROUPS, P])
        ps = st.ps("mixed", [P, LT, GROUPS, P])
        with nc.Block() as block:
            @block.sync
            def _(sp):
                sp.dma_start(w[:, 0, :].rearrange("t (g s) -> t g s", s=P), w_s.rearrange("g t s -> t g s")).then_inc(loaded, 16)
                sp.dma_start(b[:, :], b_s.rearrange("g t -> t g"), allow_slow_non_contiguous=True).then_inc(loaded, 16)

            @block.tensor
            def _(pe):
                pe.wait_ge(loaded, 32)
                for g in range(GROUPS):
                    last = nc.tensor.transpose(ps_w[:, g, :], w[:, 0, g * P:(g + 1) * P], ident)
                last.then_inc(turned, 1)
                pe.wait_ge(masked, 1)
                for c in range(LT):
                    for g in range(GROUPS):
                        last = nc.tensor.matmul(ps[:, c, g, :], wt[:, g, :], uv[:, c, D + g * P:D + (g + 1) * P], start=True, stop=True)
                    last.then_inc(mixed, 1)

            @block.vector
            def _(dve):
                link = Link(dve, chain)
                dve.wait_ge(turned, 1)
                nc.vector.tensor_tensor(wt[:, :, :], ps_w[:, :, :], keep[:, :].unsqueeze(1).to_broadcast([P, GROUPS, P]), ALU.mult).then_inc(masked, 1)
                for c in range(LT):
                    dve.wait_ge(mixed, c + 1)
                    o = out[:, c, :].rearrange("p (g e) -> p g e", e=P)
                    link(nc.vector.tensor_tensor(o, ps[:, c, :, :], b[:, :].unsqueeze(2).to_broadcast([P, GROUPS, P]), ALU.add))
                    link(nc.vector.tensor_tensor(out[:, c, :], out[:, c, :], uv[:, c, 0:D], ALU.mult))


def stage_conv(nc, name, x, tiles, w, b, out, silu):
    taps = 4
    with stage(nc, name) as st:
        wc = st.sb("w", [P, taps, tiles])
        bc = st.sb("b", [P, tiles])
        loaded, chain, summed = (st.sem(n) for n in ("loaded", "chain", "summed"))
        with nc.Block() as block:
            @block.sync
            def _(sp):
                for k in range(taps):
                    sp.dma_start(wc[:, k, :], w[k].rearrange("(c p) -> p c", p=P), allow_slow_non_contiguous=True).then_inc(loaded, 16)
                sp.dma_start(bc[:, :], b.rearrange("(c p) -> p c", p=P), allow_slow_non_contiguous=True).then_inc(loaded, 16)

            @block.vector
            def _(dve):
                dve.wait_ge(loaded, 16 * (taps + 1))
                for c in range(tiles):
                    last = nc.vector.tensor_scalar(out[:, c, :], x[:, c, :], wc[:, taps - 1, c:c + 1], bc[:, c:c + 1], ALU.mult, ALU.add)
                last.then_inc(chain, 1)
                for back in range(1, taps):
                    dve.wait_ge(chain, back)
                    for c in range(tiles):
                        o = out[:, c, back:SEQ]
                        last = nc.vector.scalar_tensor_tensor(o, x[:, c, 0:SEQ - back], wc[:, taps - 1 - back, c:c + 1], o, ALU.mult, ALU.add)
                    last.then_inc(chain, 1)
                dve.wait_ge(chain, taps)
                dve.sem_inc(summed, 1)

            @block.scalar
            def _(act):
                if silu:
                    act.wait_ge(summed, 1)
                    nc.scalar.activation(out[:, :, :], out[:, :, :], ACT.Silu)


def stage_lru(nc, x, gate, w_r, b_r, w_i, b_i, lam):
    with stage(nc, "lru") as st:
        wr = st.sb("wr", [P, GROUPS, P])
        wi = st.sb("wi", [P, GROUPS, P])
        cols = st.sb("cols", [P, 6, GROUPS])
        r = st.sb("r", [P, GROUPS, SEQ])
        i_t = st.sb("i", [P, GROUPS, SEQ])
        th = st.sb("th", [P, GROUPS, SEQ])
        den = st.sb("den", [P, GROUPS, SEQ])
        ps = st.ps("ps", [P, 2, 2, SEQ])
        names = "loaded gated emptied ln_ready r_ready loga_ready tanh_ready a_ready root_in root_out chain achain".split()
        loaded, gated, emptied, ln_ready, r_ready, loga_ready, tanh_ready, a_ready, root_in, root_out, chain, achain = (st.sem(n) for n in names)
        with nc.Block() as block:
            @block.sync
            def _(sp):
                sp.dma_start(wr[:, :, :], w_r.rearrange("h i j -> i h j")).then_inc(loaded, 16)
                sp.dma_start(wi[:, :, :], w_i.rearrange("h i j -> i h j")).then_inc(loaded, 16)
                for n, src in enumerate((b_r, b_i, lam)):
                    sp.dma_start(cols[:, n, :], src.rearrange("(c p) -> p c", p=P), allow_slow_non_contiguous=True).then_inc(loaded, 16)

            @block.tensor
            def _(pe):
                pe.wait_ge(loaded, 80)
                for h in range(GROUPS):
                    if h >= 2:
                        pe.wait_ge(emptied, h - 1)
                    nc.tensor.matmul(ps[:, h % 2, 0, :], wr[:, h, :], x[:, h, :], start=True, stop=True)
                    nc.tensor.matmul(ps[:, h % 2, 1, :], wi[:, h, :], x[:, h, :], start=True, stop=True).then_inc(gated, 1)

            @block.scalar
            def _(act):
                link = Link(act, achain)
                act.wait_ge(loaded, 80)
                link(nc.scalar.activation(cols[:, 3, :], cols[:, 2, :], ACT.Abs))
                link(nc.scalar.activation(cols[:, 3, :], cols[:, 3, :], ACT.Exp, scale=-1.0))
                nc.scalar.activation(cols[:, 3, :], cols[:, 3, :], ACT.Ln, bias=1.0).then_inc(ln_ready, 1)
                for h in range(GROUPS):
                    act.wait_ge(gated, h + 1)
                    nc.scalar.activation(r[:, h, :], ps[:, h % 2, 0, :], ACT.Sigmoid, bias=cols[:, 0, h:h + 1])
                    nc.scalar.activation(i_t[:, h, :], ps[:, h % 2, 1, :], ACT.Sigmoid, bias=cols[:, 1, h:h + 1]).then_inc(emptied, 1)
                act.wait_ge(loga_ready, 1)
                nc.scalar.activation(th[:, :, :], r[:, :, :], ACT.Tanh).then_inc(tanh_ready, 1)
                act.wait_ge(tanh_ready, 1)
                nc.scalar.activation(r[:, :, :], r[:, :, :], ACT.Exp).then_inc(a_ready, 1)
                act.wait_ge(root_in, 1)
                nc.scalar.activation(th[:, :, :], th[:, :, :], ACT.Sqrt).then_inc(root_out, 1)

            @block.vector
            def _(dve):
                link = Link(dve, chain)
                dve.wait_ge(ln_ready, 1)
                link(nc.vector.scalar_tensor_tensor(cols[:, 4, :], cols[:, 2, :], 0.0, cols[:, 3, :], ALU.min, ALU.subtract))
                link(nc.vector.tensor_scalar(cols[:, 4, :], cols[:, 4, :], 8.0, None, ALU.mult))
                dve.wait_ge(emptied, GROUPS)
                for h in range(GROUPS):
                    last = nc.vector.tensor_scalar(r[:, h, :], r[:, h, :], cols[:, 4, h:h + 1], None, ALU.mult)
                last.then_inc(loga_ready, 1)
                link(nc.vector.tensor_tensor(i_t[:, :, :], i_t[:, :, :], x[:, :, :], ALU.mult))
                dve.wait_ge(tanh_ready, 1)
                link(nc.vector.tensor_scalar(den[:, :, :], th[:, :, :], -1.0, 1.0, ALU.mult, ALU.add))
                link(nc.vector.reciprocal(den[:, :, :], den[:, :, :]))
                nc.vector.scalar_tensor_tensor(th[:, :, :], th[:, :, :], -2.0, den[:, :, :], ALU.mult, ALU.mult).then_inc(root_in, 1)
                dve.wait_ge(root_out, 1)
                link(nc.vector.tensor_tensor(i_t[:, :, :], i_t[:, :, :], th[:, :, :], ALU.mult))
                dve.wait_ge(a_ready, 1)
                for h in range(GROUPS):
                    last = nc.vector.tensor_tensor_scan(den[:, h, :], r[:, h, :], i_t[:, h, :], 0.0, ALU.mult, ALU.add)
                link(last)
                link(nc.vector.tensor_tensor(gate[:, :, :], gate[:, :, :], den[:, :, :], ALU.mult))


def stage_ssd(nc, act_t, w_dt, dt_bias, a_log, d_skip, xbc, x_tok, z, ident, sel, far, y):
    with stage(nc, "ssd") as st:
        wd = st.sb("wd", [P, KC, S_HEADS])
        par = st.sb("par", [S_HEADS, 4])
        dsk = st.sb("dsk", [P, S_HEADS])
        row = st.sb("row", [S_HEADS, 6, SEQ])
        col = st.sb("col", [P, LT, 2, S_HEADS])
        xdt = st.sb("xdt", [P, LT, D])
        m_far = st.sb("m_far", [P, 2, SEQ])
        e = st.sb("e", [P, 2, LT, SEQ])
        w = st.sb("w", [P, 2, LT, SEQ])
        ps_d = st.ps("dt", [P, BANK])
        ps_c = st.ps("cb", [P, LT, SEQ])
        ps_m = st.ps("cum_bcast", [P, 2, BANK])
        ps_y = st.ps("y", [P, LT, D])
        names = ("loaded dt_done dt_sum ln_ready ea_ready cum_ready cols_done xdt_ready crossed sent far_ready e_ready w_ready mult_done chain achain").split()
        (loaded, dt_done, dt_sum, ln_ready, ea_ready, cum_ready, cols_done, xdt_ready, crossed, sent, far_ready, e_ready, w_ready,
         mult_done, chain, achain) = (st.sem(n) for n in names)
        with nc.Block() as block:
            @block.sync
            def _(sp):
                sp.dma_start(wd[:, :, :], w_dt.rearrange("(k p) n -> p k n", p=P)).then_inc(loaded, 16)
                sp.dma_start(par[:, 0:1], dt_bias.rearrange("(h o) -> h o", o=1)).then_inc(loaded, 16)
                sp.dma_start(par[:, 1:2], a_log.rearrange("(h o) -> h o", o=1)).then_inc(loaded, 16)
                sp.dma_start(dsk[:, :], d_skip.partition_broadcast(P)).then_inc(loaded, 16)

            @block.tensor
            def _(pe):
                pe.wait_ge(loaded, 64)
                for k in range(KC):
                    last = nc.tensor.matmul(ps_d[0:S_HEADS, 0:SEQ], wd[:, k, :], act_t[:, k, 0:SEQ], start=(k == 0), stop=(k == KC - 1))
                last.then_inc(dt_done, 1)
                pe.wait_ge(cum_ready, 1)
                for c in range(LT):
                    for n, r in enumerate((2, 4)):
                        at = 256 + (2 * c + n) * S_HEADS
                        last = nc.tensor.matmul(ps_d[:, at:at + S_HEADS], row[:, r, c * P:(c + 1) * P], ident[0:S_HEADS, 0:S_HEADS], start=True, stop=True)
                last.then_inc(cols_done, 1)
                pe.wait_ge(xdt_ready, 1)
                for h in range(S_HEADS):
                    g = h // (S_HEADS // S_GROUPS)
                    if h % (S_HEADS // S_GROUPS) == 0:
                        if h:
                            pe.wait_ge(w_ready, h)
                        for s in range(LT):
                            last = nc.tensor.matmul(ps_c[:, s, :], xbc[:, 8 + g, s * P:(s + 1) * P], xbc[:, 12 + g, :], start=True, stop=True)
                        last.then_inc(crossed, 1)
                    if h >= 2:
                        pe.wait_ge(e_ready, h - 1)
                    nc.tensor.matmul(ps_m[:, h % 2, 0:SEQ], sel[0:S_HEADS, h, :], row[:, 4, :], start=True, stop=True).then_inc(sent, 1)
                    pe.wait_ge(w_ready, h + 1)
                    for t in range(LT):
                        for s in range(t + 1):
                            last = nc.tensor.matmul(ps_y[:, t, h * S_DIM:(h + 1) * S_DIM], w[:, h % 2, s, t * P:(t + 1) * P],
                                                    xdt[:, s, h * S_DIM:(h + 1) * S_DIM], start=(s == 0), stop=(s == t))
                    last.then_inc(mult_done, 1)

            @block.scalar
            def _(act):
                link = Link(act, achain)
                act.wait_ge(loaded, 64)
                act.wait_ge(dt_done, 1)
                nc.scalar.activation(par[:, 2:3], par[:, 1:2], ACT.Exp).then_inc(ea_ready, 1)
                nc.scalar.activation(row[:, 0, :], ps_d[0:S_HEADS, 0:SEQ], ACT.Identity, bias=par[:, 0:1]).then_inc(dt_sum, 1)
                act.wait_ge(dt_sum, 1)
                link(nc.scalar.activation(row[:, 1, :], row[:, 0, :], ACT.Abs))
                link(nc.scalar.activation(row[:, 1, :], row[:, 1, :], ACT.Exp, scale=-1.0))
                nc.scalar.activation(row[:, 1, :], row[:, 1, :], ACT.Ln, bias=1.0).then_inc(ln_ready, 1)
                act.wait_ge(xdt_ready, 1)
                for h in range(S_HEADS):
                    act.wait_ge(sent, h + 1)
                    act.wait_ge(far_ready, h + 1)
                    if h >= 2:
                        act.wait_ge(w_ready, h - 1)
                    b = h % 2
                    for s in range(LT):
                        last = nc.scalar.activation(e[:, b, s, s * P:(s + 1) * P], m_far[:, b, s * P:(s + 1) * P], ACT.Exp, bias=col[:, s, 1, h:h + 1])
                    last = nc.scalar.activation(e[:, b, 0, P:SEQ], ps_m[:, b, P:SEQ], ACT.Exp, bias=col[:, 0, 1, h:h + 1])
                    last.then_inc(e_ready, 1)

            @block.vector
            def _(dve):
                link = Link(dve, chain)
                link(nc.vector.memset(row[:, 5, :], 1.0))
                dve.wait_ge(ln_ready, 1)
                link(nc.vector.scalar_tensor_tensor(row[:, 2, :], row[:, 0, :], 0.0, row[:, 1, :], ALU.max, ALU.add))
                dve.wait_ge(ea_ready, 1)
                link(nc.vector.tensor_scalar(row[:, 3, :], row[:, 2, :], par[:, 2:3], -1.0, ALU.mult, ALU.mult))
                nc.vector.tensor_tensor_scan(row[:, 4, :], row[:, 5, :], row[:, 3, :], 0.0, ALU.mult, ALU.add).then_inc(cum_ready, 1)
                dve.wait_ge(cols_done, 1)
                pc = ps_d[:, 256:256 + 4 * S_HEADS].rearrange("p (c n h) -> p c n h", n=2, h=S_HEADS)
                nc.vector.tensor_copy(col[:, :, 0, :], pc[:, :, 0, :])
                link(nc.vector.tensor_scalar(col[:, :, 1, :], pc[:, :, 1, :], -1.0, None, ALU.mult))
                for c in range(LT):
                    xv = x_tok[:, c, :].rearrange("p (h e) -> p h e", e=S_DIM)
                    last = nc.vector.tensor_tensor(xdt[:, c, :].rearrange("p (h e) -> p h e", e=S_DIM), xv,
                                                   col[:, c, 0, :].unsqueeze(2).to_broadcast([P, S_HEADS, S_DIM]), ALU.mult)
                last.then_inc(xdt_ready, 1)
                for h in range(S_HEADS):
                    b = h % 2
                    dve.wait_ge(sent, h + 1)
                    if h >= 2:
                        dve.wait_ge(e_ready, h - 1)
                    nc.vector.tensor_tensor(m_far[:, b, :], ps_m[:, b, 0:SEQ], far[:, 0, 0:SEQ], ALU.subtract).then_inc(far_ready, 1)
                    dve.wait_ge(e_ready, h + 1)
                    dve.wait_ge(crossed, h // (S_HEADS // S_GROUPS) + 1)
                    if h >= 2:
                        dve.wait_ge(mult_done, h - 1)
                    nc.vector.tensor_tensor(w[:, b, 0, :], ps_c[:, 0, :], e[:, b, 0, :], ALU.mult)
                    nc.vector.tensor_tensor(w[:, b, 1, P:SEQ], ps_c[:, 1, P:SEQ], e[:, b, 1, P:SEQ], ALU.mult).then_inc(w_ready, 1)
                dve.wait_ge(mult_done, S_HEADS)
                for c in range(LT):
                    yv = y[:, c, :].rearrange("p (h e) -> p h e", e=S_DIM)
                    xv = x_tok[:, c, :].rearrange("p (h e) -> p h e", e=S_DIM)
                    link(nc.vector.tensor_tensor(yv, xv, dsk[:, :].unsqueeze(2).to_broadcast([P, S_HEADS, S_DIM]), ALU.mult))
                    link(nc.vector.tensor_tensor(y[:, c, :], ps_y[:, c, :], y[:, c, :], ALU.add))
                    link(nc.vector.tensor_tensor(y[:, c, :], y[:, c, :], z[:, c, :], ALU.mult))


def stage_merge_branches(nc, g, b_gate, branches, out):
    with stage(nc, "merge") as st:
        rows = st.sb("rows", [P, 3, D])
        loaded, biased, gated, chain = (st.sem(n) for n in ("loaded", "biased", "gated", "chain"))
        with nc.Block() as block:
            @block.sync
            def _(sp):
                for i in range(3):
                    sp.dma_start(rows[:, i, :], b_gate[i].partition_broadcast(P)).then_inc(loaded, 16)

            @block.scalar
            def _(act):
                for n in range(3 * LT):
                    c, i = divmod(n, 3)
                    act.wait_ge(biased, n + 1)
                    part = g[:, c, i * D:(i + 1) * D]
                    nc.scalar.activation(part, part, ACT.Sigmoid).then_inc(gated, 1)

            @block.vector
            def _(dve):
                link = Link(dve, chain)
                dve.wait_ge(loaded, 48)
                for n in range(3 * LT):
                    c, i = divmod(n, 3)
                    part = g[:, c, i * D:(i + 1) * D]
                    nc.vector.tensor_tensor(part, part, rows[:, i, :], ALU.add).then_inc(biased, 1)
                for n in range(3 * LT):
                    c, i = divmod(n, 3)
                    part = g[:, c, i * D:(i + 1) * D]
                    dve.wait_ge(gated, n + 1)
                    if i == 0:
                        link(nc.vector.tensor_tensor(out[:, c, :], part, branches[i][:, c, :], ALU.mult))
                    else:
                        link(nc.vector.tensor_tensor(part, part, branches[i][:, c, :], ALU.mult))
                        link(nc.vector.tensor_tensor(out[:, c, :], out[:, c, :], part, ALU.add))


def stage_ops(nc, name, make):
    with stage(nc, name) as st:
        chain = st.sem("chain")
        with nc.Block() as block:
            @block.vector
            def _(dve):
                make(Link(dve, chain))


def token_tiles(n):
    return [(i * P, P) for i in range(n)]


def buffers(nc, ctx):
    return lambda name, shape, dt=F32: ctx.enter_context(nc.sbuf_tensor(name, shape, dt))


def peer(nc, name, layer, n_tiles, consts, a, h, h_t, y, landed, landed0):
    with ExitStack() as ctx:
        sb = buffers(nc, ctx)
        expert = sb(f"{name}_expert", [P, n_tiles, PICKS], U32)
        weight = sb(f"{name}_weight", [P, n_tiles, PICKS])
        with ExitStack() as ctx2:
            sb = buffers(nc, ctx2)
            keys = sb(f"{name}_keys", [P, 1, HALVES * P])
            keys_t = sb(f"{name}_keys_t", [P, HALVES, P])
            q_t = sb(f"{name}_q_t", [P, HALVES, n_tiles * P])
            stage_load(nc, f"{name}_load", [(keys[:, 0, :].rearrange("n (i k) -> n i k", k=P),
                                             a["peer_keys"][layer].rearrange("h two n k -> n (h two) k"))])
            stage_transpose(nc, f"{name}_kt", consts["ident"][:, :], keys, keys_t, [0], HALVES)
            stage_linear(nc, f"{name}_q", h_t, token_tiles(n_tiles), a["peer_wq"][layer], HALVES * P, q_t, feature=True)
            stage_peer_select(nc, f"{name}_select", q_t, keys_t, n_tiles, consts["iota"], layer, expert, weight)
        stage_peer_experts(nc, f"{name}_experts", h, n_tiles, a["peer_u"].rearrange("l e d -> (l e) d"),
                           a["peer_v"].rearrange("l e d -> (l e) d"), expert, weight, y, landed, landed0)


def mixer_ab(nc, consts, a, h_t, y):
    w = a["ab_w_in"][0]
    tiles = token_tiles(TT)
    with ExitStack() as ctx:
        sb = buffers(nc, ctx)
        cat = sb("ab_cat", [P, TT, D])
        o = sb("ab_o", [P, TT, M_W])
        hm = sb("ab_hm", [P, TT, M_W])
        with ExitStack() as ctx2:
            sb = buffers(nc, ctx2)
            qk_t = sb("ab_qk_t", [P, 2 * H_M, TOK])
            v_aug = sb("ab_v_aug", [P, TT, H_M, P + 2])
            g_cols = sb("ab_g_cols", [P, 2, TT, 2, H_M])
            m_rows = sb("ab_m_rows", [H_M, 2, TOK])
            qkv = sb("ab_qkv", [P, TT, A_Q + 2 * A_KV])
            with ExitStack() as ctx3:
                v = buffers(nc, ctx3)("ab_v", [P, TT, M_W])
                stage_linear(nc, "ab_v_lin", h_t, tiles, w[:, 2 * M_W:3 * M_W], M_W, v)
                stage_value_ones(nc, "ab_ones", v, v_aug)
            stage_linear(nc, "ab_qk", h_t, tiles, w[:, 0:2 * M_W], 2 * M_W, qk_t, feature=True)
            stage_linear(nc, "ab_o_lin", h_t, tiles, w[:, 3 * M_W:4 * M_W], M_W, o)
            stage_gates(nc, h_t, w[:, 4 * M_W:4 * M_W + 16], a["ab_gate_b"][0], consts["ident"], consts["sel"], g_cols, m_rows)
            stage_linear(nc, "ab_qkv_lin", h_t, tiles, w[:, 4 * M_W + 16:4 * M_W + 16 + A_Q + 2 * A_KV], A_Q + 2 * A_KV, qkv)
            stage_mlstm(nc, qk_t, v_aug, g_cols, m_rows, consts["sel"], consts["far"], hm)
            stage_attention(nc, qkv, consts["cos"], consts["sin"], consts["bars"], a["ab_sink"][0], consts["ident"][:, :], cat)
        stage_head_norm(nc, "ab_norm", hm, range(TT), H_M, P, a["ab_norm_w"][0], o, ACT.Sigmoid, cat, LN_EPS)
        cat_t = buffers(nc, ctx)("ab_cat_t", [P, KC, TOK])
        stage_transpose(nc, "ab_turn", consts["ident"][:, :], cat, cat_t, range(TT), KC)
        stage_linear(nc, "ab_out", cat_t, tiles, a["ab_w_out"][0], D, y)


def mixer_c(nc, consts, a, h_t, y):
    w = a["gla_w_in"][0]
    ck, cv = H_C * P, H_C * DV_C
    lat = [(CTX + i * P, P) for i in range(LT)]
    with ExitStack() as ctx:
        sb = buffers(nc, ctx)
        g = sb("c_g", [P, LT, cv])
        hc = sb("c_h", [P, LT, cv])
        lat_t = sb("c_lat_t", [P, KC, SEQ])
        stage_ops(nc, "c_lat", lambda link: link(nc.vector.tensor_copy(lat_t[:, :, :], h_t[:, :, CTX:TOK])))
        with ExitStack() as ctx2:
            sb = buffers(nc, ctx2)
            q_t = sb("c_q_t", [P, H_C, SEQ])
            k_t = sb("c_k_t", [P, H_C, TOK])
            v = sb("c_v", [P, TT, cv])
            stage_linear(nc, "c_q", lat_t, token_tiles(LT), w[:, 0:ck], ck, q_t, feature=True)
            stage_linear(nc, "c_k", h_t, token_tiles(TT), w[:, ck:2 * ck], ck, k_t, feature=True)
            stage_linear(nc, "c_v_lin", h_t, token_tiles(TT), w[:, 2 * ck:2 * ck + cv], cv, v)
            stage_linear(nc, "c_g_lin", lat_t, token_tiles(LT), w[:, 2 * ck + cv:2 * ck + 2 * cv], cv, g)
            stage_gla(nc, w[:, 2 * ck + 2 * cv:2 * ck + 2 * cv + 2 * RANK], a["gla_gate_up"][0], a["gla_gate_b"][0], h_t, q_t, k_t, v,
                      consts["sees"], consts["ident"][:, :], hc)
        stage_head_norm(nc, "c_norm", hc, range(LT), H_C, DV_C, a["gla_norm_w"][0], g, ACT.Silu, hc, LN_EPS)
        stage_transpose(nc, "c_turn", consts["ident"][:, :], hc, lat_t, range(LT), KC)
        stage_linear(nc, "c_out", lat_t, token_tiles(LT), a["gla_w_out"][0], D, y)


def rms(nc, name, x, g, out):
    stage_head_norm(nc, name, x, range(LT), 1, D, g, None, None, out, EPS2)


def second_block(nc, consts, a, x, out):
    ident = consts["ident"][:, :]
    tiles = token_tiles(LT)
    w = a["w_in_2"][0]
    za, xb, lg, z, xbc, dt, gr = 0, 2 * D, 3 * D, 4 * D, 5 * D, 7 * D, 7 * D + S_HEADS
    with ExitStack() as ctx:
        sb = buffers(nc, ctx)
        hn = sb("b_hn", [P, LT, D])
        h_t = sb("b_h_t", [P, KC, SEQ])
        rms(nc, "b_rms1", x, a["norm_mix_g_2"][0], hn)
        stage_transpose(nc, "b_turn1", ident, hn, h_t, range(LT), KC)
        with ExitStack() as ctx2:
            branches = [buffers(nc, ctx2)(f"b_branch{i}", [P, LT, D]) for i in range(3)]
            with ExitStack() as c:
                sb = buffers(nc, c)
                uv, ya, ya_t = sb("b_uv", [P, LT, 2 * D]), sb("b_ya", [P, LT, D]), sb("b_ya_t", [P, KC, SEQ])
                stage_linear(nc, "b_za", h_t, tiles, w[:, za:za + 2 * D], 2 * D, uv, func=ACT.Gelu_apprx_tanh)
                stage_layer_norm(nc, "b_ln", uv, D, a["gmlp_ln_g_2"][0], a["gmlp_ln_b_2"][0], EPS2)
                stage_spatial(nc, uv, a["gmlp_w_s_2"][0], a["gmlp_b_s_2"][0], ident, consts["sees"][:, 0, :], ya)
                stage_transpose(nc, "b_turna", ident, ya, ya_t, range(LT), KC)
                stage_linear(nc, "b_wa", ya_t, tiles, a["w_branch_a_2"][0], D, branches[0])
            with ExitStack() as c:
                sb = buffers(nc, c)
                xr, xc, gate = (sb(f"b_{n}", [P, KC, SEQ]) for n in ("xr", "xc", "gate"))
                stage_linear(nc, "b_xb", h_t, tiles, w[:, xb:xb + D], D, xr, feature=True)
                stage_linear(nc, "b_lg", h_t, tiles, w[:, lg:lg + D], D, gate, feature=True, func=ACT.Gelu_apprx_tanh)
                stage_conv(nc, "b_conv", xr, KC, a["lru_conv_w_2"][0], a["lru_conv_b_2"][0], xc, False)
                stage_lru(nc, xc, gate, a["lru_w_r_2"][0], a["lru_b_r_2"][0], a["lru_w_i_2"][0], a["lru_b_i_2"][0], a["lru_lambda_2"][0])
                stage_linear(nc, "b_wb", gate, tiles, a["w_branch_b_2"][0], D, branches[1])
            with ExitStack() as c:
                sb = buffers(nc, c)
                zs, x_tok, y = (sb(f"b_{n}", [P, LT, D]) for n in ("zs", "x_tok", "y"))
                xr, xc = (sb(f"b_s{n}", [P, 2 * KC, SEQ]) for n in ("xr", "xc"))
                stage_linear(nc, "b_z", h_t, tiles, w[:, z:z + D], D, zs, func=ACT.Silu)
                stage_linear(nc, "b_xbc", h_t, tiles, w[:, xbc:xbc + 2 * D], 2 * D, xr, feature=True)
                stage_conv(nc, "b_sconv", xr, 2 * KC, a["ssd_conv_w_2"][0], a["ssd_conv_b_2"][0], xc, True)
                stage_transpose(nc, "b_turnx", ident, xc, x_tok, range(KC), LT)
                stage_ssd(nc, h_t, w[:, dt:dt + S_HEADS], a["ssd_dt_bias_2"][0], a["ssd_a_log_2"][0], a["ssd_d_2"][0], xc, x_tok, zs,
                          consts["ident"], consts["sel"], consts["far"], y)
                stage_head_norm(nc, "b_norm", y, range(LT), S_GROUPS, D // S_GROUPS, a["ssd_norm_g_2"][0], None, None, y, EPS2)
                y_t = sb("b_y_t", [P, KC, SEQ])
                stage_transpose(nc, "b_turnc", ident, y, y_t, range(LT), KC)
                stage_linear(nc, "b_wc", y_t, tiles, a["w_branch_c_2"][0], D, branches[2])
            with ExitStack() as c:
                g = buffers(nc, c)("b_g", [P, LT, 3 * D])
                stage_linear(nc, "b_g_lin", h_t, tiles, w[:, gr:gr + 3 * D], 3 * D, g)
                stage_merge_branches(nc, g, a["b_gate_2"][0], branches, hn)
            stage_transpose(nc, "b_turnm", ident, hn, h_t, range(LT), KC)
            stage_linear(nc, "b_out", h_t, tiles, a["w_out_2"][0], D, branches[0])
            stage_ops(nc, "b_res1", lambda link: link(nc.vector.tensor_tensor(x, x, branches[0][:, :, :], ALU.add)))
        rms(nc, "b_rms2", x, a["norm_mlp_g_2"][0], hn)
        stage_transpose(nc, "b_turn2", ident, hn, h_t, range(LT), KC)
        with ExitStack() as c:
            sb = buffers(nc, c)
            up = sb("b_up", [P, 4 * KC, SEQ])
            down = sb("b_down", [P, LT, D])
            stage_linear(nc, "b_mlp1", h_t, tiles, a["w_mlp_up_2"][0], 4 * D, up, feature=True, func=ACT.Relu)
            stage_ops(nc, "b_sq", lambda link: link(nc.vector.tensor_tensor(up[:, :, :], up[:, :, :], up[:, :, :], ALU.mult)))
            stage_linear(nc, "b_mlp2", up, tiles, a["w_mlp_down_2"][0], D, down, kb=4)
            stage_ops(nc, "b_res2", lambda link: link(nc.vector.tensor_tensor(x, x, down[:, :, :], ALU.add)))
        rms(nc, "b_rms3", x, a["final_norm_g_2"], hn)
        with stage(nc, "b_store") as st:
            stored = st.sem("stored")
            with nc.Block() as block:
                @block.sync
                def _(sp):
                    sp.dma_start(out[0].rearrange("(m p) d -> p m d", p=P), hn[:, :, :]).then_inc(stored, 16)
                    sp.wait_ge(stored, 16)


def shape_constants():
    pos = np.arange(SEQ)
    freq = (10000.0 ** (-np.arange(16, dtype=np.float32) / 16)).astype(np.float32)
    ang = np.concatenate([(pos // 64).astype(np.float32)[:, None] * freq, (pos % 64).astype(np.float32)[:, None] * freq], -1)
    cos = np.concatenate([np.ones((CTX, 32)), np.cos(ang)]).astype(np.float32)
    sin = np.concatenate([np.zeros((CTX, 32)), np.sin(ang)]).astype(np.float32)
    i = np.arange(P)
    seen = i[:, None] <= i[None, :]
    bars = np.zeros((P, LT, TOK), np.float32)
    bars[:, 0, 3 * P:] = np.where(i[None, :] <= i[:, None], 0, -BIG)
    bars[:, 1, 2 * P:3 * P] = np.where(i[:, None] <= i[None, :], 0, -BIG)
    sel = np.zeros((16, 16, P), np.float32)
    sel[np.arange(16), np.arange(16), :] = 1
    return {
        "ident": np.eye(P, dtype=np.float32),
        "cos": np.ascontiguousarray(cos.reshape(TT, P, 32).transpose(1, 0, 2)),
        "sin": np.ascontiguousarray(sin.reshape(TT, P, 32).transpose(1, 0, 2)),
        "far": np.stack([np.tile(np.where(m, 0, BIG), (1, TT)) for m in (seen, seen.T)], 1).astype(np.float32),
        "bars": bars,
        "sel": sel,
        "iota": np.tile(np.arange(TOPK, dtype=np.float32), (P, 1)),
        "sees": np.stack([seen, seen.T], 1).astype(np.float32),
    }


def build(nc, a, const_d, out):
    mod_rows = nc.dram_tensor("mod_rows", [DEPTH, 2, 6 * D], F32, kind="Internal").ap()

    def row(layer, context, chunk):
        return mod_rows[layer, 1 if context else 0, chunk * D:(chunk + 1) * D]

    def mods(layer, chunk, n_ctx=2):
        return [((0, 1), row(layer, True, chunk + 1), row(layer, True, chunk)),
                ((2, 3), row(layer, False, chunk + 1), row(layer, False, chunk))]

    with ExitStack() as ctx:
        sb = buffers(nc, ctx)
        consts = {k: sb(f"const_{k}", list(v.shape)) for k, v in const_d.items()}
        x = sb("x_tiles", [P, TT, D])
        landed = [ctx.enter_context(nc.semaphore(f"row_landed{k}")) for k in range(TOPK)]
        stage_load(nc, "load", [(consts[k][tuple([slice(None)] * len(d.shape))], d) for k, d in const_d.items()] + [
            (x[:, 0:2, :], a["ctx"][0].rearrange("(m p) d -> p m d", p=P)),
            (x[:, 2:4, :], a["x"][0].rearrange("(m p) d -> p m d", p=P))])
        stage_modulation(nc, a["c"], a["c_ctx"], a["w_mod"], a["b_mod"], mod_rows)
        ident = consts["ident"][:, :]
        with ExitStack() as c1:
            sb = buffers(nc, c1)
            h = sb("h_tiles", [P, TT, D])
            h_t = sb("h_t", [P, KC, TOK])
            y = sb("y_tiles", [P, TT, D])
            both = [(i, i) for i in range(TT)]
            stage_transpose(nc, "l0_mod1", ident, h, h_t, range(TT), KC, mod=mods(0, 0), x=x)
            mixer_ab(nc, consts, a, h_t, y)
            stage_residual_norm(nc, "l0_ln1", x, y, both, [((0, 1), row(0, True, 2)), ((2, 3), row(0, False, 2))], a["ln_w"][0, 0], a["ln_b"][0, 0])
            stage_transpose(nc, "l0_mod2", ident, h, h_t, range(TT), KC, mod=mods(0, 3), x=x)
            peer(nc, "l0_peer", 0, TT, consts, a, h[:, :, :], h_t, y[:, :, :], landed, 0)
            stage_residual_norm(nc, "l0_ln2", x, y, both, [((0, 1), row(0, True, 5)), ((2, 3), row(0, False, 5))], a["ln_w"][0, 1], a["ln_b"][0, 1])
            stage_transpose(nc, "l1_mod1", ident, h, h_t, range(TT), KC, mod=mods(1, 0), x=x)
            mixer_c(nc, consts, a, h_t, y)
            latents = [(2 + i, i) for i in range(LT)]
            stage_residual_norm(nc, "l1_ln1", x, y, latents, [((2, 3), row(1, False, 2))], a["ln_w"][1, 0], a["ln_b"][1, 0])
            stage_transpose(nc, "l1_mod2", ident, h[:, 0:2, :], h_t[:, :, 0:SEQ], range(LT), KC,
                            mod=[((0, 1), row(1, False, 4), row(1, False, 3))], x=x[:, 2:4, :])
            peer(nc, "l1_peer", 1, LT, consts, a, h[:, 0:LT, :], h_t, y[:, 0:LT, :], landed, 32 * HEADS * TT)
            stage_residual_norm(nc, "l1_ln2", x, y, latents, [((2, 3), row(1, False, 5))], a["ln_w"][1, 1], a["ln_b"][1, 1])
        second_block(nc, consts, a, x[:, 2:4, :], out)


def kernel(**inputs):
    import concourse.bacc as bacc
    from concourse.bass_utils import run_bass_kernel_spmd

    nc = bacc.Bacc("TRN2", target_bir_lowering=False, num_devices=1)
    arrays, a, const_d = {}, {}, {}
    for name, value in inputs.items():
        arrays[f"in_{name}"] = np.ascontiguousarray(value)
        a[name] = nc.dram_tensor(f"in_{name}", arrays[f"in_{name}"].shape, F32, kind="ExternalInput").ap()
    for name, value in shape_constants().items():
        arrays[f"constant_{name}"] = value
        const_d[name] = nc.dram_tensor(f"constant_{name}", value.shape, F32, kind="ExternalInput").ap()
    out = nc.dram_tensor("out", [1, SEQ, D], F32, kind="ExternalOutput").ap()
    build(nc, a, const_d, out)
    r = run_bass_kernel_spmd(nc, [arrays], core_ids=[0])
    return r.results[0]["out"]
```

```python
import math
from contextlib import ExitStack, contextmanager

import numpy as np

import concourse.bass as bass
from concourse import mybir
from concourse.alu_op_type import AluOpType as ALU

F32 = mybir.dt.float32
U32 = mybir.dt.uint32
ACT = mybir.ActivationFunctionType
AX_X = mybir.AxisListType.X

P = 128
D = 1024
KC = D // P
SEQ = 256
CTX = 256
TOK = CTX + SEQ
TT = TOK // P
BANK = 512
DEPTH = 2
ALPHA = (2 * DEPTH) ** 0.25
LN_EPS = 1e-5
EPS2 = 1e-6
BIG = 1e30
N_EXPERTS = 128 * 128


def ds(start, size):
    return bass.ds(start, size)


class Stage:

    def __init__(self, nc, name, ctx):
        self.nc, self.name, self.ctx, self.sems = nc, name, ctx, []

    def sem(self, name):
        s = self.ctx.enter_context(self.nc.semaphore(f"{self.name}_{name}"))
        self.sems.append(s)
        return s

    def sb(self, name, shape, dt=F32):
        return self.ctx.enter_context(self.nc.sbuf_tensor(f"{self.name}_{name}", shape, dt))

    def ps(self, name, shape, dt=F32):
        return self.ctx.enter_context(self.nc.psum_tensor(f"{self.name}_{name}", shape, dt))


@contextmanager
def stage(nc, name):
    with ExitStack() as ctx:
        st = Stage(nc, name, ctx)
        yield st
        for s in st.sems:
            nc.gpsimd.sem_clear(s)
        nc.all_engine_barrier()


class Link:

    def __init__(self, eng, sem, base=0):
        self.eng, self.sem, self.n = eng, sem, base

    def __call__(self, ins):
        self.n = self.n + 1
        ins.then_inc(self.sem, 1)
        self.eng.wait_ge(self.sem, self.n)


class Weights:

    def __init__(self, nc, ctx, plan):
        self.slots = ctx.enter_context(nc.sbuf_tensor("weight_slots", [P, 2, KC, BANK], F32))
        self.loaded = [ctx.enter_context(nc.semaphore(f"weights_loaded{s}")) for s in range(2)]
        self.plan = plan
        self.at = 0
        self.n = 0

    def tiles(self, entry):
        _, w, n_cols, kb = entry
        rows = w.rearrange("(b k p) n -> b p k n", p=P, k=KC)
        return [(rows[b], n0, min(BANK, n_cols - n0)) for n0 in range(0, n_cols, BANK) for b in range(kb)]

    def ahead(self, i):
        at = self.at
        while at < len(self.plan) and self.plan[at] is not None:
            tiles = self.tiles(self.plan[at])
            if i < len(tiles):
                return tiles[i]
            i -= len(tiles)
            at += 1
        return None

    def load(self, sp, i, n0=None):
        tile = self.ahead(i)
        if tile is None:
            return
        rows, first, width = tile
        slot = (self.n + i) % 2
        sp.dma_start(self.slots[:, slot, :, 0:width], rows[:, :, ds(first if n0 is None else n0, width)]).then_inc(self.loaded[slot], 16)

    def begin(self, sp):
        if self.plan[self.at] is None:
            self.at += 1
        for i in range(2):
            self.load(sp, i)

    def count(self, i, turn):
        before = (self.n + 1 - (self.n + i) % 2) // 2
        return 16 * before + 16 * turn + 16


def stage_linear(nc, name, weights, act_t, tiles, out, feature=False, func=None, side=None, rows=None):
    planned, w, n_cols, kb = weights.plan[weights.at]
    assert planned == name, (planned, name)
    n_tok = tiles[-1][0] + tiles[-1][1]
    full, tail = divmod(n_cols, BANK)
    steps = len(weights.tiles(weights.plan[weights.at]))
    by_tile = len(out.shape) == 4
    if by_tile:
        flat = out
    elif feature:
        flat = out.rearrange("p f t -> p (f t)")
    else:
        flat = out.rearrange("p m n -> p (m n)")
    per_bank = BANK // n_tok if feature else 1
    n_banks = 4 // per_bank if feature else len(tiles)

    def groups(width):
        if feature:
            return [(f, P, n_tok, f // per_bank, f % per_bank * n_tok) for f in range(width // P)]
        return [(m, size, width, m, 0) for m, (_, size) in enumerate(tiles)]

    def where(n0, g, size):
        if feature:
            return ds((n0 // P + g) * n_tok if isinstance(n0, int) else n0 * n_tok // P + g * n_tok, size)
        return ds(g * n_cols + n0, size)

    both = func is None and len(groups(BANK)) > 1 and side is None
    with stage(nc, name) as st:
        acc = st.ps("acc", [P, 2, n_banks, BANK])
        mm_done = st.sem("mm_done")
        act_out = st.sem("act_out")
        dve_out = st.sem("dve_out")
        rows_loaded = st.sem("rows_loaded")
        parts = side(st) if side else []

        def do(engine, eng, at):
            if at < len(parts) and engine in parts[at]:
                parts[at][engine](eng)

        def multiply(pe, i, width, turn, half, b, t):
            slot = (weights.n + i) % 2 if isinstance(i, int) else (weights.n + half) % 2
            pe.wait_ge(weights.loaded[slot], weights.count(i if isinstance(i, int) else half, turn))
            if b == 0:
                pe.wait_ge(act_out, t + 1)
                if both:
                    pe.wait_ge(dve_out, t + 1)
            todo = groups(width)
            for g, rows, cols, bank, col in todo:
                for k in range(KC):
                    wt = weights.slots[:, slot, k, :]
                    if feature:
                        lhs, rhs = wt[:, g * P:(g + 1) * P], act_t[:, b * KC + k, 0:n_tok]
                    else:
                        lhs, rhs = act_t[:, b * KC + k, tiles[g][0]:tiles[g][0] + rows], wt[:, 0:width]
                    last = nc.tensor.matmul(acc[0:rows, half, bank, col:col + cols], lhs, rhs,
                                            start=(b == 0 and k == 0), stop=(b == kb - 1 and k == KC - 1))
                if g == todo[-1][0]:
                    last.then_inc(mm_done, 1)
                if side:
                    do("tensor", pe, (t * kb + b) * len(todo) + g)

        def empty(eng, mine, n_steps, n0, width, half, dve, tile):
            eng.wait_ge(mm_done, n_steps + 2)
            todo = [x for x in groups(width) if not both or x[3] % 2 == (1 if dve else 0)]
            for i, (g, rows, cols, bank, col) in enumerate(todo):
                src = acc[0:rows, half, bank, col:col + cols]
                if by_tile:
                    f = ds(tile * (BANK // P) + g, 1)
                    dst, src = flat[:, :, f, :].rearrange("p m o t -> p m (o t)"), src.rearrange("p (m t) -> p m t", t=P)
                else:
                    dst = flat[0:rows, where(n0, g, cols)]
                if dve:
                    ins = nc.vector.tensor_copy(dst, src)
                else:
                    ins = nc.scalar.activation(dst, src, func or ACT.Copy)
                if i == len(todo) - 1:
                    ins.then_inc(mine, 1)
            if not todo:
                eng.sem_inc(mine, 1)

        pairs = full // 2 if kb == 1 and full >= 4 and not side else 0
        rest = list(range(2 * pairs, full + (1 if tail else 0)))

        def run(eng, one):
            if pairs:
                with eng.Fori(0, pairs) as i:
                    for s in range(2):
                        one(i * 2 + s, i * (2 * BANK) + s * BANK, BANK, s, i)
            for t in rest:
                one(t, t * BANK, tail if t == full else BANK, t % 2, t // 2)

        with nc.Block() as block:
            @block.sync
            def _(sp):
                for part in parts:
                    if "sync" in part:
                        part["sync"](sp)
                if rows:
                    rows.load(sp, rows_loaded)
                looped = max(pairs - 1, 0)
                if looped:
                    with sp.Fori(0, looped) as i:
                        for s in range(2):
                            sp.wait_ge(mm_done, i * 2 + (s + 3))
                            weights.load(sp, s + 2, i * (2 * BANK) + (s + 2) * BANK)
                for i in range(2 * looped, steps):
                    sp.wait_ge(mm_done, i + 3)
                    weights.load(sp, i + 2)
                if rows:
                    sp.wait_ge(rows_loaded, 16 * len(rows.pairs))
                    rows.there = True

            @block.tensor
            def _(pe):
                pe.sem_inc(mm_done, 2)

                def one(t, n0, width, half, turn):
                    for b in range(kb):
                        i = t * kb + b
                        multiply(pe, i, width, i // 2 if isinstance(i, int) else turn, half, b, t)
                run(pe, one)
                for at in range(steps * len(groups(BANK)), len(parts)):
                    do("tensor", pe, at)

            @block.scalar
            def _(act):
                act.sem_inc(act_out, 2)

                def one(t, n0, width, half, turn):
                    per = kb * len(groups(BANK))
                    if side:
                        for at in range(t * per, (t + 1) * per):
                            do("scalar", act, at)
                    empty(act, act_out, t * kb + kb, n0, width, half, False, t)
                run(act, one)
                for at in range(steps * len(groups(BANK)), len(parts)):
                    do("scalar", act, at)

            @block.vector
            def _(dve):
                dve.sem_inc(dve_out, 2)
                if both:
                    run(dve, lambda t, n0, width, half, turn: empty(dve, dve_out, t * kb + kb, n0, width, half, True, t))
                for at in range(len(parts)):
                    do("vector", dve, at)
    weights.n += steps
    weights.at += 1


def stage_transpose(nc, name, ident, src, dst, tiles, chunks, mod=None, x=None, make=None):
    with stage(nc, name) as st:
        loaded = st.sem("loaded")
        made = st.sem("made")
        turned = st.sem("turned")
        emptied = st.sem("emptied")
        chain = st.sem("chain")
        ps = st.ps("turned", [P, 4, 4, P])
        rows = st.sb("rows", [P, 4, D]) if mod else None
        per = min(4, chunks)
        quads = [(m, q) for m in range(len(tiles)) for q in range(chunks // per)]
        with nc.Block() as block:
            if mod:
                @block.vector
                def _(dve):
                    link = Link(dve, chain)
                    dve.wait_ge(loaded, 32 * len(mod))
                    for i, (ms, _, _) in enumerate(mod):
                        for m in ms:
                            link(nc.vector.tensor_tensor(src[:, m, :], x[:, m, :], rows[:, 2 * i, :], ALU.mult))
                            nc.vector.tensor_tensor(src[:, m, :], src[:, m, :], rows[:, 2 * i + 1, :], ALU.add).then_inc(made, 1)

            if make:
                @block.vector
                def _(dve):
                    link = Link(dve, chain)
                    for i in range(len(tiles)):
                        make(link, i).then_inc(made, 1)

            @block.tensor
            def _(pe):
                for i, (m, q) in enumerate(quads):
                    if mod or make:
                        pe.wait_ge(made, m + 1)
                    if i >= 4:
                        pe.wait_ge(emptied, i - 3)
                    for k in range(per):
                        c = per * q + k
                        last = nc.tensor.transpose(ps[:, i % 4, k, :], src[:, tiles[m], c * P:(c + 1) * P], ident)
                    last.then_inc(turned, 1)

            @block.scalar
            def _(act):
                for i, (_, scale, shift) in enumerate(mod or []):
                    act.dma_start(rows[:, 2 * i, :], scale.partition_broadcast(P)).then_inc(loaded, 16)
                    act.dma_start(rows[:, 2 * i + 1, :], shift.partition_broadcast(P)).then_inc(loaded, 16)
                for i, (m, q) in enumerate(quads):
                    act.wait_ge(turned, i + 1)
                    nc.scalar.activation(dst[:, per * q:per * q + per, m * P:(m + 1) * P], ps[:, i % 4, 0:per, :], ACT.Copy).then_inc(emptied, 1)


def turn_parts(nc, st, ident, src, dst, tiles, chunks, banks=2, ready=None, per_part=2):
    per = min(4, chunks)
    turned, emptied = st.sem("turn_done"), st.sem("turn_emptied")
    ps = st.ps("turn", [P, banks, 4, P])
    quads = [(m, q) for m in range(len(tiles)) for q in range(chunks // per)]

    def part(lo, hi):
        def tensor(pe):
            if lo == 0 and ready:
                ready(pe)
            for i in range(lo, hi):
                m, q = quads[i]
                if i >= banks:
                    pe.wait_ge(emptied, i - banks + 1)
                for k in range(per):
                    c = per * q + k
                    last = nc.tensor.transpose(ps[:, i % banks, k, :], src[:, tiles[m], c * P:(c + 1) * P], ident)
                last.then_inc(turned, 1)

        def scalar(act):
            for i in range(lo, hi):
                m, q = quads[i]
                act.wait_ge(turned, i + 1)
                nc.scalar.activation(dst[:, per * q:per * q + per, m * P:(m + 1) * P], ps[:, i % banks, 0:per, :], ACT.Copy).then_inc(emptied, 1)
        return {"tensor": tensor, "scalar": scalar}

    parts = [part(lo, min(lo + per_part, len(quads))) for lo in range(0, len(quads), per_part)]
    return parts, emptied, len(quads)


class Modulation:

    def __init__(self, nc, st, weights, name, silu_c, bias, mod_rows, first, banks):
        planned, _, n, _ = weights.plan[weights.at]
        assert planned == name, (planned, name)
        self.nc, self.weights, self.silu_c, self.banks = nc, weights, silu_c, banks
        self.tiles = n // BANK
        self.bias, self.mod_rows, self.first = bias, mod_rows, first
        self.bias_sb = st.sb("mod_bias", [2, 2, BANK])
        self.rows = st.sb("mod_rows", [2, 2, BANK])
        self.used, self.taken = st.sem("mod_used"), st.sem("mod_taken")
        self.bias_loaded = [st.sem(f"mod_bias_loaded{s}") for s in range(2)]
        self.stored = [st.sem(f"mod_stored{s}") for s in range(2)]
        self.link_sem = st.sem("mod_chain")
        self.links = 0

    def share(self, u, units):
        return range(u * self.tiles * KC // units, (u + 1) * self.tiles * KC // units)

    def tensor(self, pe, u, units):
        for step in self.share(u, units):
            i, k = divmod(step, KC)
            slot = (self.weights.n + i) % 2
            if k == 0:
                pe.wait_ge(self.weights.loaded[slot], self.weights.count(i, i // 2))
                if i >= len(self.banks):
                    pe.wait_ge(self.taken, i - len(self.banks) + 1)
            ins = self.nc.tensor.matmul(self.banks[i % len(self.banks)][0:2, :], self.silu_c[:, k, :], self.weights.slots[:, slot, k, :],
                                        start=(k == 0), stop=(k == KC - 1))
            if k == KC - 1:
                ins.then_inc(self.used, 1)

    def vector(self, dve, u, units):
        for step in self.share(u, units):
            i, k = divmod(step, KC)
            if k != KC - 1:
                continue
            s, turn = i % 2, i // 2
            dve.wait_ge(self.used, i + 1)
            dve.wait_ge(self.bias_loaded[s], 16 * turn + 16)
            if turn:
                dve.wait_ge(self.stored[s], 16 * turn)
            ins = self.nc.vector.tensor_tensor(self.rows[:, s, :], self.banks[i % len(self.banks)][0:2, :], self.bias_sb[:, s, :], ALU.add)
            if (self.first + i * BANK) // D in (1, 4):
                ins.then_inc(self.link_sem, 1)
                self.links = self.links + 1
                dve.wait_ge(self.link_sem, self.links)
                ins = self.nc.vector.tensor_scalar(self.rows[:, s, :], self.rows[:, s, :], 1.0, None, ALU.add)
            ins.then_inc(self.taken, 1)

    def sync(self, sp):
        def bias(i):
            at = self.first + i * BANK
            if i < self.tiles:
                sp.dma_start(self.bias_sb[:, i % 2, :], self.bias[at:at + BANK].partition_broadcast(2)).then_inc(self.bias_loaded[i % 2], 16)

        bias(0)
        bias(1)
        for i in range(self.tiles):
            sp.wait_ge(self.used, i + 1)
            self.weights.load(sp, i + 2)
            sp.wait_ge(self.taken, i + 1)
            at = self.first + i * BANK
            sp.dma_start(self.mod_rows[:, at:at + BANK], self.rows[:, i % 2, :]).then_inc(self.stored[i % 2], 16)
            bias(i + 2)
        for s in range(2):
            sp.wait_ge(self.stored[s], 16 * ((self.tiles + 1 - s) // 2))

    def done(self):
        self.weights.n += self.tiles
        self.weights.at += 1


def stage_conditions(nc, weights, c, c_ctx, silu_c):
    with stage(nc, "conditions") as st:
        cols = st.sb("cols", [P, KC, 2])
        loaded = st.sem("loaded")
        with nc.Block() as block:
            @block.sync
            def _(sp):
                sp.dma_start(cols[:, :, 0], c.rearrange("a (k p) -> p (a k)", p=P), allow_slow_non_contiguous=True).then_inc(loaded, 16)
                sp.dma_start(cols[:, :, 1], c_ctx.rearrange("(k p) -> p k", p=P), allow_slow_non_contiguous=True).then_inc(loaded, 16)
                weights.begin(sp)

            @block.scalar
            def _(act):
                act.wait_ge(loaded, 32)
                nc.scalar.activation(silu_c[:, :, :], cols[:, :, :], ACT.Silu)


def stage_first_modulation(nc, weights, silu_c, bias, mod_rows, pairs):
    with stage(nc, "mod0") as st:
        loaded = st.sem("loaded")
        ps = st.ps("mod", [P, 2, BANK])
        mod = Modulation(nc, st, weights, "mod0_first", silu_c, bias, mod_rows, 0, [ps[:, i, :] for i in range(2)])
        with nc.Block() as block:
            @block.sync
            def _(sp):
                for dst, src in pairs:
                    sp.dma_start(dst, src).then_inc(loaded, 16)
                mod.sync(sp)
                sp.wait_ge(loaded, 16 * len(pairs))

            @block.tensor
            def _(pe):
                mod.tensor(pe, 0, 1)

            @block.vector
            def _(dve):
                mod.vector(dve, 0, 1)
    mod.done()


class NormRows:

    def __init__(self, sb, name, gates, ln, mods=()):
        sources = [g for _, g in gates] + list(ln) + [r for _, scale, shift in mods for r in (scale, shift)]
        self.buffer = sb(f"{name}_rows", [P, len(sources), D])
        self.pairs = [(self.buffer[:, i, :], src.partition_broadcast(P)) for i, src in enumerate(sources)]
        n = len(gates)
        self.norm_rows = n + 2
        self.gate = {m: self.buffer[:, i, :] for i, (ms, _) in enumerate(gates) for m in ms}
        self.weight, self.bias = self.buffer[:, n, :], self.buffer[:, n + 1, :]
        self.mod = {m: (self.buffer[:, n + 2 + 2 * i, :], self.buffer[:, n + 3 + 2 * i, :]) for i, (ms, _, _) in enumerate(mods) for m in ms}
        self.there = False

    def load(self, eng, sem, mod_sem=None):
        for i, (dst, src) in enumerate(self.pairs):
            eng.dma_start(dst, src).then_inc(mod_sem if mod_sem is not None and i >= self.norm_rows else sem, 16)


def stage_residual_norm(nc, name, x, y, tiles, rows, weights=None, turn=None, keys=None):
    with stage(nc, name) as st:
        loaded, chain, var_ready, std_ready = st.sem("loaded"), st.sem("chain"), st.sem("var_ready"), st.sem("std_ready")
        keys_loaded, made, turned, emptied = st.sem("keys_loaded"), st.sem("made"), st.sem("turned"), st.sem("emptied")
        stats = st.sb("stats", [P, 2, 6])
        agg = st.sb("agg", [P, 4, 2])
        std = st.sb("std", [P, 4])
        rstd = st.sb("rstd", [P, 4])
        ps = st.ps("turned", [P, 4, 4, P])
        mods_loaded = st.sem("mods_loaded")
        quads = []
        if keys:
            for q in range(HALVES // 4):
                quads.append((0, [keys[1][:, c, :] for c in range(4 * q, 4 * q + 4)], keys[2][:, 4 * q:4 * q + 4, :]))
        if turn:
            ident, h, h_t = turn
            for i in range(len(tiles)):
                for q in range(KC // 4):
                    quads.append((i + 1, [h[:, i, c * P:(c + 1) * P] for c in range(4 * q, 4 * q + 4)], h_t[:, 4 * q:4 * q + 4, i * P:(i + 1) * P]))
        with nc.Block() as block:
            @block.sync
            def _(sp):
                if not rows.there:
                    rows.load(sp, loaded, mods_loaded)
                if keys:
                    sp.dma_start(keys[1], keys[0]).then_inc(keys_loaded, 16)
                if weights:
                    weights.begin(sp)

            @block.vector
            def _(dve):
                link = Link(dve, chain)
                if not rows.there:
                    dve.wait_ge(loaded, 16 * rows.norm_rows)

                def sums(i):
                    m, ym = tiles[i]
                    link(nc.vector.tensor_tensor(y[:, ym, :], y[:, ym, :], rows.gate[m], ALU.mult))
                    link(nc.vector.scalar_tensor_tensor(x[:, m, :], x[:, m, :], ALPHA, y[:, ym, :], ALU.mult, ALU.add))
                    nc.vector.bn_stats(stats[:, 0, :], x[:, m, 0:BANK]).then_inc(chain, 1)
                    link.n += 1
                    link(nc.vector.bn_stats(stats[:, 1, :], x[:, m, BANK:D]))
                    link(nc.vector.bn_aggr(agg[:, i, :], stats[:, :, :].rearrange("p a b -> p (a b)")))
                    nc.vector.tensor_scalar(agg[:, i, 1:2], agg[:, i, 1:2], LN_EPS, None, ALU.add).then_inc(var_ready, 1)

                def normalise(i):
                    m, ym = tiles[i]
                    dve.wait_ge(std_ready, i + 1)
                    link(nc.vector.reciprocal(rstd[:, i:i + 1], std[:, i:i + 1]))
                    link(nc.vector.tensor_scalar(x[:, m, :], x[:, m, :], agg[:, i, 0:1], rstd[:, i:i + 1], ALU.subtract, ALU.mult))
                    link(nc.vector.tensor_tensor(x[:, m, :], x[:, m, :], rows.weight, ALU.mult))
                    link(nc.vector.tensor_tensor(x[:, m, :], x[:, m, :], rows.bias, ALU.add))
                    if turn:
                        scale, shift = rows.mod[m]
                        if not rows.there:
                            dve.wait_ge(mods_loaded, 16 * (len(rows.pairs) - rows.norm_rows))
                        link(nc.vector.tensor_tensor(h[:, i, :], x[:, m, :], scale, ALU.mult))
                        nc.vector.tensor_tensor(h[:, i, :], h[:, i, :], shift, ALU.add).then_inc(made, 1)

                sums(0)
                for i in range(len(tiles)):
                    if i + 1 < len(tiles):
                        sums(i + 1)
                    normalise(i)

            if quads:
                @block.tensor
                def _(pe):
                    if keys:
                        pe.wait_ge(keys_loaded, 16)
                    for i, (tile, blocks, _) in enumerate(quads):
                        if tile:
                            pe.wait_ge(made, tile)
                        if i >= 4:
                            pe.wait_ge(emptied, i - 3)
                        for k, src in enumerate(blocks):
                            last = nc.tensor.transpose(ps[:, i % 4, k, :], src, ident)
                        last.then_inc(turned, 1)

            @block.scalar
            def _(act):
                def copy(i):
                    act.wait_ge(turned, i + 1)
                    nc.scalar.activation(quads[i][2], ps[:, i % 4, :, :], ACT.Copy).then_inc(emptied, 1)

                def root(i):
                    act.wait_ge(var_ready, i + 1)
                    nc.scalar.activation(std[:, i:i + 1], agg[:, i, 1:2], ACT.Sqrt).then_inc(std_ready, 1)

                root(0)
                for i in range(len(tiles)):
                    if i + 1 < len(tiles):
                        root(i + 1)
                    for q, (tile, _, _) in enumerate(quads):
                        if max(tile, 1) == i + 1:
                            copy(q)


H_M = 4
H_A, H_KV, DH_A = 8, 2, 64
GROUP = H_A // H_KV
M_W = H_M * P
A_Q = H_A * DH_A
A_KV = H_KV * DH_A

SEEN = [{0: [(1, 4)], 1: [(2, 4)], 2: [(3, 4)], 3: []},
        {0: [(2, 4)], 1: [(0, 1), (2, 4)], 2: [], 3: [(2, 3)]}]


def sources(d, t):
    return [s for s in range(TT) if s == t or any(a <= t < b for a, b in SEEN[d][s])]


def reversed_time(ap2, seg):
    a = ap2[:, seg * SEQ:(seg + 1) * SEQ]
    return a[:, ::-1]


def stage_gates(nc, act_t, w, gate_b, ident, sel, g_cols, m_rows):
    with stage(nc, "gates") as st:
        wg = st.sb("w", [P, KC, 16])
        wq = st.sb("w_quadrants", [P, KC, 4, 32])
        bias = st.sb("bias", [4, 4])
        g = st.sb("g", [4, 4, TOK])
        tmp = st.sb("tmp", [4, 2, TOK])
        scan = st.sb("scan", [4, 2, 3, TOK])
        zero_one = st.sb("zero_one", [4, 2, TOK])
        mm = st.sb("mm", [4, 2, 2, TOK])
        rows = st.sb("rows", [4, 2, 2, TOK])
        ps = st.ps("ps", [P, BANK])
        pc = st.ps("pc", [P, 2, TT, 2, 4])
        loaded, mm_done, g_ready = st.sem("loaded"), st.sem("mm_done"), st.sem("g_ready")
        ln_ready, chain, m_ready, e_ready, rows_ready, cols_done = (
            st.sem(x) for x in ("ln_ready", "chain", "m_ready", "e_ready", "rows_ready", "cols_done"))
        achain, spread = st.sem("achain"), st.sem("spread")
        with nc.Block() as block:
            @block.tensor
            def _(pe):
                pe.wait_ge(spread, 1)
                for k in range(KC):
                    last = nc.tensor.matmul(ps[:, :], wq[:, k, :, :].rearrange("p j c -> p (j c)"), act_t[:, k, 0:TOK],
                                            start=(k == 0), stop=(k == KC - 1))
                last.then_inc(mm_done, 1)
                pe.wait_ge(rows_ready, 1)
                for d in range(2):
                    for m in range(TT):
                        for y in range(2):
                            last = nc.tensor.matmul(pc[:, d, m, y, :], rows[:, d, y, m * P:(m + 1) * P], ident[0:4, 0:4],
                                                    start=True, stop=True)
                last.then_inc(cols_done, 1)

            @block.scalar
            def _(act):
                link = Link(act, achain)
                act.dma_start(wg[:, :, :], w.rearrange("(k p) n -> p k n", p=P)).then_inc(loaded, 16)
                act.dma_start(bias[:, :], gate_b.rearrange("d y h -> h (d y)"), allow_slow_non_contiguous=True).then_inc(loaded, 16)
                act.wait_ge(mm_done, 1)
                for j in range(4):
                    link(nc.scalar.activation(g[:, j, :], ps[32 * j:32 * j + 4, :], ACT.Identity, bias=bias[:, j:j + 1]))
                for d in range(2):
                    link(nc.scalar.activation(tmp[:, d, :], g[:, 2 * d + 1, :], ACT.Abs))
                    link(nc.scalar.activation(tmp[:, d, :], tmp[:, d, :], ACT.Exp, scale=-1.0))
                    nc.scalar.activation(tmp[:, d, :], tmp[:, d, :], ACT.Ln, bias=1.0).then_inc(ln_ready, 1)
                for d in range(2):
                    act.wait_ge(m_ready, d + 1)
                    nc.scalar.activation(mm[:, d, 1, :], mm[:, d, 1, :], ACT.Exp, scale=-1.0).then_inc(e_ready, 1)

            @block.vector
            def _(dve):
                link = Link(dve, chain)
                link(nc.vector.memset(wq[:, :, :, :].rearrange("p k j c -> p (k j c)"), 0.0))
                dve.wait_ge(loaded, 32)
                nc.vector.tensor_copy(wq[:, :, :, 0:4], wg[:, :, :].rearrange("p k (j c) -> p k j c", c=4)).then_inc(spread, 1)
                link(nc.vector.memset(zero_one[:, 0, :], 0.0))
                link(nc.vector.memset(zero_one[:, 1, :], 1.0))
                for d in range(2):
                    dve.wait_ge(ln_ready, d + 1)
                    for seg in range(2):
                        sl = slice(seg * SEQ, (seg + 1) * SEQ)
                        src = (lambda ap: ap[:, sl]) if d == 0 else (lambda ap: reversed_time(ap, seg))
                        last = nc.vector.scalar_tensor_tensor(scan[:, d, 0, sl], src(g[:, 2 * d + 1, :]), 0.0, src(tmp[:, d, :]), ALU.min, ALU.subtract)
                    link(last)
                    link(nc.vector.tensor_tensor_scan(scan[:, d, 1, :], zero_one[:, 1, :], scan[:, d, 0, :], 0.0, ALU.mult, ALU.add))
                    for seg in range(2):
                        sl = slice(seg * SEQ, (seg + 1) * SEQ)
                        src = (lambda ap: ap[:, sl]) if d == 0 else (lambda ap: reversed_time(ap, seg))
                        last = nc.vector.tensor_tensor(scan[:, d, 2, sl], src(g[:, 2 * d, :]), scan[:, d, 1, sl], ALU.subtract)
                    link(last)
                    link(nc.vector.tensor_tensor_scan(mm[:, d, 0, :], zero_one[:, 0, :], scan[:, d, 2, :], 0.0, ALU.add, ALU.max))
                    nc.vector.tensor_tensor(mm[:, d, 1, :], mm[:, d, 0, :], scan[:, d, 1, :], ALU.add).then_inc(m_ready, 1)
                for d in range(2):
                    dve.wait_ge(e_ready, d + 1)
                    for seg in range(2):
                        sl = slice(seg * SEQ, (seg + 1) * SEQ)
                        src = (lambda ap: ap[:, sl]) if d == 0 else (lambda ap: reversed_time(ap, seg))
                        nc.vector.tensor_copy(rows[:, d, 0, sl], src(scan[:, d, 2, :]))
                        nc.vector.tensor_copy(rows[:, d, 1, sl], src(mm[:, d, 1, :]))
                        last = nc.vector.tensor_copy(m_rows[:, d, sl], src(mm[:, d, 0, :]))
                last.then_inc(rows_ready, 1)
                dve.wait_ge(cols_done, 1)
                nc.vector.tensor_copy(g_cols[:, :, :, :, :].rearrange("p d m y h -> p (d m y h)"),
                                      pc[:, :, :, :, :].rearrange("p d m y h -> p (d m y h)"))


def stage_mlstm(nc, qk_t, v_aug, g_cols, m_rows, sel, far, hm, weights, mod_args):
    with stage(nc, "mlstm") as st:
        m_far = st.sb("m_far", [P, TOK])
        e = st.sb("e", [P, TT, TOK])
        w = st.sb("w", [P, TT, TOK])
        den = st.sb("den", [P, TT])
        ps_s = st.ps("scores", [P, TT, BANK])
        ps_m = st.ps("m_bcast", [P, BANK])
        ps_o = st.ps("out", [P, 2, BANK])
        scored, m_sent, far_ready, e_ready, w_ready, out_done, out_taken, chain = (
            st.sem(x) for x in ("scored", "m_sent", "far_ready", "e_ready", "w_ready", "out_done", "out_taken", "chain"))
        units = [(h, d) for h in range(H_M) for d in range(2)]
        ps_mod = st.ps("mod", [P, BANK])
        mod = Modulation(nc, st, weights, "mod0_rest", *mod_args, 2 * D, [ps_mod[:, :]])

        def out_ap(t, cols):
            return ps_o[:, t // 2, (t % 2) * 256:(t % 2) * 256 + cols]

        with nc.Block() as block:
            @block.tensor
            def _(pe):
                for u, (h, d) in enumerate(units):
                    if u:
                        pe.wait_ge(w_ready, u)
                    if d == 0:
                        for s in range(TT):
                            last = nc.tensor.matmul(ps_s[:, s, :], qk_t[:, H_M + h, s * P:(s + 1) * P], qk_t[:, h, :],
                                                    start=True, stop=True)
                        last.then_inc(scored, 1)
                    nc.tensor.matmul(ps_m[:, :], sel[0:4, h, :], m_rows[:, d, :], start=True, stop=True).then_inc(m_sent, 1)
                    mod.tensor(pe, u, len(units))
                    pe.wait_ge(w_ready, u + 1)
                    if u:
                        pe.wait_ge(out_taken, u)
                    for t in range(TT):
                        src = sources(d, t)
                        for s in src:
                            last = nc.tensor.matmul(out_ap(t, P + 1), w[:, s, t * P:(t + 1) * P], v_aug[:, s, h, 0:P + 1],
                                                    start=(s == src[0]), stop=(s == src[-1]))
                    last.then_inc(out_done, 1)

            @block.scalar
            def _(act):
                for u, (h, d) in enumerate(units):
                    act.wait_ge(m_sent, u + 1)
                    act.wait_ge(far_ready, u + 1)
                    if u:
                        act.wait_ge(w_ready, u)
                    for s in range(TT):
                        a = g_cols[:, d, s, 0, h:h + 1]
                        last = nc.scalar.activation(e[:, s, s * P:(s + 1) * P], m_far[:, s * P:(s + 1) * P], ACT.Exp, bias=a, scale=-1.0)
                        for t0, t1 in SEEN[d][s]:
                            last = nc.scalar.activation(e[:, s, t0 * P:t1 * P], ps_m[:, t0 * P:t1 * P], ACT.Exp, bias=a, scale=-1.0)
                    last.then_inc(e_ready, 1)

            @block.sync
            def _(sp):
                mod.sync(sp)

            @block.vector
            def _(dve):
                link = Link(dve, chain)
                for u, (h, d) in enumerate(units):
                    dve.wait_ge(m_sent, u + 1)
                    if u:
                        dve.wait_ge(e_ready, u)
                    nc.vector.tensor_tensor(m_far[:, :], ps_m[:, :], far[:, d, :], ALU.add).then_inc(far_ready, 1)
                    dve.wait_ge(e_ready, u + 1)
                    dve.wait_ge(scored, h + 1)
                    if u:
                        dve.wait_ge(out_done, u)
                    for s in range(TT):
                        for t0, t1 in [(s, s + 1)] + SEEN[d][s]:
                            sl = slice(t0 * P, t1 * P)
                            last = nc.vector.scalar_tensor_tensor(w[:, s, sl], ps_s[:, s, sl], float(P) ** -0.5, e[:, s, sl], ALU.mult, ALU.mult)
                    last.then_inc(w_ready, 1)
                    mod.vector(dve, u, len(units))
                    dve.wait_ge(out_done, u + 1)
                    sums = ps_o[:, :, :].rearrange("p a (b c) -> p (a b) c", c=256)[:, :, P]
                    link(nc.vector.tensor_copy(den[:, :], sums))
                    link(nc.vector.scalar_tensor_tensor(den[:, :], den[:, :], -1.0, den[:, :], ALU.mult, ALU.max))
                    link(nc.vector.tensor_tensor(den[:, :], den[:, :], g_cols[:, d, :, 1, h], ALU.max))
                    link(nc.vector.reciprocal(den[:, :], den[:, :]))
                    for t in range(TT):
                        o = hm[:, t, h * P:(h + 1) * P]
                        if d == 0:
                            link(nc.vector.tensor_scalar(o, out_ap(t, P), den[:, t:t + 1], None, ALU.mult))
                        else:
                            link(nc.vector.scalar_tensor_tensor(o, out_ap(t, P), den[:, t:t + 1], o, ALU.mult, ALU.add))
                    dve.sem_inc(out_taken, 1)
    mod.done()


def stage_value_ones(nc, name, v, v_aug):
    with stage(nc, name) as st:
        chain = st.sem("chain")
        with nc.Block() as block:
            @block.vector
            def _(dve):
                link = Link(dve, chain)
                link(nc.vector.memset(v_aug[:, :, :, P:P + 1].rearrange("p m h o -> p (m h) o"), 1.0))
                for m in range(TT):
                    link(nc.vector.tensor_copy(v_aug[:, m, :, 0:P], v[:, m, :].rearrange("p (h e) -> p h e", e=P)))


def stage_attention(nc, qkv, cos, sin, bars, sink, ident, cat, weights, mod_args):
    heads = H_A + H_KV
    scale = DH_A ** -0.5
    with stage(nc, "attn") as st:
        qr = st.sb("qr", [P, GROUP, H_KV, DH_A])
        kr = st.sb("kr", [P, H_KV, DH_A])
        t1, t2, t3, t4 = (st.sb(f"rot{i}", [P, heads, 32]) for i in range(4))
        qt = st.sb("qt", [P, GROUP, TOK])
        kt = st.sb("kt", [P, TOK])
        sink_b = st.sb("sink", [P, H_A])
        s_sb = st.sb("s", [P, 2, TOK])
        p_sb = st.sb("p", [P, 2, TOK])
        pt = st.sb("pt", [P, 2, TOK])
        small = st.sb("small", [P, 4, 8])
        ps_t = st.ps("turn", [P, 2, BANK])
        ps_s = st.ps("scores", [P, 2, BANK])
        ps_p = st.ps("p_turn", [P, 2, BANK])
        ps_o = st.ps("out", [P, 2, BANK])
        names = ("loaded", "rotated", "turned", "copied", "scored", "masked", "max_ready", "exped", "p_turned",
                 "p_copied", "out_done", "out_taken", "chain", "achain")
        loaded, rotated, turned, copied, scored, masked, max_ready, exped, p_turned, p_copied, out_done, out_taken, chain, achain = (
            st.sem(x) for x in names)
        units = [(m, kv, j) for m in range(TT) for kv in range(H_KV) for j in range(GROUP)]
        mod = Modulation(nc, st, weights, "mod1_first", *mod_args, 0, [ps_t[:, i, :] for i in range(2)])

        def keys(m):
            return CTX if m < 2 else TOK

        with nc.Block() as block:
            @block.sync
            def _(sp):
                sp.dma_start(sink_b[:, :], sink.partition_broadcast(P)).then_inc(loaded, 16)
                mod.sync(sp)

            @block.tensor
            def _(pe):
                for m in range(TT):
                    pe.wait_ge(rotated, m + 1)
                    if m:
                        pe.wait_ge(copied, m)
                    for j in range(GROUP):
                        nc.tensor.transpose(ps_t[:, 0, j * P:(j + 1) * P], qr[:, j, :, :].rearrange("p a b -> p (a b)"), ident)
                    nc.tensor.transpose(ps_t[:, 1, 0:P], kr[:, :, :].rearrange("p a b -> p (a b)"), ident).then_inc(turned, 1)
                pe.wait_ge(copied, TT)

                def score(u):
                    m, kv, j = units[u]
                    if u >= 2:
                        pe.wait_ge(masked, u - 1)
                    rows = slice(kv * DH_A, (kv + 1) * DH_A)
                    nc.tensor.matmul(ps_s[:, u % 2, 0:keys(m)], qt[rows, j, m * P:(m + 1) * P], kt[rows, 0:keys(m)],
                                     start=True, stop=True).then_inc(scored, 1)

                def turn(u):
                    pe.wait_ge(exped, u + 1)
                    if u >= 2:
                        pe.wait_ge(p_copied, u - 1)
                    for s in range(keys(units[u][0]) // P):
                        last = nc.tensor.transpose(ps_p[:, u % 2, s * P:(s + 1) * P], p_sb[:, u % 2, s * P:(s + 1) * P], ident)
                    last.then_inc(p_turned, 1)

                score(0)
                score(1)
                turn(0)
                for u, (m, kv, j) in enumerate(units):
                    if u + 2 < len(units):
                        score(u + 2)
                    if u + 1 < len(units):
                        turn(u + 1)
                    mod.tensor(pe, u, len(units))
                    pe.wait_ge(p_copied, u + 1)
                    if u >= 2:
                        pe.wait_ge(out_taken, u - 1)
                    for s in range(keys(m) // P):
                        v = qkv[:, s, A_Q + A_KV + kv * DH_A:A_Q + A_KV + (kv + 1) * DH_A]
                        last = nc.tensor.matmul(ps_o[:, u % 2, 0:DH_A], pt[:, u % 2, s * P:(s + 1) * P], v,
                                                start=(s == 0), stop=(s == keys(m) // P - 1))
                    last.then_inc(out_done, 1)

            @block.scalar
            def _(act):
                link = Link(act, achain)
                for m in range(TT):
                    act.wait_ge(turned, m + 1)
                    link(nc.scalar.activation(qt[:, :, m * P:(m + 1) * P], ps_t[:, 0, :].rearrange("p (j t) -> p j t", t=P), ACT.Copy))
                    nc.scalar.activation(kt[:, m * P:(m + 1) * P], ps_t[:, 1, 0:P], ACT.Copy).then_inc(copied, 1)

                def exponentials(u):
                    m, kv, j = units[u]
                    b, sm, n = u % 2, u % 4, keys(m)
                    act.wait_ge(max_ready, u + 1)
                    if u >= 2:
                        act.wait_ge(p_turned, u - 1)
                    if u >= 4:
                        act.wait_ge(out_taken, u - 3)
                    h = kv * GROUP + j
                    nc.scalar.activation(small[:, sm, 3:4], sink_b[:, h:h + 1], ACT.Exp, bias=small[:, sm, 1:2])
                    nc.scalar.activation(p_sb[:, b, 0:n], s_sb[:, b, 0:n], ACT.Exp, bias=small[:, sm, 1:2], scale=scale,
                                         accum_out=small[:, sm, 2:3]).then_inc(exped, 1)

                exponentials(0)
                for u, (m, kv, j) in enumerate(units):
                    b, n = u % 2, keys(m)
                    if u + 1 < len(units):
                        exponentials(u + 1)
                    act.wait_ge(p_turned, u + 1)
                    if u >= 2:
                        act.wait_ge(out_done, u - 1)
                    nc.scalar.activation(pt[:, b, 0:n], ps_p[:, b, 0:n], ACT.Copy).then_inc(p_copied, 1)

            @block.vector
            def _(dve):
                link = Link(dve, chain)
                for m in range(TT):
                    x = qkv[:, m, 0:heads * DH_A].rearrange("p (h r two) -> p h r two", two=2, r=32)
                    x1, x2 = x[:, :, :, 0], x[:, :, :, 1]
                    c = cos[:, m, :].unsqueeze(1).to_broadcast([P, heads, 32])
                    s = sin[:, m, :].unsqueeze(1).to_broadcast([P, heads, 32])
                    nc.vector.tensor_tensor(t1[:, :, :], x1, c, ALU.mult)
                    nc.vector.tensor_tensor(t2[:, :, :], x2, s, ALU.mult)
                    nc.vector.tensor_tensor(t3[:, :, :], x1, s, ALU.mult)
                    link(nc.vector.tensor_tensor(t4[:, :, :], x2, c, ALU.mult))
                    if m:
                        dve.wait_ge(turned, m)
                    for a, b, op, which in ((t1, t2, ALU.subtract, 0), (t3, t4, ALU.add, 1)):
                        for kv in range(H_KV):
                            hs = slice(kv * GROUP, (kv + 1) * GROUP)
                            o = qr[:, :, kv, :].rearrange("p j (r two) -> p j r two", two=2)[:, :, :, which]
                            nc.vector.tensor_tensor(o, a[:, hs, :], b[:, hs, :], op)
                        o = kr[:, :, :].rearrange("p j (r two) -> p j r two", two=2)[:, :, :, which]
                        link(nc.vector.tensor_tensor(o, a[:, H_A:heads, :], b[:, H_A:heads, :], op))
                    dve.sem_inc(rotated, 1)
                dve.wait_ge(loaded, 16)

                def first(u):
                    m, kv, j = units[u]
                    b, sm, n = u % 2, u % 4, keys(m)
                    h = kv * GROUP + j
                    dve.wait_ge(scored, u + 1)
                    if u >= 2:
                        dve.wait_ge(exped, u - 1)
                    if m < 2:
                        ins = nc.vector.tensor_copy(s_sb[:, b, 0:n], ps_s[:, b, 0:n])
                    else:
                        ins = nc.vector.tensor_tensor(s_sb[:, b, 0:n], ps_s[:, b, 0:n], bars[:, m - 2, :], ALU.add)
                    ins.then_inc(masked, 1)
                    dve.wait_ge(masked, u + 1)
                    link(nc.vector.reduce_max(small[:, sm, 0:1], s_sb[:, b, 0:n], AX_X))
                    link(nc.vector.tensor_scalar(small[:, sm, 0:1], small[:, sm, 0:1], scale, sink_b[:, h:h + 1], ALU.mult, ALU.max))
                    nc.vector.tensor_scalar(small[:, sm, 1:2], small[:, sm, 0:1], -1.0, None, ALU.mult).then_inc(max_ready, 1)

                first(0)
                first(1)
                for u, (m, kv, j) in enumerate(units):
                    if u + 2 < len(units):
                        first(u + 2)
                    mod.vector(dve, u, len(units))
                    b = u % 4
                    h = kv * GROUP + j
                    dve.wait_ge(exped, u + 1)
                    link(nc.vector.tensor_tensor(small[:, b, 4:5], small[:, b, 2:3], small[:, b, 3:4], ALU.add))
                    link(nc.vector.reciprocal(small[:, b, 5:6], small[:, b, 4:5]))
                    dve.wait_ge(out_done, u + 1)
                    nc.vector.tensor_scalar(cat[:, m, M_W + h * DH_A:M_W + (h + 1) * DH_A], ps_o[:, u % 2, 0:DH_A], small[:, b, 5:6], None,
                                            ALU.mult).then_inc(out_taken, 1)
    mod.done()


def stage_head_norm(nc, name, h, tiles, heads, width, norm_w, gate, gate_func, out, eps):
    n = heads * width
    with stage(nc, name) as st:
        rows = st.sb("rows", [P, n])
        sq = st.sb("sq", [P, n])
        ss = st.sb("ss", [P, 4, heads])
        rs = st.sb("rs", [P, 4, heads])
        loaded, chain, ss_ready, rs_ready, gated = (st.sem(x) for x in ("loaded", "chain", "ss_ready", "rs_ready", "gated"))
        with nc.Block() as block:
            @block.scalar
            def _(act):
                act.dma_start(rows[:, :], norm_w.partition_broadcast(P)).then_inc(loaded, 16)
                for i, m in enumerate(tiles):
                    act.wait_ge(ss_ready, i + 1)
                    nc.scalar.activation(rs[:, i, :], ss[:, i, :], ACT.Sqrt).then_inc(rs_ready, 1)
                for i, m in enumerate(tiles):
                    if gate is not None:
                        nc.scalar.activation(gate[:, m, :], gate[:, m, :], gate_func).then_inc(gated, 1)

            @block.vector
            def _(dve):
                link = Link(dve, chain)
                for i, m in enumerate(tiles):
                    for head in range(heads):
                        hs = slice(head * width, (head + 1) * width)
                        last = nc.vector.scalar_tensor_tensor(sq[:, hs], h[:, m, hs], 1.0, h[:, m, hs], ALU.mult, ALU.mult, accum_out=ss[:, i, head:head + 1])
                    link(last)
                    nc.vector.tensor_scalar(ss[:, i, :], ss[:, i, :], 1.0 / width, eps, ALU.mult, ALU.add).then_inc(ss_ready, 1)
                dve.wait_ge(loaded, 16)
                for i, m in enumerate(tiles):
                    dve.wait_ge(rs_ready, i + 1)
                    link(nc.vector.reciprocal(rs[:, i, :], rs[:, i, :]))
                    for head in range(heads):
                        hs = slice(head * width, (head + 1) * width)
                        last = nc.vector.scalar_tensor_tensor(out[:, m, hs], h[:, m, hs], rs[:, i, head:head + 1], rows[:, hs], ALU.mult, ALU.mult)
                    link(last)
                    if gate is None:
                        continue
                    dve.wait_ge(gated, i + 1)
                    link(nc.vector.tensor_tensor(out[:, m, 0:n], out[:, m, 0:n], gate[:, m, 0:n], ALU.mult))


HEADS, TOPK, KEYS = 8, 16, 128
HALVES = 2 * HEADS
PICKS = HEADS * TOPK


def stage_peer(nc, name, h, n_tiles, q_t, k_t, u, v, iota, ident, layer, y, diag, slots, landed, landed0):
    USES = TOPK + TOPK // 2
    ODD = TOPK // 2
    with stage(nc, name) as st:
        more_slots = st.sb("ring", [P, TOPK // 2, D])
        slots = slots.rearrange("p s k n -> p (s k n)").rearrange("p (s d) -> p s d", d=D)

        def row(k, lo=0, hi=D):
            return (slots if k < TOPK // 2 else more_slots)[:, k % (TOPK // 2), lo:hi]

        q_cur = st.sb("q_cur", [P, 2, 2, P])
        k_cur = st.sb("k_cur", [P, 2, 2, P])
        zeros = st.sb("zeros", [P, BANK])
        top = st.sb("top", [P, 2, TOPK])
        idx = st.sb("idx", [P, 2, TOPK], U32)
        idx_f = st.sb("idx_f", [P, 2, TOPK])
        left = st.sb("left", [P, 2, KEYS])
        cand = st.sb("cand", [P, TOPK, TOPK])
        cand2 = st.sb("cand2", [P, TOPK * TOPK])
        best = st.sb("best", [P, TOPK])
        pos = st.sb("pos", [P, TOPK], U32)
        ab = st.sb("ab", [P, 2, TOPK], U32)
        ab_f = st.sb("ab_f", [P, 2, TOPK])
        hot = st.sb("hot", [P, 2, TOPK, TOPK])
        ids = st.sb("ids", [P, 2, TOPK])
        next_picks = st.sb("next_picks", [P, 2, TOPK], U32)
        picks = st.sb("picks", [P, 2, TOPK], U32)
        soft = st.sb("soft", [P, TOPK])
        tot = st.sb("tot", [P, 1])
        share = st.sb("share", [P, 2, TOPK])
        dots = st.sb("dots", [P, 2, TOPK])
        gel = st.sb("gel", [P, 2, TOPK])
        wgt = st.sb("wgt", [P, 2, TOPK])
        hp = st.ps("h", [P, D])
        acc = st.ps("acc", [P, D])
        acc_pe = st.ps("acc_pe", [P, D])
        ps_s = st.ps("scores", [P, 2, 2, KEYS])
        names = ("used_dve used_pe q_ready scored chosen picks_ready passed h_ready gelu_done soft_in soft_out w_ready diag_ready "
                 "zero_ready pe_sum_done pe_sum_taken chain tiles_chain keys_wrapped passed_dve").split()
        (used_dve, used_pe, q_ready, scored, chosen, picks_ready, passed, h_ready, gelu_done, soft_in, soft_out, w_ready, diag_ready,
         zero_ready, pe_sum_done, pe_sum_taken, chain, tiles_chain, keys_wrapped, passed_dve) = (st.sem(n) for n in names)
        steps = n_tiles * HEADS
        q_flat = q_t.rearrange("p m i t -> p (m i t)")
        k_flat = k_t.rearrange("p i n -> p (i n)")

        def run(eng, first, one, before, after):
            for s in range(2):
                first(s, s)
            for t in range(n_tiles):
                before(t)
                pairs = HEADS // 2 - (1 if t == n_tiles - 1 else 0)
                with eng.Fori(0, pairs) as g:
                    for half in range(2):
                        one(g * 2 + (t * HEADS + half), half, g * 2 + half, True, t)
                if t == n_tiles - 1:
                    for half in range(2):
                        one(steps - 2 + half, half, HEADS - 2 + half, False, t)
                after(t)

        nothing = lambda *_: None
        with nc.Block() as block:
            @block.gpsimd
            def _(pool):
                def one(step, half, head, more, t):
                    pool.wait_ge(chosen, step + 1)
                    pool.sem_inc(passed, 1)
                    nc.gpsimd.tensor_copy(picks[:, half, :], next_picks[:, half, :]).then_inc(picks_ready, 1)
                    pool.wait_ge(picks_ready, step + 1)
                    pool.sem_inc(passed, 1)
                    for k in range(TOPK):
                        if k % 2 == 0:
                            pool.wait_ge(used_dve, step * USES + (TOPK + k // 2 + 1))
                        else:
                            pool.wait_ge(used_pe, step * ODD + (k // 2 + 1))
                        pool.sem_inc(passed, 1)
                        pool.indirect_dma_start(row(k), None, u, bass.IndirectOffsetOnAxis(ap=picks[:, half, k:k + 1], axis=0)).then_inc(landed[k], 16)
                    for k in range(TOPK):
                        pool.wait_ge(used_dve, step * USES + (USES + k + 1))
                        pool.sem_inc(passed, 1)
                        pool.indirect_dma_start(row(k), None, v, bass.IndirectOffsetOnAxis(ap=picks[:, half, k:k + 1], axis=0)).then_inc(landed[k], 16)
                run(pool, nothing, one, nothing, nothing)

            @block.scalar
            def _(act):
                def queries(step, half, head):
                    nc.scalar.activation(q_cur[:, half, :, :].rearrange("p i t -> p (i t)"), q_flat[:, ds(step * 2 * P, 2 * P)], ACT.Copy)
                    nc.scalar.activation(k_cur[:, half, :, :].rearrange("p i t -> p (i t)"), k_flat[:, ds(head * 2 * P, 2 * P)], ACT.Copy).then_inc(q_ready, 1)

                def exps(step):
                    act.wait_ge(soft_in, step + 1)
                    nc.scalar.activation(soft[:, :], soft[:, :], ACT.Exp).then_inc(soft_out, 1)

                def first(step, half):
                    if step == 0:
                        nc.scalar.activation(k_t[:, HALVES:HALVES + 4, :], k_t[:, 0:4, :], ACT.Copy).then_inc(keys_wrapped, 1)
                        act.wait_ge(keys_wrapped, 1)
                    queries(step, half, step)
                    exps(step)

                def before(t):
                    if t:
                        act.wait_ge(used_dve, t * HEADS * USES + TOPK)
                    nc.scalar.activation(hp[:, :], h[:, t, :], ACT.Copy).then_inc(h_ready, 1)

                def one(step, half, head, more, t):
                    if more:
                        act.wait_ge(scored, step + 1)
                        queries(step + 2, half, head + 2)
                    act.wait_ge(used_dve, step * USES + (USES + TOPK))
                    nc.scalar.activation(gel[:, half, :], dots[:, half, :], ACT.Gelu).then_inc(gelu_done, 1)
                    if more:
                        exps(step + 2)
                    act.wait_ge(w_ready, step + 1)
                    for i in range(ODD):
                        last = nc.scalar.activation(diag[:, half * ODD + i, :], ident, ACT.Copy, scale=wgt[:, half, 2 * i + 1:2 * i + 2])
                    last.then_inc(diag_ready, 1)

                def after(t):
                    act.wait_ge(pe_sum_done, t + 1)
                    nc.scalar.activation(y[:, t, :], acc_pe[:, :], ACT.Copy).then_inc(pe_sum_taken, 1)
                run(act, first, one, before, after)

            @block.tensor
            def _(pe):
                def score(step, half):
                    pe.wait_ge(q_ready, step + 1)
                    for i in range(2):
                        last = nc.tensor.matmul(ps_s[:, half, i, :], q_cur[:, half, i, :], k_cur[:, half, i, :], start=True, stop=True)
                    last.then_inc(scored, 1)

                def before(t):
                    if t == 0:
                        pe.wait_ge(zero_ready, 1)
                    else:
                        pe.wait_ge(pe_sum_taken, t)
                    for c in range(2):
                        nc.tensor.matmul(acc_pe[:, c * BANK:(c + 1) * BANK], zeros[:, 0:P], zeros[:, :], start=True, stop=False)

                def one(step, half, head, more, t):
                    if more:
                        pe.wait_ge(chosen, step + 1)
                        score(step + 2, half)
                    pe.wait_ge(diag_ready, step + 1)
                    for i in range(ODD):
                        k = 2 * i + 1
                        pe.wait_ge(landed[k], step * 32 + (landed0 + 32))
                        for c in range(2):
                            last = nc.tensor.matmul(acc_pe[:, c * BANK:(c + 1) * BANK], diag[:, half * ODD + i, :], row(k, c * BANK, (c + 1) * BANK),
                                                    start=False, stop=False)
                        last.then_inc(used_pe, 1)

                def after(t):
                    for c in range(2):
                        last = nc.tensor.matmul(acc_pe[:, c * BANK:(c + 1) * BANK], zeros[:, 0:P], zeros[:, :], start=False, stop=True)
                    last.then_inc(pe_sum_done, 1)
                pe.sem_inc(used_pe, ODD)
                run(pe, score, one, before, after)

            @block.vector
            def _(dve):
                per_pick, per_share = 15, 3

                def pick(step, half, link):
                    dve.wait_ge(scored, step + 1)
                    dve.sem_inc(passed_dve, 1)

                    def top16(groups, src, rest, out, where):
                        for i in range(groups):
                            last = nc.vector.max(out(i)[:, 0:8], src(i))
                        link(last)
                        dve.sem_inc(passed_dve, 1)
                        for i in range(groups):
                            nc.vector.max_index(where(i)[:, 0:8], out(i)[:, 0:8], src(i))
                            last = nc.vector.match_replace(rest(i), out(i)[:, 0:8], src(i), -BIG)
                        link(last)
                        dve.sem_inc(passed_dve, 1)
                        for i in range(groups):
                            last = nc.vector.max(out(i)[:, 8:16], rest(i))
                        link(last)
                        dve.sem_inc(passed_dve, 1)
                        for i in range(groups):
                            last = nc.vector.max_index(where(i)[:, 8:16], out(i)[:, 8:16], rest(i))
                        link(last)
                        dve.sem_inc(passed_dve, 1)

                    top16(2, lambda i: ps_s[:, half, i, :], lambda i: left[:, i, :], lambda i: top[:, i, :], lambda i: idx[:, i, :])
                    nc.vector.tensor_copy(idx_f[:, :, :], idx[:, :, :])
                    link(nc.vector.tensor_tensor(cand[:, :, :], top[:, 0, :].unsqueeze(2).to_broadcast([P, TOPK, TOPK]),
                                                 top[:, 1, :].unsqueeze(1).to_broadcast([P, TOPK, TOPK]), ALU.add))
                    dve.sem_inc(passed_dve, 1)
                    top16(1, lambda i: cand[:, :, :].rearrange("p a b -> p (a b)"), lambda i: cand2[:, :], lambda i: best[:, :], lambda i: pos[:, :])
                    nc.vector.tensor_scalar(ab[:, 0, :], pos[:, :], 4, None, ALU.logical_shift_right)
                    nc.vector.tensor_scalar(soft[:, :], best[:, :], best[:, 0:1], None, ALU.subtract).then_inc(soft_in, 1)
                    link(nc.vector.tensor_scalar(ab[:, 1, :], pos[:, :], TOPK - 1, None, ALU.bitwise_and))
                    link(nc.vector.tensor_copy(ab_f[:, :, :], ab[:, :, :]))
                    link(nc.vector.tensor_tensor(hot[:, :, :, :], ab_f[:, :, :].unsqueeze(3).to_broadcast([P, 2, TOPK, TOPK]),
                                                 iota.unsqueeze(1).unsqueeze(1).to_broadcast([P, 2, TOPK, TOPK]), ALU.is_equal))
                    link(nc.vector.tensor_tensor(hot[:, :, :, :], hot[:, :, :, :], idx_f[:, :, :].unsqueeze(2).to_broadcast([P, 2, TOPK, TOPK]), ALU.mult))
                    link(nc.vector.reduce_sum(ids[:, :, :], hot[:, :, :, :], AX_X))
                    link(nc.vector.scalar_tensor_tensor(ids[:, 0, :], ids[:, 0, :], float(KEYS), ids[:, 1, :], ALU.mult, ALU.add))
                    nc.vector.tensor_scalar(next_picks[:, half, :], ids[:, 0, :], float(layer * N_EXPERTS), None, ALU.add).then_inc(chosen, 1)

                def shares(step, half, link):
                    dve.wait_ge(soft_out, step + 1)
                    link(nc.vector.reduce_sum(tot[:, :], soft[:, :], AX_X))
                    link(nc.vector.reciprocal(tot[:, :], tot[:, :]))
                    link(nc.vector.tensor_scalar(share[:, half, :], soft[:, :], tot[:, 0:1], None, ALU.mult))

                def first(step, half):
                    link = Link(dve, chain, step * (per_pick + per_share))
                    pick(step, half, link)
                    shares(step, half, link)
                    assert link.n == (step + 1) * (per_pick + per_share), link.n

                tiles_link = Link(dve, tiles_chain)

                def before(t):
                    dve.wait_ge(h_ready, t + 1)
                    tiles_link(nc.vector.memset(acc[:, :], 0.0))

                def one(step, half, head, more, t):
                    for k in range(TOPK):
                        dve.wait_ge(landed[k], step * 32 + (landed0 + 16))
                        nc.vector.scalar_tensor_tensor(row(k), row(k), 1.0, hp[:, :], ALU.mult, ALU.mult,
                                                       accum_out=dots[:, half, k:k + 1]).then_inc(used_dve, 1)
                    link = Link(dve, chain, (step + 2) * (per_pick + per_share))
                    if more:
                        pick(step + 2, half, link)
                    dve.wait_ge(gelu_done, step + 1)
                    nc.vector.tensor_tensor(wgt[:, half, :], gel[:, half, :], share[:, half, :], ALU.mult).then_inc(w_ready, 1)
                    dve.wait_ge(w_ready, step + 1)
                    for i in range(TOPK // 2):
                        dve.wait_ge(landed[2 * i], step * 32 + (landed0 + 32))
                        dve.wait_ge(used_dve, step * USES + (USES + TOPK + i))
                        nc.vector.scalar_tensor_tensor(acc[:, :], row(2 * i), wgt[:, half, 2 * i:2 * i + 1], acc[:, :],
                                                       ALU.mult, ALU.add).then_inc(used_dve, 1)
                    if more:
                        shares(step + 2, half, link)

                def after(t):
                    dve.wait_ge(used_dve, (t + 1) * HEADS * USES + USES)
                    dve.wait_ge(pe_sum_taken, t + 1)
                    tiles_link(nc.vector.tensor_tensor(y[:, t, :], y[:, t, :], acc[:, :], ALU.add))
                nc.vector.memset(zeros[:, :], 0.0).then_inc(zero_ready, 1)
                dve.sem_inc(used_dve, USES)
                run(dve, first, one, before, after)


H_C, DV_C, RANK = 4, 256, 16
SUB = 32
NSUB = P // SUB
FAR_CAP = 80.0


def stage_gla(nc, low_w, gate_up, gate_b, act_t, q_t, k_t, v, sees, ident, x_all, tmp_all, h_out, weights, mod_args):
    order = [[0, 1, 2, 3], [1, 0, 3, 2]]
    units = [(h, d) for h in range(H_C) for d in range(2)]
    n_units = len(units)
    half = n_units // 2
    with stage(nc, "gla") as st:
        wl = st.sb("w_low", [P, KC, 2 * RANK])
        up = st.sb("up", [RANK, 2, H_C * P])
        bias = st.sb("bias", [P, 2, H_C])
        low = st.sb("low", [RANK, 2, TOK])
        ones = st.sb("ones", [P, P])
        cum = st.sb("cum", [P, 3, TT, P])
        kd = st.sb("kd", [P, 2, TT, P])
        ecum = st.sb("ecum", [P, 3, 2, P])
        etot = st.sb("etot", [P, 3, TT])
        ks = st.sb("ks", [P, 2, 2, NSUB, P])
        qs = st.sb("qs", [P, 2, 2, NSUB, SUB])
        kd_tok = st.sb("kd_tok", [P, TT, P])
        sc = st.sb("sc", [P, 2, 2, P])
        state = st.sb("state", [P, 2, DV_C])
        ps_l = st.ps("logits", [P, 2, BANK])
        ps_k = st.ps("kd_turn", [P, TT, P])
        ps_v = st.ps("kv", [P, 4, DV_C])
        ps_o = st.ps("out", [P, 2, DV_C])
        ps_mod = st.ps("mod", [P, BANK])
        mod = Modulation(nc, st, weights, "mod1_rest", *mod_args, 2 * D, [ps_mod[:, :]])
        names = ("loaded low_done low_ready logit_done x_taken ln_ready cum_ready args_ready kd_exp sub_exp "
                 "kd_ready qk_ready kd_turned kd_copied scored sc_ready kv_done state_ready out_done out_taken chain achain").split()
        (loaded, low_done, low_ready, logit_done, x_taken, ln_ready, cum_ready, args_ready, kd_exp, sub_exp,
         kd_ready, qk_ready, kd_turned, kd_copied, scored, sc_ready, kv_done, state_ready, out_done, out_taken, chain, achain) = (
            st.sem(n) for n in names)
        with nc.Block() as block:
            @block.sync
            def _(sp):
                sp.dma_start(wl[:, :, :], low_w.rearrange("(k p) n -> p k n", p=P)).then_inc(loaded, 16)
                sp.dma_start(up[:, :, :], gate_up.rearrange("d r n -> r d n")).then_inc(loaded, 16)
                for d in range(2):
                    sp.dma_start(bias[:, d, :], gate_b[d].rearrange("(h p) -> p h", p=P), allow_slow_non_contiguous=True).then_inc(loaded, 16)
                mod.sync(sp)

            @block.tensor
            def _(pe):
                pe.wait_ge(loaded, 64)
                for d in range(2):
                    for k in range(KC):
                        last = nc.tensor.matmul(ps_l[0:RANK, d, :], wl[:, k, d * RANK:(d + 1) * RANK], act_t[:, k, 0:TOK],
                                                start=(k == 0), stop=(k == KC - 1))
                    last.then_inc(low_done, 1)
                pe.wait_ge(low_ready, 2)
                for u, (h, d) in enumerate(units):
                    if u >= 2:
                        pe.wait_ge(x_taken, u - 1)
                    nc.tensor.matmul(ps_l[:, u % 2, :], up[:, d, h * P:(h + 1) * P], low[:, d, :], start=True, stop=True).then_inc(logit_done, 1)
                pe.wait_ge(x_taken, n_units)

                def turn_and_score(u):
                    pe.wait_ge(kd_ready, u + 1)
                    if u:
                        pe.wait_ge(kd_copied, u)
                    for c in range(TT):
                        last = nc.tensor.transpose(ps_k[:, c, :], kd[:, u % 2, c, :], ident)
                    last.then_inc(kd_turned, 1)
                    pe.wait_ge(qk_ready, u + 1)
                    if u >= 2:
                        pe.wait_ge(sc_ready, u - 1)
                    for c in range(2):
                        for j in range(NSUB):
                            last = nc.tensor.matmul(ps_l[:, u % 2, c * P + j * SUB:c * P + (j + 1) * SUB], ks[:, u % 2, c, j, :], qs[:, u % 2, c, j, :],
                                                    start=True, stop=True)
                    last.then_inc(scored, 1)

                def keys_values(u):
                    h, d = units[u]
                    pe.wait_ge(kd_copied, u + 1)
                    if u:
                        pe.wait_ge(state_ready, u)
                    for i in range(3):
                        c = order[d][i]
                        last = nc.tensor.matmul(ps_v[:, i, :], kd_tok[:, c, :], v[:, c, h * DV_C:(h + 1) * DV_C], start=True, stop=True)
                    last.then_inc(kv_done, 1)

                turn_and_score(0)
                keys_values(0)
                for u, (h, d) in enumerate(units):
                    if u + 1 < n_units:
                        turn_and_score(u + 1)
                    mod.tensor(pe, u, n_units)
                    pe.wait_ge(sc_ready, u + 1)
                    pe.wait_ge(state_ready, u + 1)
                    if u:
                        pe.wait_ge(out_taken, u)
                    for i in range(2):
                        c = order[d][2 + i]
                        nc.tensor.matmul(ps_o[:, c - 2, :], ecum[:, u % 3, c - 2, :], state[:, i, :], start=True, stop=False)
                        last = nc.tensor.matmul(ps_o[:, c - 2, :], sc[:, d, c - 2, :], v[:, c, h * DV_C:(h + 1) * DV_C], start=False, stop=True)
                    last.then_inc(out_done, 1)
                    if u + 1 < n_units:
                        keys_values(u + 1)

            @block.scalar
            def _(act):
                link = Link(act, achain)
                for d in range(2):
                    act.wait_ge(low_done, d + 1)
                    nc.scalar.activation(low[:, d, :], ps_l[0:RANK, d, :], ACT.Copy).then_inc(low_ready, 1)
                for u, (h, d) in enumerate(units):
                    act.wait_ge(logit_done, u + 1)
                    nc.scalar.activation(x_all[:, u, :], ps_l[:, u % 2, :], ACT.Identity, bias=bias[:, d, h:h + 1])
                    nc.scalar.activation(tmp_all[:, u, :], ps_l[:, u % 2, :], ACT.Abs, bias=bias[:, d, h:h + 1]).then_inc(x_taken, 1)
                act.wait_ge(x_taken, n_units)
                for i in range(2):
                    t = tmp_all[:, i * half:(i + 1) * half, :]
                    link(nc.scalar.activation(t, t, ACT.Exp, scale=-1.0))
                for i in range(2):
                    t = tmp_all[:, i * half:(i + 1) * half, :]
                    nc.scalar.activation(t, t, ACT.Ln, bias=1.0).then_inc(ln_ready, 1)

                def exponentials(u):
                    b, b3 = u % 2, u % 3
                    end = P - 1 if units[u][1] == 0 else 0
                    act.wait_ge(args_ready, u + 1)
                    if u >= 3:
                        act.wait_ge(out_done, u - 2)
                    nc.scalar.activation(kd[:, b, :, :], kd[:, b, :, :], ACT.Exp, scale=1.0 / 16.0)
                    nc.scalar.activation(etot[:, b3, :], cum[:, b3, :, end], ACT.Exp, scale=1.0 / 16.0).then_inc(kd_exp, 1)
                    nc.scalar.activation(ks[:, b, :, :, :], ks[:, b, :, :, :], ACT.Exp, scale=1.0 / 16.0)
                    nc.scalar.activation(qs[:, b, :, :, :], qs[:, b, :, :, :], ACT.Exp, scale=1.0 / 16.0)
                    nc.scalar.activation(ecum[:, b3, :, :], cum[:, b3, 2:4, :], ACT.Exp, scale=1.0 / 16.0).then_inc(sub_exp, 1)

                def copy_keys(u):
                    act.wait_ge(kd_turned, u + 1)
                    if u:
                        act.wait_ge(kv_done, u)
                    nc.scalar.activation(kd_tok[:, :, :], ps_k[:, :, :], ACT.Copy).then_inc(kd_copied, 1)

                exponentials(0)
                exponentials(1)
                copy_keys(0)
                for u in range(n_units - 1):
                    copy_keys(u + 1)
                    if u + 2 < n_units:
                        exponentials(u + 2)

            @block.vector
            def _(dve):
                link = Link(dve, chain)
                link(nc.vector.memset(ones[:, :], 1.0))
                link(nc.vector.memset(sc[:, :, :, :].rearrange("p a b c -> p (a b c)"), 0.0))

                def exponents(u):
                    d, b, b3 = units[u][1], u % 2, u % 3
                    end = P - 1 if d == 0 else 0
                    if u >= 2:
                        dve.wait_ge(scored, u - 1)
                    if u % half == 0:
                        dve.wait_ge(ln_ready, u // half + 1)
                        xs = x_all[:, u:u + half, :]
                        link(nc.vector.scalar_tensor_tensor(xs, xs, 0.0, tmp_all[:, u:u + half, :], ALU.min, ALU.subtract))
                    for c in range(TT):
                        a, o = x_all[:, u, c * P:(c + 1) * P], cum[:, b3, c, :]
                        if d:
                            a, o = a[:, ::-1], o[:, ::-1]
                        last = nc.vector.tensor_tensor_scan(o, ones[:, :], a, 0.0, ALU.mult, ALU.add)
                    last.then_inc(cum_ready, 1)
                    dve.wait_ge(cum_ready, u + 1)
                    nc.vector.tensor_tensor(kd[:, b, :, :], cum[:, b3, :, end:end + 1].to_broadcast([P, TT, P]), cum[:, b3, :, :], ALU.subtract)
                    for c in range(2):
                        cu = cum[:, b3, 2 + c, :]
                        ref = cu.rearrange("p (j s) -> p j s", s=SUB)[:, :, SUB // 2:SUB // 2 + 1]
                        nc.vector.tensor_tensor(ks[:, b, c, :, :], ref.to_broadcast([P, NSUB, P]), cu.unsqueeze(1).to_broadcast([P, NSUB, P]), ALU.subtract)
                        last = nc.vector.tensor_tensor(qs[:, b, c, :, :], cu.rearrange("p (j s) -> p j s", s=SUB), ref.to_broadcast([P, NSUB, SUB]), ALU.subtract)
                    link(last)
                    nc.vector.tensor_scalar(ks[:, b, :, :, :], ks[:, b, :, :, :], 16.0 * FAR_CAP, None, ALU.min)
                    nc.vector.tensor_scalar(qs[:, b, :, :, :], qs[:, b, :, :, :], 16.0 * FAR_CAP, None, ALU.min).then_inc(args_ready, 1)

                def products(u):
                    h, b = units[u][0], u % 2
                    dve.wait_ge(kd_exp, u + 1)
                    nc.vector.tensor_tensor(kd[:, b, :, :], kd[:, b, :, :], k_t[:, h, :].rearrange("p (c s) -> p c s", s=P), ALU.mult).then_inc(kd_ready, 1)
                    dve.wait_ge(sub_exp, u + 1)
                    for c in range(2):
                        kk = k_t[:, h, (2 + c) * P:(3 + c) * P]
                        qq = q_t[:, h, c * P:(c + 1) * P]
                        q_sub = qs[:, b, c, :, :].rearrange("p j s -> p (j s)")
                        nc.vector.tensor_tensor(ks[:, b, c, :, :], ks[:, b, c, :, :], kk.unsqueeze(1).to_broadcast([P, NSUB, P]), ALU.mult)
                        nc.vector.scalar_tensor_tensor(q_sub, q_sub, float(P) ** -0.5, qq, ALU.mult, ALU.mult)
                        last = nc.vector.scalar_tensor_tensor(ecum[:, u % 3, c, :], ecum[:, u % 3, c, :], float(P) ** -0.5, qq, ALU.mult, ALU.mult)
                    last.then_inc(qk_ready, 1)

                def take_scores(u):
                    d = units[u][1]
                    dve.wait_ge(scored, u + 1)
                    for c in range(2):
                        last = nc.vector.copy_predicated(sc[:, d, c, :], sees[:, d, :].bitcast(U32), ps_l[:, u % 2, c * P:(c + 1) * P])
                    last.then_inc(sc_ready, 1)
                    dve.wait_ge(kv_done, u + 1)
                    et = etot[:, u % 3, :]
                    link(nc.vector.tensor_copy(state[:, 0, :], ps_v[:, 0, :]))
                    link(nc.vector.scalar_tensor_tensor(state[:, 0, :], state[:, 0, :], et[:, order[d][1]:order[d][1] + 1], ps_v[:, 1, :],
                                                        ALU.mult, ALU.add))
                    nc.vector.scalar_tensor_tensor(state[:, 1, :], state[:, 0, :], et[:, order[d][2]:order[d][2] + 1], ps_v[:, 2, :],
                                                   ALU.mult, ALU.add).then_inc(state_ready, 1)

                def take_results(u):
                    h, d = units[u]
                    dve.wait_ge(out_done, u + 1)
                    if u:
                        dve.wait_ge(out_taken, u)
                    for c in range(2):
                        o = h_out[:, c, h * DV_C:(h + 1) * DV_C]
                        if d == 0:
                            last = nc.vector.tensor_copy(o, ps_o[:, c, :])
                        else:
                            last = nc.vector.tensor_tensor(o, ps_o[:, c, :], o, ALU.add)
                    last.then_inc(out_taken, 1)

                exponents(0)
                exponents(1)
                products(0)
                for u in range(n_units):
                    if u + 1 < n_units:
                        products(u + 1)
                    if u + 2 < n_units:
                        exponents(u + 2)
                    if u:
                        take_results(u - 1)
                    take_scores(u)
                    mod.vector(dve, u, n_units)
                take_results(n_units - 1)
    mod.done()


LT = SEQ // P
GROUPS = 8
S_HEADS, S_DIM, S_GROUPS = 16, 64, 4


def norm_parts(st, x, off, w, b, eps):
    rows = st.sb("ln_rows", [P, 2, D])
    stats = st.sb("ln_stats", [P, 2, 6])
    agg = st.sb("ln_agg", [P, LT, 2])
    std = st.sb("ln_std", [P, LT])
    loaded, chain, var_ready, std_ready, normed = (st.sem(f"ln_{n}") for n in ("loaded", "chain", "var_ready", "std_ready", "normed"))

    def sync(sp):
        sp.dma_start(rows[:, 0, :], w.partition_broadcast(P)).then_inc(loaded, 16)
        sp.dma_start(rows[:, 1, :], b.partition_broadcast(P)).then_inc(loaded, 16)

    def vector(dve):
        link = Link(dve, chain)
        for i in range(LT):
            for j in range(2):
                link(st.nc.vector.bn_stats(stats[:, j, :], x[:, i, off + j * BANK:off + (j + 1) * BANK]))
            link(st.nc.vector.bn_aggr(agg[:, i, :], stats[:, :, :].rearrange("p a b -> p (a b)")))
            st.nc.vector.tensor_scalar(agg[:, i, 1:2], agg[:, i, 1:2], eps, None, ALU.add).then_inc(var_ready, 1)
        dve.wait_ge(loaded, 32)
        for i in range(LT):
            t = x[:, i, off:off + D]
            dve.wait_ge(std_ready, i + 1)
            link(st.nc.vector.reciprocal(std[:, i:i + 1], std[:, i:i + 1]))
            link(st.nc.vector.tensor_scalar(t, t, agg[:, i, 0:1], std[:, i:i + 1], ALU.subtract, ALU.mult))
            link(st.nc.vector.tensor_tensor(t, t, rows[:, 0, :], ALU.mult))
            st.nc.vector.tensor_tensor(t, t, rows[:, 1, :], ALU.add).then_inc(normed, 1)

    def scalar(act):
        for i in range(LT):
            act.wait_ge(var_ready, i + 1)
            st.nc.scalar.activation(std[:, i:i + 1], agg[:, i, 1:2], ACT.Sqrt).then_inc(std_ready, 1)
    return {"sync": sync, "vector": vector, "scalar": scalar}, normed


def gmlp_parts(nc, st, uv, ln_w, ln_b, w_s, b_s, ident, keep, ya, ya_t):
    w = st.sb("w_s", [P, 1, GROUPS * P])
    wt = st.sb("w_s_t", [P, GROUPS, P])
    b = st.sb("b_s", [P, GROUPS])
    loaded, turned, masked, mixed, read, chain = (st.sem(f"mix_{n}") for n in ("loaded", "turned", "masked", "mixed", "read", "chain"))
    ps = st.ps("mix", [P, GROUPS, P])
    norm, normed = norm_parts(st, uv, D, ln_w, ln_b, EPS2)

    def sync(sp):
        sp.dma_start(w[:, 0, :].rearrange("t (g s) -> t g s", s=P), w_s.rearrange("g t s -> t g s")).then_inc(loaded, 16)
        sp.dma_start(b[:, :], b_s.rearrange("g t -> t g"), allow_slow_non_contiguous=True).then_inc(loaded, 16)

    def turn_w(pe):
        pe.wait_ge(loaded, 32)
        for g in range(GROUPS):
            last = nc.tensor.transpose(ps[:, g, :], w[:, 0, g * P:(g + 1) * P], ident)
        last.then_inc(turned, 1)

    def mask_w(dve):
        dve.wait_ge(turned, 1)
        nc.vector.tensor_tensor(wt[:, :, :], ps[:, :, :], keep.unsqueeze(1).to_broadcast([P, GROUPS, P]), ALU.mult).then_inc(masked, 1)

    def mix(c):
        def tensor(pe):
            pe.wait_ge(masked, 1)
            pe.wait_ge(normed, c + 1)
            if c:
                pe.wait_ge(read, c)
            for g in range(GROUPS):
                last = nc.tensor.matmul(ps[:, g, :], wt[:, g, :], uv[:, c, D + g * P:D + (g + 1) * P], start=True, stop=True)
            last.then_inc(mixed, 1)

        def vector(dve):
            dve.wait_ge(mixed, c + 1)
            o = ya[:, c, :].rearrange("p (g e) -> p g e", e=P)
            nc.vector.tensor_tensor(o, ps[:, :, :], b[:, :].unsqueeze(2).to_broadcast([P, GROUPS, P]), ALU.add).then_inc(read, 1)
            dve.wait_ge(read, c + 1)
            nc.vector.tensor_tensor(ya[:, c, :], ya[:, c, :], uv[:, c, 0:D], ALU.mult).then_inc(chain, 1)
        return {"tensor": tensor, "vector": vector}

    turns, _, _ = turn_parts(nc, st, ident, ya, ya_t, range(LT), KC, ready=lambda pe: pe.wait_ge(chain, LT))
    return [norm, {"sync": sync, "tensor": turn_w, "vector": mask_w}, {}, {}, mix(0), {}, mix(1), {}] + turns


def conv_parts(nc, st, tag, x, tiles, w, b, out, silu):
    taps = 4
    wc = st.sb(f"{tag}_w", [P, taps, tiles])
    bc = st.sb(f"{tag}_b", [P, tiles])
    loaded, chain, silu_done = (st.sem(f"{tag}_{n}") for n in ("loaded", "chain", "silu_done"))

    def sync(sp):
        for k in range(taps):
            sp.dma_start(wc[:, k, :], w[k].rearrange("(c p) -> p c", p=P), allow_slow_non_contiguous=True).then_inc(loaded, 16)
        sp.dma_start(bc[:, :], b.rearrange("(c p) -> p c", p=P), allow_slow_non_contiguous=True).then_inc(loaded, 16)

    def vector(dve):
        dve.wait_ge(loaded, 16 * (taps + 1))
        for c in range(tiles):
            last = nc.vector.tensor_scalar(out[:, c, :], x[:, c, :], wc[:, taps - 1, c:c + 1], bc[:, c:c + 1], ALU.mult, ALU.add)
        last.then_inc(chain, 1)
        for back in range(1, taps):
            dve.wait_ge(chain, back)
            for c in range(tiles):
                o = out[:, c, back:SEQ]
                last = nc.vector.scalar_tensor_tensor(o, x[:, c, 0:SEQ - back], wc[:, taps - 1 - back, c:c + 1], o, ALU.mult, ALU.add)
            last.then_inc(chain, 1)
        dve.wait_ge(chain, taps)

    def scalar(act):
        act.wait_ge(chain, taps)
        nc.scalar.activation(out[:, :, :], out[:, :, :], ACT.Silu).then_inc(silu_done, 1)
    part = {"sync": sync, "vector": vector}
    return ([part, {}, {}, {"scalar": scalar}], silu_done) if silu else ([part], chain)


def lru_parts(nc, st, x, gate, w_r, b_r, w_i, b_i, lam, x_ready):
    wr = st.sb("wr", [P, GROUPS, P])
    wi = st.sb("wi", [P, GROUPS, P])
    cols = st.sb("cols", [P, 6, GROUPS])
    r = st.sb("r", [P, GROUPS, SEQ])
    i_t = st.sb("i", [P, GROUPS, SEQ])
    th = st.sb("th", [P, GROUPS, SEQ])
    den = st.sb("den", [P, GROUPS, SEQ])
    ps = st.ps("gates", [P, 2, 2, SEQ])
    names = "loaded gated emptied ln_ready loga_ready tanh_ready a_ready root_in root_out chain achain".split()
    loaded, gated, emptied, ln_ready, loga_ready, tanh_ready, a_ready, root_in, root_out, chain, achain = (st.sem(n) for n in names)

    def sync(sp):
        sp.dma_start(wr[:, :, :], w_r.rearrange("h i j -> i h j")).then_inc(loaded, 16)
        sp.dma_start(wi[:, :, :], w_i.rearrange("h i j -> i h j")).then_inc(loaded, 16)
        for n, src in enumerate((b_r, b_i, lam)):
            sp.dma_start(cols[:, n, :], src.rearrange("(c p) -> p c", p=P), allow_slow_non_contiguous=True).then_inc(loaded, 16)

    def decay(act):
        link = Link(act, achain)
        act.wait_ge(loaded, 80)
        link(nc.scalar.activation(cols[:, 3, :], cols[:, 2, :], ACT.Abs))
        link(nc.scalar.activation(cols[:, 3, :], cols[:, 3, :], ACT.Exp, scale=-1.0))
        nc.scalar.activation(cols[:, 3, :], cols[:, 3, :], ACT.Ln, bias=1.0).then_inc(ln_ready, 1)

    def gates(h0):
        def tensor(pe):
            pe.wait_ge(loaded, 80)
            x_ready(pe)
            for h in (h0, h0 + 1):
                if h >= 2:
                    pe.wait_ge(emptied, h - 1)
                nc.tensor.matmul(ps[:, h % 2, 0, :], wr[:, h, :], x[:, h, :], start=True, stop=True)
                nc.tensor.matmul(ps[:, h % 2, 1, :], wi[:, h, :], x[:, h, :], start=True, stop=True).then_inc(gated, 1)

        def scalar(act):
            for h in (h0, h0 + 1):
                act.wait_ge(gated, h + 1)
                nc.scalar.activation(r[:, h, :], ps[:, h % 2, 0, :], ACT.Sigmoid, bias=cols[:, 0, h:h + 1])
                nc.scalar.activation(i_t[:, h, :], ps[:, h % 2, 1, :], ACT.Sigmoid, bias=cols[:, 1, h:h + 1]).then_inc(emptied, 1)
        return {"tensor": tensor, "scalar": scalar}

    def powers(act):
        act.wait_ge(loga_ready, 1)
        nc.scalar.activation(th[:, :, :], r[:, :, :], ACT.Tanh).then_inc(tanh_ready, 1)
        act.wait_ge(tanh_ready, 1)
        nc.scalar.activation(r[:, :, :], r[:, :, :], ACT.Exp).then_inc(a_ready, 1)

    def root(act):
        act.wait_ge(root_in, 1)
        nc.scalar.activation(th[:, :, :], th[:, :, :], ACT.Sqrt).then_inc(root_out, 1)

    def vector(dve):
        link = Link(dve, chain)
        dve.wait_ge(ln_ready, 1)
        link(nc.vector.scalar_tensor_tensor(cols[:, 4, :], cols[:, 2, :], 0.0, cols[:, 3, :], ALU.min, ALU.subtract))
        link(nc.vector.tensor_scalar(cols[:, 4, :], cols[:, 4, :], 8.0, None, ALU.mult))
        dve.wait_ge(emptied, GROUPS)
        for h in range(GROUPS):
            last = nc.vector.tensor_scalar(r[:, h, :], r[:, h, :], cols[:, 4, h:h + 1], None, ALU.mult)
        last.then_inc(loga_ready, 1)
        link(nc.vector.tensor_tensor(i_t[:, :, :], i_t[:, :, :], x[:, :, :], ALU.mult))
        dve.wait_ge(tanh_ready, 1)
        link(nc.vector.tensor_scalar(den[:, :, :], th[:, :, :], -1.0, 1.0, ALU.mult, ALU.add))
        link(nc.vector.reciprocal(den[:, :, :], den[:, :, :]))
        nc.vector.scalar_tensor_tensor(th[:, :, :], th[:, :, :], -2.0, den[:, :, :], ALU.mult, ALU.mult).then_inc(root_in, 1)
        dve.wait_ge(root_out, 1)
        link(nc.vector.tensor_tensor(i_t[:, :, :], i_t[:, :, :], th[:, :, :], ALU.mult))
        dve.wait_ge(a_ready, 1)
        for h in range(GROUPS):
            last = nc.vector.tensor_tensor_scan(den[:, h, :], r[:, h, :], i_t[:, h, :], 0.0, ALU.mult, ALU.add)
        link(last)
        link(nc.vector.tensor_tensor(gate[:, :, :], gate[:, :, :], den[:, :, :], ALU.mult))

    return [{"sync": sync, "scalar": decay}, {}] + [gates(h) for h in range(0, GROUPS, 2)] + [
        {"vector": vector, "scalar": powers}, {}, {"scalar": root}]


def ssd_parts(nc, st, act_t, w_dt, dt_bias, a_log, d_skip, xbc, x_tok, z, ident, sel, far, y, xdt):
    per_group = S_HEADS // S_GROUPS
    wd = st.sb("wd", [P, KC, S_HEADS])
    par = st.sb("par", [S_HEADS, 4])
    dsk = st.sb("dsk", [P, S_HEADS])
    row = st.sb("row", [S_HEADS, 6, SEQ])
    col = st.sb("col", [P, LT, 2, S_HEADS])
    m_far = st.sb("m_far", [P, 2, SEQ])
    e = st.sb("e", [P, 2, LT, SEQ])
    w = st.sb("w", [P, 2, LT, SEQ])
    ps_m = st.ps("cum_bcast", [P, 2, SEQ])
    ps_c = st.ps("cb", [P, LT, SEQ])
    turns, turn_emptied, n_turns = turn_parts(nc, st, ident[:, :], xbc, x_tok, range(KC), LT, banks=1, per_part=4)
    ps_y = st.ps("y", [P, 2, LT, P])
    ps_d = ps_y[:, :, :, :].rearrange("p a b c -> p (a b c)")
    names = ("loaded dt_done dt_sum ln_ready ea_ready cum_ready cols_done xdt_ready crossed sent far_ready e_ready w_ready "
             "mult_done y_taken chain achain").split()
    (loaded, dt_done, dt_sum, ln_ready, ea_ready, cum_ready, cols_done, xdt_ready, crossed, sent, far_ready, e_ready, w_ready,
     mult_done, y_taken, chain, achain) = (st.sem(f"ssd_{n}") for n in names)
    dve_link = Link(nc.vector, chain)

    def sync(sp):
        sp.dma_start(wd[:, :, :], w_dt.rearrange("(k p) n -> p k n", p=P)).then_inc(loaded, 16)
        sp.dma_start(par[:, 0:1], dt_bias.rearrange("(h o) -> h o", o=1)).then_inc(loaded, 16)
        sp.dma_start(par[:, 1:2], a_log.rearrange("(h o) -> h o", o=1)).then_inc(loaded, 16)
        sp.dma_start(dsk[:, :], d_skip.partition_broadcast(P)).then_inc(loaded, 16)

    def dt_tensor(pe):
        pe.wait_ge(loaded, 64)
        for k in range(KC):
            last = nc.tensor.matmul(ps_d[0:S_HEADS, 0:SEQ], wd[:, k, :], act_t[:, k, 0:SEQ], start=(k == 0), stop=(k == KC - 1))
        last.then_inc(dt_done, 1)

    def dt_scalar(act):
        link = Link(act, achain)
        act.wait_ge(loaded, 64)
        act.wait_ge(dt_done, 1)
        nc.scalar.activation(par[:, 2:3], par[:, 1:2], ACT.Exp).then_inc(ea_ready, 1)
        nc.scalar.activation(row[:, 0, :], ps_d[0:S_HEADS, 0:SEQ], ACT.Identity, bias=par[:, 0:1]).then_inc(dt_sum, 1)
        act.wait_ge(dt_sum, 1)
        link(nc.scalar.activation(row[:, 1, :], row[:, 0, :], ACT.Abs))
        link(nc.scalar.activation(row[:, 1, :], row[:, 1, :], ACT.Exp, scale=-1.0))
        nc.scalar.activation(row[:, 1, :], row[:, 1, :], ACT.Ln, bias=1.0).then_inc(ln_ready, 1)

    def dt_vector(dve):
        link = dve_link
        link(nc.vector.memset(row[:, 5, :], 1.0))
        dve.wait_ge(ln_ready, 1)
        link(nc.vector.scalar_tensor_tensor(row[:, 2, :], row[:, 0, :], 0.0, row[:, 1, :], ALU.max, ALU.add))
        dve.wait_ge(ea_ready, 1)
        link(nc.vector.tensor_scalar(row[:, 3, :], row[:, 2, :], par[:, 2:3], -1.0, ALU.mult, ALU.mult))
        nc.vector.tensor_tensor_scan(row[:, 4, :], row[:, 5, :], row[:, 3, :], 0.0, ALU.mult, ALU.add).then_inc(cum_ready, 1)

    def col_tensor(pe):
        pe.wait_ge(cum_ready, 1)
        for c in range(LT):
            for n, r in enumerate((2, 4)):
                at = 256 + (2 * c + n) * S_HEADS
                last = nc.tensor.matmul(ps_d[:, at:at + S_HEADS], row[:, r, c * P:(c + 1) * P], ident[0:S_HEADS, 0:S_HEADS], start=True, stop=True)
        last.then_inc(cols_done, 1)

    def col_vector(dve):
        link = dve_link
        dve.wait_ge(cols_done, 1)
        pc = ps_d[:, 256:256 + 4 * S_HEADS].rearrange("p (c n h) -> p c n h", n=2, h=S_HEADS)
        nc.vector.tensor_copy(col[:, :, 0, :], pc[:, :, 0, :])
        link(nc.vector.tensor_scalar(col[:, :, 1, :], pc[:, :, 1, :], -1.0, None, ALU.mult))
        dve.wait_ge(turn_emptied, n_turns)
        for c in range(LT):
            xv = x_tok[:, c, :].rearrange("p (h e) -> p h e", e=S_DIM)
            last = nc.vector.tensor_tensor(xdt[:, c, :].rearrange("p (h e) -> p h e", e=S_DIM), xv,
                                           col[:, c, 0, :].unsqueeze(2).to_broadcast([P, S_HEADS, S_DIM]), ALU.mult)
        last.then_inc(xdt_ready, 1)

    def send(pe, h):
        g = h // per_group
        if h % per_group == 0:
            if h:
                pe.wait_ge(w_ready, h)
            for s in range(LT):
                last = nc.tensor.matmul(ps_c[:, s, :], xbc[:, 8 + g, s * P:(s + 1) * P], xbc[:, 12 + g, :], start=True, stop=True)
            last.then_inc(crossed, 1)
        if h >= 2:
            pe.wait_ge(e_ready, h // 2 * 2)
            pe.wait_ge(far_ready, h // 2 * 2)
        nc.tensor.matmul(ps_m[:, h % 2, :], sel[0:S_HEADS, h, :], row[:, 4, :], start=True, stop=True).then_inc(sent, 1)

    def multiply(pe, h):
        pe.wait_ge(w_ready, h + 1)
        if h >= 2:
            pe.wait_ge(y_taken, h // 2 * 2)
        for t in range(LT):
            for s in range(t + 1):
                last = nc.tensor.matmul(ps_y[:, h % 2, t, 0:S_DIM], w[:, h % 2, s, t * P:(t + 1) * P],
                                        xdt[:, s, h * S_DIM:(h + 1) * S_DIM], start=(s == 0), stop=(s == t))
        last.then_inc(mult_done, 1)

    def head_scalar(act, h):
        b = h % 2
        act.wait_ge(sent, h // 2 * 2 + 2)
        act.wait_ge(far_ready, h // 2 * 2 + 2)
        if h >= 2:
            act.wait_ge(w_ready, h - 1)
        for s in range(LT):
            nc.scalar.activation(e[:, b, s, s * P:(s + 1) * P], m_far[:, b, s * P:(s + 1) * P], ACT.Exp, bias=col[:, s, 1, h:h + 1])
        nc.scalar.activation(e[:, b, 0, P:SEQ], ps_m[:, b, P:SEQ], ACT.Exp, bias=col[:, 0, 1, h:h + 1]).then_inc(e_ready, 1)

    def head_far(dve, h):
        dve.wait_ge(sent, h // 2 * 2 + 2)
        if h >= 2:
            dve.wait_ge(e_ready, h - 1)
        nc.vector.tensor_tensor(m_far[:, h % 2, :], ps_m[:, h % 2, :], far[:, 0, 0:SEQ], ALU.subtract).then_inc(far_ready, 1)

    def head_weights(dve, h):
        b = h % 2
        dve.wait_ge(e_ready, h + 1)
        dve.wait_ge(crossed, h // per_group + 1)
        if h >= 2:
            dve.wait_ge(mult_done, h - 1)
        nc.vector.tensor_tensor(w[:, b, 0, :], ps_c[:, 0, :], e[:, b, 0, :], ALU.mult)
        nc.vector.tensor_tensor(w[:, b, 1, P:SEQ], ps_c[:, 1, P:SEQ], e[:, b, 1, P:SEQ], ALU.mult).then_inc(w_ready, 1)

    def head_take(dve, h):
        dve.wait_ge(mult_done, h // 2 * 2 + 2)
        hs = slice(h * S_DIM, (h + 1) * S_DIM)
        nc.vector.scalar_tensor_tensor(y[:, :, hs], x_tok[:, :, hs], dsk[:, h:h + 1], ps_y[:, h % 2, :, 0:S_DIM], ALU.mult, ALU.add).then_inc(y_taken, 1)

    def pair(j):
        hs = [h for h in (2 * j, 2 * j + 1) if h < S_HEADS]
        before = [h for h in (2 * j - 2, 2 * j - 1) if h >= 0]

        def tensor(pe):
            if j == 0:
                pe.wait_ge(xdt_ready, 1)
            for h in before:
                multiply(pe, h)
            for h in hs:
                send(pe, h)

        def scalar(act):
            if j == 0:
                act.wait_ge(xdt_ready, 1)
            for h in hs:
                head_scalar(act, h)

        def vector(dve):
            for h in hs:
                head_far(dve, h)
            for h in before:
                head_take(dve, h)
            for h in hs:
                head_weights(dve, h)
            if not hs:
                dve.wait_ge(y_taken, S_HEADS)
                dve_link(nc.vector.tensor_tensor(y[:, :, :], y[:, :, :], z[:, :, :], ALU.mult))
        return {"tensor": tensor, "scalar": scalar, "vector": vector}

    return [{"sync": sync, "tensor": dt_tensor, "scalar": dt_scalar, "vector": dt_vector}] + turns + [
        {"tensor": col_tensor, "vector": col_vector}] + [pair(j) for j in range(S_HEADS // 2 + 1)]


def gate_parts(nc, st, g, b_gate, branches, out):
    rows = st.sb("gate_rows", [P, 3, D])
    loaded, biased, gated, chain = (st.sem(f"gate_{n}") for n in ("loaded", "biased", "gated", "chain"))
    link = Link(nc.vector, chain)
    order = [(c, i) for i in range(3) for c in range(LT)]

    def logits(c, i):
        return g[:, c, i * D:(i + 1) * D]

    def sync(sp):
        for i in range(3):
            sp.dma_start(rows[:, i, :], b_gate[i].partition_broadcast(P)).then_inc(loaded, 16)

    def bias(dve):
        dve.wait_ge(loaded, 48)
        for c, i in order:
            nc.vector.tensor_tensor(logits(c, i), logits(c, i), rows[:, i, :], ALU.add).then_inc(biased, 1)

    def sigmoid(act):
        for n, (c, i) in enumerate(order):
            act.wait_ge(biased, n + 1)
            nc.scalar.activation(logits(c, i), logits(c, i), ACT.Sigmoid).then_inc(gated, 1)

    def products(dve):
        for n, (c, i) in enumerate(order[:2 * LT]):
            dve.wait_ge(gated, n + 1)
            if i == 0:
                link(nc.vector.tensor_tensor(out[:, c, :], logits(c, i), branches[i][:, c, :], ALU.mult))
            else:
                link(nc.vector.tensor_tensor(logits(c, i), logits(c, i), branches[i][:, c, :], ALU.mult))
                link(nc.vector.tensor_tensor(out[:, c, :], out[:, c, :], logits(c, i), ALU.add))

    return [{"sync": sync, "vector": bias, "scalar": sigmoid}, {"vector": products}]


def stage_rms(nc, name, x, g, out, ident, added=None, out_t=None, stored=None, loads=()):
    with stage(nc, name) as st:
        sq = st.sb("sq", [P, D])
        ss = st.sb("ss", [P, LT])
        rs = st.sb("rs", [P, LT])
        loaded, chain, ss_ready, rs_ready, made, turned, emptied, out_stored = (
            st.sem(n) for n in ("loaded", "chain", "ss_ready", "rs_ready", "made", "turned", "emptied", "out_stored"))
        ps = st.ps("turned", [P, 4, 4, P])
        quads = [(m, q) for m in range(LT) for q in range(KC // 4)] if out_t is not None else []
        with nc.Block() as block:
            if loads or stored is not None:
                @block.sync
                def _(sp):
                    for dst, src in loads:
                        sp.dma_start(dst, src).then_inc(loaded, 16)
                    if stored is not None:
                        for m in range(LT):
                            sp.wait_ge(made, m + 1)
                            sp.dma_start(stored[:, m, :], out[:, m, :]).then_inc(out_stored, 16)
                        sp.wait_ge(out_stored, 16 * LT)

            @block.vector
            def _(dve):
                link = Link(dve, chain)
                for m in range(LT):
                    if added is not None:
                        link(nc.vector.tensor_tensor(x[:, m, :], x[:, m, :], added[:, m, :], ALU.add))
                    link(nc.vector.scalar_tensor_tensor(sq[:, :], x[:, m, :], 1.0, x[:, m, :], ALU.mult, ALU.mult, accum_out=ss[:, m:m + 1]))
                    nc.vector.tensor_scalar(ss[:, m:m + 1], ss[:, m:m + 1], 1.0 / D, EPS2, ALU.mult, ALU.add).then_inc(ss_ready, 1)
                if loads:
                    dve.wait_ge(loaded, 16 * len(loads))
                for m in range(LT):
                    dve.wait_ge(rs_ready, m + 1)
                    link(nc.vector.reciprocal(rs[:, m:m + 1], rs[:, m:m + 1]))
                    nc.vector.scalar_tensor_tensor(out[:, m, :], x[:, m, :], rs[:, m:m + 1], g, ALU.mult, ALU.mult).then_inc(made, 1)

            if quads:
                @block.tensor
                def _(pe):
                    for i, (m, q) in enumerate(quads):
                        pe.wait_ge(made, m + 1)
                        for k in range(4):
                            c = 4 * q + k
                            last = nc.tensor.transpose(ps[:, i, k, :], out[:, m, c * P:(c + 1) * P], ident)
                        last.then_inc(turned, 1)

            @block.scalar
            def _(act):
                for m in range(LT):
                    act.wait_ge(ss_ready, m + 1)
                    nc.scalar.activation(rs[:, m:m + 1], ss[:, m:m + 1], ACT.Sqrt).then_inc(rs_ready, 1)
                for i, (m, q) in enumerate(quads):
                    act.wait_ge(turned, i + 1)
                    nc.scalar.activation(out_t[:, 4 * q:4 * q + 4, m * P:(m + 1) * P], ps[:, i, :, :], ACT.Copy)


def stage_ops(nc, name, make):
    with stage(nc, name) as st:
        chain = st.sem("chain")
        with nc.Block() as block:
            @block.vector
            def _(dve):
                make(Link(dve, chain))


def weight_plan(a):
    plan = []

    def some(w, *parts):
        for name, at, n in parts:
            plan.append((name, w[:, at:at + n], n, 1))

    some(a["w_mod"][0], ("mod0_first", 0, 2 * D))
    qkv = 4 * M_W + 16
    some(a["ab_w_in"][0], ("ab_v", 2 * M_W, M_W), ("ab_qk", 0, 2 * M_W), ("ab_o", 3 * M_W, M_W), ("ab_qkv", qkv, A_Q + 2 * A_KV))
    some(a["w_mod"][0], ("mod0_rest", 2 * D, 4 * D))
    some(a["w_mod"][1], ("mod1_first", 0, 2 * D))
    some(a["ab_w_out"][0], ("ab_out", 0, D))
    some(a["peer_wq"][0], ("l0_peer_q", 0, HALVES * P))
    plan.append(None)
    ck, cv = H_C * P, H_C * DV_C
    some(a["gla_w_in"][0], ("c_q", 0, ck), ("c_k", ck, ck), ("c_v", 2 * ck, cv), ("c_g", 2 * ck + cv, cv))
    some(a["w_mod"][1], ("mod1_rest", 2 * D, 4 * D))
    some(a["gla_w_out"][0], ("c_out", 0, D))
    some(a["peer_wq"][1], ("l1_peer_q", 0, HALVES * P))
    plan.append(None)
    za, xb, lg, z, xbc, dt, g = 0, 2 * D, 3 * D, 4 * D, 5 * D, 7 * D, 7 * D + S_HEADS
    some(a["w_in_2"][0], ("b_xb", xb, D), ("b_lg", lg, D), ("b_za", za, 2 * D))
    some(a["w_branch_b_2"][0], ("b_wb", 0, D))
    some(a["w_in_2"][0], ("b_xbc", xbc, 2 * D), ("b_z", z, D), ("b_g", g, 3 * D))
    some(a["w_branch_a_2"][0], ("b_wa", 0, D))
    some(a["w_branch_c_2"][0], ("b_wc", 0, D))
    some(a["w_out_2"][0], ("b_out", 0, D))
    some(a["w_mlp_up_2"][0], ("b_mlp1", 0, 4 * D))
    plan.append(("b_mlp2", a["w_mlp_down_2"][0], D, 4))
    return plan


def token_tiles(n):
    return [(i * P, P) for i in range(n)]


def buffers(nc, ctx):
    return lambda name, shape, dt=F32: ctx.enter_context(nc.sbuf_tensor(name, shape, dt))


def peer(nc, weights, name, layer, n_tiles, consts, a, keys_t, h, h_t, y, landed, landed0):
    with ExitStack() as ctx:
        sb = buffers(nc, ctx)
        q_t = sb(f"{name}_q_t", [P, n_tiles, HALVES, P])
        stage_linear(nc, f"{name}_q", weights, h_t, token_tiles(n_tiles), q_t, feature=True)
        stage_peer(nc, f"{name}_experts", h, n_tiles, q_t[:, :, :, :], keys_t[:, :, :], a["peer_u"].rearrange("l e d -> (l e) d"),
                   a["peer_v"].rearrange("l e d -> (l e) d"), consts["iota"][:, :], consts["ident"][:, :], layer, y,
                   h_t[:, 0:4, :].rearrange("p c (i t) -> p (c i) t", t=P), weights.slots[:, :, :, :], landed, landed0)


def mixer_ab(nc, weights, consts, a, cat, h_t, y, mod0, mod1):
    w = a["ab_w_in"][0]
    tiles = token_tiles(TT)
    with ExitStack() as ctx:
        sb = buffers(nc, ctx)
        o = sb("ab_o", [P, TT, M_W])
        hm = sb("ab_hm", [P, TT, M_W])
        with ExitStack() as ctx2:
            sb = buffers(nc, ctx2)
            qk_t = y[:, :, :].rearrange("p m (a t) -> p (m a) t", t=TOK)
            v_aug = sb("ab_v_aug", [P, TT, H_M, P + 2])
            g_cols = sb("ab_g_cols", [P, 2, TT, 2, H_M])
            m_rows = sb("ab_m_rows", [H_M, 2, TOK])
            qkv = sb("ab_qkv", [P, TT, A_Q + 2 * A_KV])
            with ExitStack() as ctx3:
                v = buffers(nc, ctx3)("ab_v", [P, TT, M_W])
                stage_linear(nc, "ab_v", weights, h_t, tiles, v)
                stage_value_ones(nc, "ab_ones", v, v_aug)
            stage_linear(nc, "ab_qk", weights, h_t, tiles, qk_t, feature=True)
            stage_linear(nc, "ab_o", weights, h_t, tiles, o)
            stage_gates(nc, h_t, w[:, 4 * M_W:4 * M_W + 16], a["ab_gate_b"][0], consts["ident"], consts["sel"], g_cols, m_rows)
            stage_linear(nc, "ab_qkv", weights, h_t, tiles, qkv)
            stage_mlstm(nc, qk_t, v_aug, g_cols, m_rows, consts["sel"], consts["far"], hm, weights, mod0)
            stage_attention(nc, qkv, consts["cos"], consts["sin"], consts["bars"], a["ab_sink"][0], consts["ident"][:, :], cat, weights, mod1)
        stage_head_norm(nc, "ab_norm", hm, range(TT), H_M, P, a["ab_norm_w"][0], o, ACT.Sigmoid, cat, LN_EPS)
        stage_transpose(nc, "ab_turn", consts["ident"][:, :], cat, h_t, range(TT), KC)


def mixer_c(nc, weights, consts, a, h, h_t, y, mod1):
    w = a["gla_w_in"][0]
    ck, cv = H_C * P, H_C * DV_C
    scratch = [t[:, :, :].rearrange("p m (a t) -> p (m a) t", t=TOK) for t in (h, y)]
    with ExitStack() as ctx:
        sb = buffers(nc, ctx)
        g = sb("c_g", [P, LT, cv])
        lat_t = h_t[:, :, CTX:TOK]
        hc = sb("c_h", [P, LT, cv])
        with ExitStack() as ctx2:
            sb = buffers(nc, ctx2)
            q_t = sb("c_q_t", [P, H_C, SEQ])
            k_t = sb("c_k_t", [P, H_C, TOK])
            v = sb("c_v", [P, TT, cv])
            stage_linear(nc, "c_q", weights, lat_t, token_tiles(LT), q_t, feature=True)
            stage_linear(nc, "c_k", weights, h_t, token_tiles(TT), k_t, feature=True)
            stage_linear(nc, "c_v", weights, h_t, token_tiles(TT), v)
            stage_linear(nc, "c_g", weights, lat_t, token_tiles(LT), g)
            stage_gla(nc, w[:, 2 * ck + 2 * cv:2 * ck + 2 * cv + 2 * RANK], a["gla_gate_up"][0], a["gla_gate_b"][0], h_t, q_t, k_t, v,
                      consts["sees"], consts["ident"][:, :], *scratch, hc, weights, mod1)
        stage_head_norm(nc, "c_norm", hc, range(LT), H_C, DV_C, a["gla_norm_w"][0], g, ACT.Silu, hc, LN_EPS)
        stage_transpose(nc, "c_turn", consts["ident"][:, :], hc, h_t, range(LT), KC)


def second_block(nc, weights, consts, a, x, hn, out):
    ident = consts["ident"][:, :]
    tiles = token_tiles(LT)
    w = a["w_in_2"][0]
    dt = 7 * D
    with ExitStack() as ctx:
        sb = buffers(nc, ctx)
        h_t = sb("b_h_t", [P, KC, SEQ])
        norm_rows = sb("b_rms_rows", [P, 3, D])
        loads = [(norm_rows[:, i, :], g.partition_broadcast(P)) for i, g in enumerate((a["norm_mix_g_2"][0], a["norm_mlp_g_2"][0], a["final_norm_g_2"]))]
        stage_rms(nc, "b_rms1", x, norm_rows[:, 0, :], hn, ident, out_t=h_t, loads=loads)
        with ExitStack() as ctx2:
            branches = [buffers(nc, ctx2)(f"b_branch{i}", [P, LT, D]) for i in range(3)]
            with ExitStack() as c:
                sb = buffers(nc, c)
                uv = sb("b_uv", [P, LT, 2 * D])
                with ExitStack() as c2:
                    sb = buffers(nc, c2)
                    xr, xc, gate = (sb(f"b_{n}", [P, KC, SEQ]) for n in ("xr", "xc", "gate"))
                    stage_linear(nc, "b_xb", weights, h_t, tiles, xr, feature=True)
                    stage_linear(nc, "b_lg", weights, h_t, tiles, gate, feature=True, func=ACT.Gelu_apprx_tanh,
                                 side=lambda st: conv_parts(nc, st, "conv", xr, KC, a["lru_conv_w_2"][0], a["lru_conv_b_2"][0], xc, False)[0])
                    stage_linear(nc, "b_za", weights, h_t, tiles, uv, func=ACT.Gelu_apprx_tanh,
                                 side=lambda st: lru_parts(nc, st, xc, gate, a["lru_w_r_2"][0], a["lru_b_r_2"][0], a["lru_w_i_2"][0],
                                                           a["lru_b_i_2"][0], a["lru_lambda_2"][0], lambda pe: None))
                    stage_linear(nc, "b_wb", weights, gate, tiles, branches[1])
                with ExitStack() as c2:
                    sb = buffers(nc, c2)
                    ya, ya_t, zs = sb("b_ya", [P, LT, D]), sb("b_ya_t", [P, KC, SEQ]), sb("b_zs", [P, LT, D])
                    xc = sb("b_sxc", [P, 2 * KC, SEQ])
                    y, x_tok = (uv[:, i, :].rearrange("p (m d) -> p m d", d=D) for i in range(2))
                    with ExitStack() as c3:
                        xr = buffers(nc, c3)("b_sxr", [P, 2 * KC, SEQ])
                        stage_linear(nc, "b_xbc", weights, h_t, tiles, xr, feature=True,
                                     side=lambda st: gmlp_parts(nc, st, uv, a["gmlp_ln_g_2"][0], a["gmlp_ln_b_2"][0], a["gmlp_w_s_2"][0],
                                                                a["gmlp_b_s_2"][0], ident, consts["sees"][:, 0, :], ya, ya_t))
                        stage_linear(nc, "b_z", weights, h_t, tiles, zs, func=ACT.Silu,
                                     side=lambda st: conv_parts(nc, st, "conv", xr, 2 * KC, a["ssd_conv_w_2"][0], a["ssd_conv_b_2"][0], xc, True)[0])
                    g = sb("b_g", [P, LT, 3 * D])
                    stage_linear(nc, "b_g", weights, h_t, tiles, g,
                                 side=lambda st: ssd_parts(nc, st, h_t, w[:, dt:dt + S_HEADS], a["ssd_dt_bias_2"][0], a["ssd_a_log_2"][0],
                                                           a["ssd_d_2"][0], xc, x_tok, zs, consts["ident"], consts["sel"], consts["far"], y, ya))
                    stage_head_norm(nc, "b_norm", y, range(LT), S_GROUPS, D // S_GROUPS, a["ssd_norm_g_2"][0], None, None, y, EPS2)
                    y_t = ya[:, :, :].rearrange("p m (k t) -> p (m k) t", t=SEQ)
                    stage_linear(nc, "b_wa", weights, ya_t, tiles, branches[0],
                                 side=lambda st: turn_parts(nc, st, ident, y, y_t, range(LT), KC)[0])
                    stage_linear(nc, "b_wc", weights, y_t, tiles, branches[2],
                                 side=lambda st: gate_parts(nc, st, g, a["b_gate_2"][0], branches, hn))

                    def last_branch(link, c):
                        part = g[:, c, 2 * D:3 * D]
                        link(nc.vector.tensor_tensor(part, part, branches[2][:, c, :], ALU.mult))
                        return nc.vector.tensor_tensor(hn[:, c, :], hn[:, c, :], part, ALU.add)
                    stage_transpose(nc, "b_merge", ident, hn, h_t, range(LT), KC, make=last_branch)
            stage_linear(nc, "b_out", weights, h_t, tiles, branches[0])
            stage_rms(nc, "b_rms2", x, norm_rows[:, 1, :], hn, ident, added=branches[0], out_t=h_t)
        with ExitStack() as c:
            sb = buffers(nc, c)
            up = sb("b_up", [P, 4 * KC, SEQ])
            down = sb("b_down", [P, LT, D])
            stage_linear(nc, "b_mlp1", weights, h_t, tiles, up, feature=True, func=ACT.Relu)
            stage_ops(nc, "b_sq", lambda link: link(nc.vector.tensor_tensor(up[:, :, :], up[:, :, :], up[:, :, :], ALU.mult)))
            stage_linear(nc, "b_mlp2", weights, up, tiles, down)
            stage_rms(nc, "b_rms3", x, norm_rows[:, 2, :], hn, ident, added=down, stored=out[0].rearrange("(m p) d -> p m d", p=P))


def shape_constants():
    pos = np.arange(SEQ)
    freq = (10000.0 ** (-np.arange(16, dtype=np.float32) / 16)).astype(np.float32)
    ang = np.concatenate([(pos // 64).astype(np.float32)[:, None] * freq, (pos % 64).astype(np.float32)[:, None] * freq], -1)
    cos = np.concatenate([np.ones((CTX, 32)), np.cos(ang)]).astype(np.float32)
    sin = np.concatenate([np.zeros((CTX, 32)), np.sin(ang)]).astype(np.float32)
    i = np.arange(P)
    seen = i[:, None] <= i[None, :]
    bars = np.zeros((P, LT, TOK), np.float32)
    bars[:, 0, 3 * P:] = np.where(i[None, :] <= i[:, None], 0, -BIG)
    bars[:, 1, 2 * P:3 * P] = np.where(i[:, None] <= i[None, :], 0, -BIG)
    sel = np.zeros((16, 16, P), np.float32)
    sel[np.arange(16), np.arange(16), :] = 1
    return {
        "ident": np.eye(P, dtype=np.float32),
        "cos": np.ascontiguousarray(cos.reshape(TT, P, 32).transpose(1, 0, 2)),
        "sin": np.ascontiguousarray(sin.reshape(TT, P, 32).transpose(1, 0, 2)),
        "far": np.stack([np.tile(np.where(m, 0, BIG), (1, TT)) for m in (seen, seen.T)], 1).astype(np.float32),
        "bars": bars,
        "sel": sel,
        "iota": np.tile(np.arange(TOPK, dtype=np.float32), (P, 1)),
        "sees": np.stack([seen, seen.T], 1).astype(np.float32),
    }


def build(nc, a, const_d, out):
    mod_rows = nc.dram_tensor("mod_rows", [DEPTH, 2, 6 * D], F32, kind="Internal").ap()

    def row(layer, context, chunk):
        return mod_rows[layer, 1 if context else 0, chunk * D:(chunk + 1) * D]

    def mods(layer, chunk, n_ctx=2):
        return [((0, 1), row(layer, True, chunk + 1), row(layer, True, chunk)),
                ((2, 3), row(layer, False, chunk + 1), row(layer, False, chunk))]

    def peer_keys(layer):
        return a["peer_keys"][layer].rearrange("h two n k -> n (h two) k")

    with ExitStack() as ctx:
        sb = buffers(nc, ctx)
        consts = {k: sb(f"const_{k}", list(v.shape)) for k, v in const_d.items()}
        x = sb("x_tiles", [P, TT, D])
        weights = Weights(nc, ctx, weight_plan(a))
        landed = [ctx.enter_context(nc.semaphore(f"row_landed{k}")) for k in range(TOPK)]
        silu_c = sb("silu_c", [P, KC, 2])
        stage_conditions(nc, weights, a["c"], a["c_ctx"], silu_c)
        stage_first_modulation(nc, weights, silu_c[:, :, :], a["b_mod"][0], mod_rows[0], [(consts[k][tuple([slice(None)] * len(d.shape))], d) for k, d in const_d.items()] + [
            (x[:, 0:2, :], a["ctx"][0].rearrange("(m p) d -> p m d", p=P)),
            (x[:, 2:4, :], a["x"][0].rearrange("(m p) d -> p m d", p=P))])
        ident = consts["ident"][:, :]
        with ExitStack() as c1:
            sb = buffers(nc, c1)
            h = sb("h_tiles", [P, TT, D])
            h_t = sb("h_t", [P, KC, TOK])
            y = sb("y_tiles", [P, TT, D])
            mod_args = [(silu_c[:, :, :], a["b_mod"][i], mod_rows[i]) for i in range(DEPTH)]
            both = [(i, i) for i in range(TT)]
            latents = [(2 + i, i) for i in range(LT)]

            def ln(layer, i):
                return a["ln_w"][layer, i], a["ln_b"][layer, i]

            stage_transpose(nc, "l0_mod1", ident, h, h_t, range(TT), KC, mod=mods(0, 0), x=x)
            mixer_ab(nc, weights, consts, a, h, h_t, y, *mod_args)
            with ExitStack() as c2:
                keys_t = buffers(nc, c2)("l0_keys_t", [P, HALVES + 4, P])
                with ExitStack() as c3:
                    sb = buffers(nc, c3)
                    keys = sb("l0_keys", [P, HALVES, P])
                    rows = NormRows(sb, "l0_ln1", [((0, 1), row(0, True, 2)), ((2, 3), row(0, False, 2))], ln(0, 0), mods(0, 3))
                    stage_linear(nc, "ab_out", weights, h_t, token_tiles(TT), y, rows=rows)
                    stage_residual_norm(nc, "l0_ln1", x, y, both, rows, turn=(ident, h, h_t), keys=(peer_keys(0), keys[:, :, :], keys_t))
                peer(nc, weights, "l0_peer", 0, TT, consts, a, keys_t, h[:, :, :], h_t, y[:, :, :], landed, 0)
            with ExitStack() as c2:
                rows = NormRows(buffers(nc, c2), "l0_ln2", [((0, 1), row(0, True, 5)), ((2, 3), row(0, False, 5))], ln(0, 1), mods(1, 0))
                stage_residual_norm(nc, "l0_ln2", x, y, both, rows, weights=weights, turn=(ident, h, h_t))
            mixer_c(nc, weights, consts, a, h, h_t, y, mod_args[1])
            with ExitStack() as c2:
                keys_t = buffers(nc, c2)("l1_keys_t", [P, HALVES + 4, P])
                with ExitStack() as c3:
                    sb = buffers(nc, c3)
                    keys = sb("l1_keys", [P, HALVES, P])
                    rows = NormRows(sb, "l1_ln1", [((2, 3), row(1, False, 2))], ln(1, 0), [((2, 3), row(1, False, 4), row(1, False, 3))])
                    stage_linear(nc, "c_out", weights, h_t, token_tiles(LT), y, rows=rows)
                    stage_residual_norm(nc, "l1_ln1", x, y, latents, rows, turn=(ident, h, h_t), keys=(peer_keys(1), keys[:, :, :], keys_t))
                peer(nc, weights, "l1_peer", 1, LT, consts, a, keys_t, h[:, 0:LT, :], h_t, y[:, 0:LT, :], landed, 32 * HEADS * TT)
            with ExitStack() as c2:
                rows = NormRows(buffers(nc, c2), "l1_ln2", [((2, 3), row(1, False, 5))], ln(1, 1))
                stage_residual_norm(nc, "l1_ln2", x, y, latents, rows, weights=weights)
        second_block(nc, weights, consts, a, x[:, 2:4, :], x[:, 0:2, :], out)


def kernel(**inputs):
    import concourse.bacc as bacc
    from concourse.bass_utils import run_bass_kernel_spmd

    nc = bacc.Bacc("TRN2", target_bir_lowering=False, num_devices=1)
    arrays, a, const_d = {}, {}, {}
    for name, value in inputs.items():
        arrays[f"in_{name}"] = np.ascontiguousarray(value)
        a[name] = nc.dram_tensor(f"in_{name}", arrays[f"in_{name}"].shape, F32, kind="ExternalInput").ap()
    for name, value in shape_constants().items():
        arrays[f"constant_{name}"] = value
        const_d[name] = nc.dram_tensor(f"constant_{name}", value.shape, F32, kind="ExternalInput").ap()
    out = nc.dram_tensor("out", [1, SEQ, D], F32, kind="ExternalOutput").ap()
    build(nc, a, const_d, out)
    r = run_bass_kernel_spmd(nc, [arrays], core_ids=[0])
    return r.results[0]["out"]
```
